# Optimizing a Trainium2 kernel written in Bass

```python
import jax, jax.numpy as jnp
from jax import lax
import numpy as np
import math

D_MODEL = 1024
BATCH = 1
SEQ = 512
DEPTH = 2

CHUNK = 128
RET_HEADS = 4
RET_QK_DIM = 128
RET_V_DIM = 256
RET_QK_WIDTH = RET_HEADS * RET_QK_DIM
RET_V_WIDTH = RET_HEADS * RET_V_DIM
GMLP_GROUPS = 4
GMLP_WIDTH = D_MODEL
GMLP_GROUP_DIM = GMLP_WIDTH // GMLP_GROUPS
POOL_WINDOWS = (2, 4, 8, 16)
POOL_GROUPS = 4
POOL_WIDTH = D_MODEL
POOL_GROUP_DIM = POOL_WIDTH // POOL_GROUPS
N_BRANCH = 3
BRANCH_WIDTH = D_MODEL
D_FF = 4 * D_MODEL
N_MOD = 6
ROPE_BASE = 10000.0
EPS = 1e-6
SPLITS = (RET_QK_WIDTH, RET_QK_WIDTH, RET_V_WIDTH, RET_V_WIDTH,
          GMLP_WIDTH, GMLP_WIDTH, POOL_WIDTH, N_BRANCH * D_MODEL)
D_IN = 2 * RET_QK_WIDTH + 2 * RET_V_WIDTH + 2 * GMLP_WIDTH + POOL_WIDTH + N_BRANCH * D_MODEL


def rms_norm(x, gain=None):
    xf = x.astype(jnp.float32)
    y = xf * lax.rsqrt(jnp.mean(xf * xf, axis=-1, keepdims=True) + EPS)
    if gain is not None:
        y = y * gain.astype(jnp.float32)
    return y.astype(x.dtype)

def split_columns(proj):
    pieces, start = [], 0
    for w in SPLITS:
        pieces.append(proj[..., start:start + w])
        start += w
    return pieces

def rotary(x, positions):
    half = x.shape[-1] // 2
    inv_freq = ROPE_BASE ** (-jnp.arange(half, dtype=jnp.float32) / half)
    ang = positions.astype(jnp.float32)[:, :, None] * inv_freq
    cos = jnp.cos(ang)[:, :, None, :]
    sin = jnp.sin(ang)[:, :, None, :]
    xf = x.astype(jnp.float32)
    x1, x2 = xf[..., :half], xf[..., half:]
    return jnp.concatenate([x1 * cos - x2 * sin, x2 * cos + x1 * sin], axis=-1).astype(x.dtype)

def retention(q, k, v, g, positions):
    B, S, _ = q.shape
    nc = S // CHUNK
    dt = q.dtype
    q = rotary(q.reshape(B, S, RET_HEADS, RET_QK_DIM), positions)
    k = rotary(k.reshape(B, S, RET_HEADS, RET_QK_DIM), positions) * (RET_QK_DIM ** -0.5)
    v = v.reshape(B, S, RET_HEADS, RET_V_DIM)
    log_gamma = jnp.log1p(-jnp.power(2.0, -5.0 - jnp.arange(RET_HEADS, dtype=jnp.float32)))
    pos = jnp.arange(CHUNK, dtype=jnp.float32)
    rel = pos[:, None] - pos[None, :]
    causal = rel >= 0
    decay_intra = jnp.where(causal[None],
                            jnp.exp(log_gamma[:, None, None] * jnp.where(causal, rel, 0.0)[None]),
                            0.0)
    decay_q = jnp.exp(log_gamma[:, None] * (pos + 1.0)[None])
    decay_k = jnp.exp(log_gamma[:, None] * (CHUNK - 1.0 - pos)[None])
    decay_chunk = jnp.exp(log_gamma * CHUNK)

    qc = q.reshape(B, nc, CHUNK, RET_HEADS, RET_QK_DIM)
    kc = k.reshape(B, nc, CHUNK, RET_HEADS, RET_QK_DIM)
    vc = v.reshape(B, nc, CHUNK, RET_HEADS, RET_V_DIM)
    scores = jnp.einsum('bnihd,bnjhd->bnhij', qc, kc) * decay_intra.astype(dt)
    intra = jnp.einsum('bnhij,bnjhe->bnihe', scores, vc)
    kv = jnp.einsum('bnjhd,hj,bnjhe->nbhde', kc, decay_k.astype(dt), vc).astype(jnp.float32)

    def step(state, kv_n):
        return decay_chunk[None, :, None, None] * state + kv_n, state

    _, prev = lax.scan(step, jnp.zeros((B, RET_HEADS, RET_QK_DIM, RET_V_DIM), jnp.float32), kv)
    cross = jnp.einsum('bnihd,hi,nbhde->bnihe', qc, decay_q.astype(dt), prev.astype(dt))
    o = (intra + cross).reshape(B, S, RET_HEADS, RET_V_DIM)
    o = rms_norm(o).reshape(B, S, RET_V_WIDTH)
    return jax.nn.silu(g) * o

def spatial_gating(u, v, w_s, b_s, v_gain):
    B, S, _ = u.shape
    nc = S // CHUNK
    u = jax.nn.gelu(u)
    v = rms_norm(jax.nn.gelu(v), v_gain)
    vc = v.reshape(B, nc, CHUNK, GMLP_GROUPS, GMLP_GROUP_DIM)
    mask = jnp.tril(jnp.ones((CHUNK, CHUNK), dtype=bool))
    w = jnp.where(mask[None], w_s, jnp.zeros_like(w_s))
    mixed = jnp.einsum('gts,bnsgc->bntgc', w, vc) + b_s.T[None, None, :, :, None]
    return u * mixed.reshape(B, S, GMLP_WIDTH)

def multiscale_pool(p, w_pool, b_pool, scale):
    B, S, _ = p.shape
    pg = p.reshape(B, S, POOL_GROUPS, POOL_GROUP_DIM).astype(jnp.float32)
    cs = jnp.concatenate([jnp.zeros((B, 1, POOL_GROUPS, POOL_GROUP_DIM), jnp.float32),
                          jnp.cumsum(pg, axis=1)], axis=1)
    t = jnp.arange(1, S + 1)
    outs = []
    for gi, w in enumerate(POOL_WINDOWS):
        start = jnp.maximum(t - w, 0)
        window_sum = cs[:, 1:, gi] - cs[:, start, gi]
        count = jnp.minimum(t, w).astype(jnp.float32)[None, :, None]
        outs.append(window_sum / count - pg[:, :, gi])
    pooled = jnp.stack(outs, axis=2).astype(p.dtype)
    mixed = jnp.einsum('bsgc,gce->bsge', pooled, w_pool) + b_pool[None, None]
    return mixed.reshape(B, S, POOL_WIDTH) * scale

def first_inputs(seed: int = 0) -> dict:
    key = jax.random.key(seed)
    ks = jax.random.split(key, 20)
    f32 = jnp.float32
    nrm = lambda k, shape, s: jax.random.normal(k, shape, f32) * s
    return {
        "x": nrm(ks[0], (BATCH, SEQ, D_MODEL), 1.0),
        "c": nrm(ks[1], (BATCH, D_MODEL), 1.0),
        "positions": jnp.broadcast_to(jnp.arange(SEQ, dtype=jnp.int32), (BATCH, SEQ)),
        "w_ada": nrm(ks[2], (DEPTH, D_MODEL, N_MOD * D_MODEL), 0.5 * D_MODEL ** -0.5),
        "b_ada": nrm(ks[3], (DEPTH, N_MOD * D_MODEL), 0.01),
        "norm1": 1.0 + nrm(ks[4], (DEPTH, D_MODEL), 0.02),
        "norm2": 1.0 + nrm(ks[5], (DEPTH, D_MODEL), 0.02),
        "w_in": nrm(ks[6], (DEPTH, D_MODEL, D_IN), D_MODEL ** -0.5),
        "ws_gmlp": nrm(ks[7], (DEPTH, GMLP_GROUPS, CHUNK, CHUNK), CHUNK ** -0.5),
        "bs_gmlp": 1.0 + nrm(ks[8], (DEPTH, GMLP_GROUPS, CHUNK), 0.1),
        "vnorm_gmlp": 1.0 + nrm(ks[9], (DEPTH, GMLP_WIDTH), 0.02),
        "w_pool": nrm(ks[10], (DEPTH, POOL_GROUPS, POOL_GROUP_DIM, POOL_GROUP_DIM), POOL_GROUP_DIM ** -0.5),
        "b_pool": nrm(ks[11], (DEPTH, POOL_GROUPS, POOL_GROUP_DIM), 0.01),
        "pool_scale": 1.0 + nrm(ks[12], (DEPTH, POOL_WIDTH), 0.1),
        "w_branch": nrm(ks[13], (DEPTH, N_BRANCH, BRANCH_WIDTH, D_MODEL), BRANCH_WIDTH ** -0.5),
        "w_out": nrm(ks[14], (DEPTH, D_MODEL, D_MODEL), D_MODEL ** -0.5),
        "w_ff1": nrm(ks[15], (DEPTH, D_MODEL, D_FF), D_MODEL ** -0.5),
        "w_ff2": nrm(ks[16], (DEPTH, D_FF, D_MODEL), D_FF ** -0.5),
        "final_norm": 1.0 + nrm(ks[17], (D_MODEL,), 0.02),
    }

def first_block(x, c, positions, w_ada, b_ada, norm1, norm2, w_in, ws_gmlp, bs_gmlp, vnorm_gmlp,
              w_pool, b_pool, pool_scale, w_branch, w_out, w_ff1, w_ff2, final_norm):
    B, S, _ = x.shape
    c_act = jax.nn.silu(c)
    for l in range(DEPTH):
        mod = c_act @ w_ada[l] + b_ada[l]
        sh1, sc1, gt1, sh2, sc2, gt2 = [m[:, None, :] for m in jnp.split(mod, N_MOD, axis=-1)]

        h = rms_norm(x, norm1[l]) * (1.0 + sc1) + sh1
        proj = h @ w_in[l]
        q, k, v, g, u, vs, p, gate_cols = split_columns(proj)
        y_ret = retention(q, k, v, g, positions)
        y_sgu = spatial_gating(u, vs, ws_gmlp[l], bs_gmlp[l], vnorm_gmlp[l])
        y_pool = multiscale_pool(p, w_pool[l], b_pool[l], pool_scale[l])
        branches = jnp.stack([y_ret, y_sgu, y_pool], axis=2)
        branch_proj = jnp.einsum('bsnc,ncd->bsnd', branches, w_branch[l])
        gates = jax.nn.sigmoid(gate_cols.reshape(B, S, N_BRANCH, D_MODEL))
        merged = jnp.sum(gates * branch_proj, axis=2)
        x = x + gt1 * (merged @ w_out[l])

        h2 = rms_norm(x, norm2[l]) * (1.0 + sc2) + sh2
        hidden = jnp.square(jax.nn.relu(h2 @ w_ff1[l]))
        x = x + gt2 * (hidden @ w_ff2[l])
    return rms_norm(x, final_norm)


N_A_LAYERS = DEPTH // 2
N_B_LAYERS = DEPTH - N_A_LAYERS

A_HEADS = 16
A_HEAD_DIM = D_MODEL // A_HEADS
A_QKV_WIDTH = 3 * A_HEADS * A_HEAD_DIM
Q_BLOCK = 128

B_GROUPS = ((128, 1), (512, 4), (2048, 16))
B_N_GROUPS = len(B_GROUPS)
B_HEADS_PER_GROUP = 8
B_HEAD_DIM = 64
B_WINDOW_STEPS = 128
B_Q_WIDTH = B_N_GROUPS * B_HEADS_PER_GROUP * B_HEAD_DIM
B_OUT_WIDTH = B_HEADS_PER_GROUP * B_HEAD_DIM
B_KV_WIDTH = 2 * B_Q_WIDTH
ALIBI_TOTAL_HEADS = B_N_GROUPS * B_HEADS_PER_GROUP

D_FF_2 = 2816
CONV_WIDTH = 3

RMS_EPS = 1e-6


def rms_norm_2(x, g):
    xf = x.astype(jnp.float32)
    y = xf * lax.rsqrt(jnp.mean(xf * xf, axis=-1, keepdims=True) + RMS_EPS)
    return (y * g.astype(jnp.float32)).astype(x.dtype)

def conv_ffn(h, w_up, conv_w, conv_b, w_down):
    u = h @ w_up
    c = u.shape[-1]
    u = lax.conv_general_dilated(
        u, conv_w[:, None, :].astype(u.dtype), window_strides=(1,),
        padding=[(CONV_WIDTH - 1, 0)],
        dimension_numbers=("NWC", "WIO", "NWC"),
        feature_group_count=c) + conv_b
    a, gate = jnp.split(u, 2, axis=-1)
    return (jax.nn.silu(gate) * a) @ w_down

def forgetting_attention(q, k, v, log_f):
    S = q.shape[1]
    dh = q.shape[-1]
    scale = dh ** -0.5
    c = jnp.cumsum(log_f.astype(jnp.float32), axis=1).transpose(0, 2, 1)
    outs = []
    for i in range(S // Q_BLOCK):
        q0 = i * Q_BLOCK
        q1 = q0 + Q_BLOCK
        s = jnp.einsum("bqhd,bkhd->bhqk", q[:, q0:q1], k[:, :q1]).astype(jnp.float32) * scale
        s = s + c[:, :, q0:q1, None] - c[:, :, None, :q1]
        causal = jnp.arange(q0, q1)[:, None] >= jnp.arange(q1)[None, :]
        p = jax.nn.softmax(jnp.where(causal, s, -jnp.inf), axis=-1)
        outs.append(jnp.einsum("bhqk,bkhd->bqhd", p.astype(v.dtype), v[:, :q1]))
    return jnp.concatenate(outs, axis=1)

def dilated_branch(q, k, v, dil, slopes):
    B, S, H, Dh = q.shape
    W = B_WINDOW_STEPS
    period = dil * W
    Sp = -(-S // period) * period
    nb = Sp // period
    pad = ((0, 0), (0, Sp - S), (0, 0), (0, 0))

    def blocks(t):
        return jnp.pad(t, pad).reshape(B, nb, W, dil, H, Dh)

    def with_prev(t):
        prev = jnp.pad(t, ((0, 0), (1, 0), (0, 0), (0, 0), (0, 0), (0, 0)))[:, :nb]
        return jnp.concatenate([prev, t], axis=2)

    qb = blocks(q)
    kk = with_prev(blocks(k))
    vv = with_prev(blocks(v))
    s = jnp.einsum("bnirhd,bnjrhd->bnrhij", qb, kk).astype(jnp.float32) * (Dh ** -0.5)
    qi = jnp.arange(W)[:, None]
    kj = jnp.arange(2 * W)[None, :]
    dist = qi + W - kj
    band = (dist >= 0) & (dist <= W)
    first = (jnp.arange(nb)[:, None, None] == 0) & (kj < W)[None]
    valid = band[None] & ~first
    bias = -slopes[:, None, None] * (dil * dist).astype(jnp.float32)
    s = jnp.where(valid[None, :, None, None], s + bias, -jnp.inf)
    m = jnp.max(s, axis=-1, keepdims=True)
    p = jnp.exp(s - m)
    l = jnp.sum(p, axis=-1, keepdims=True)
    o = jnp.einsum("bnrhij,bnjrhd->bnirhd", (p / l).astype(v.dtype), vv)
    lse = (m + jnp.log(l))[..., 0]
    o = o.reshape(B, Sp, H, Dh)[:, :S]
    lse = lse.transpose(0, 1, 4, 2, 3).reshape(B, Sp, H)[:, :S]
    return o, lse

def second_inputs(seed: int = 0) -> dict:
    key = jax.random.key(seed)
    ks = jax.random.split(key, 16)
    f32 = jnp.float32

    def nrm(k, shape, fan_in):
        return jax.random.normal(k, shape, f32) * (fan_in ** -0.5)

    def gain(k, shape):
        return 1.0 + 0.05 * jax.random.normal(k, shape, f32)

    return {
        "x": jax.random.normal(ks[0], (BATCH, SEQ, D_MODEL), f32),
        "a_w_in": nrm(ks[1], (N_A_LAYERS, D_MODEL, A_QKV_WIDTH + A_HEADS), D_MODEL),
        "a_b_f": 2.0 + 0.1 * jax.random.normal(ks[2], (N_A_LAYERS, A_HEADS), f32),
        "a_w_out": nrm(ks[3], (N_A_LAYERS, A_HEADS * A_HEAD_DIM, D_MODEL), A_HEADS * A_HEAD_DIM),
        "b_w_q": nrm(ks[4], (N_B_LAYERS, D_MODEL, B_Q_WIDTH), D_MODEL),
        "b_w_out": nrm(ks[5], (N_B_LAYERS, B_OUT_WIDTH, D_MODEL), B_OUT_WIDTH),
        "kv_norm_g": gain(ks[6], (D_MODEL,)),
        "w_kv": nrm(ks[7], (D_MODEL, B_KV_WIDTH), D_MODEL),
        "mix_norm_g": gain(ks[8], (DEPTH, D_MODEL)),
        "ffn_norm_g": gain(ks[9], (DEPTH, D_MODEL)),
        "ffn_w_up": nrm(ks[10], (DEPTH, D_MODEL, 2 * D_FF_2), D_MODEL),
        "ffn_conv_w": nrm(ks[11], (DEPTH, CONV_WIDTH, 2 * D_FF_2), CONV_WIDTH),
        "ffn_conv_b": 0.02 * jax.random.normal(ks[12], (DEPTH, 2 * D_FF_2), f32),
        "ffn_w_down": nrm(ks[13], (DEPTH, D_FF_2, D_MODEL), D_FF_2),
        "final_norm_g": gain(ks[14], (D_MODEL,)),
    }

def second_block(x, a_w_in, a_b_f, a_w_out, b_w_q, b_w_out, kv_norm_g, w_kv,
              mix_norm_g, ffn_norm_g, ffn_w_up, ffn_conv_w, ffn_conv_b, ffn_w_down,
              final_norm_g):
    B, S, D = x.shape
    slopes = jnp.exp2(-8.0 * jnp.arange(1, ALIBI_TOTAL_HEADS + 1, dtype=jnp.float32)
                      / ALIBI_TOTAL_HEADS).reshape(B_N_GROUPS, B_HEADS_PER_GROUP)
    kv = None
    for layer in range(DEPTH):
        if layer < N_A_LAYERS:
            h = rms_norm_2(x, mix_norm_g[layer])
            proj = h @ a_w_in[layer]
            qkv = proj[..., :A_QKV_WIDTH].reshape(B, S, 3, A_HEADS, A_HEAD_DIM)
            log_f = jax.nn.log_sigmoid(
                proj[..., A_QKV_WIDTH:].astype(jnp.float32) + a_b_f[layer].astype(jnp.float32))
            o = forgetting_attention(qkv[:, :, 0], qkv[:, :, 1], qkv[:, :, 2], log_f)
            x = x + o.reshape(B, S, A_HEADS * A_HEAD_DIM) @ a_w_out[layer]
        else:
            if kv is None:
                kv = (rms_norm_2(x, kv_norm_g) @ w_kv).reshape(
                    B, S, 2, B_N_GROUPS, B_HEADS_PER_GROUP, B_HEAD_DIM)
            bl = layer - N_A_LAYERS
            h = rms_norm_2(x, mix_norm_g[layer])
            q = (h @ b_w_q[bl]).reshape(B, S, B_N_GROUPS, B_HEADS_PER_GROUP, B_HEAD_DIM)
            outs, lses = [], []
            for g, (window, dil) in enumerate(B_GROUPS):
                o_g, lse_g = dilated_branch(q[:, :, g], kv[:, :, 0, g], kv[:, :, 1, g],
                                            dil, slopes[g])
                outs.append(o_g)
                lses.append(lse_g)
            alpha = jax.nn.softmax(jnp.stack(lses, axis=0), axis=0)
            o = jnp.sum(alpha[..., None].astype(outs[0].dtype) * jnp.stack(outs, axis=0), axis=0)
            x = x + o.reshape(B, S, B_OUT_WIDTH) @ b_w_out[bl]
        h = rms_norm_2(x, ffn_norm_g[layer])
        x = x + conv_ffn(h, ffn_w_up[layer], ffn_conv_w[layer], ffn_conv_b[layer],
                         ffn_w_down[layer])
    return rms_norm_2(x, final_norm_g)


def setup_inputs(seed=0):
    out = dict(first_inputs(seed))
    for name, value in second_inputs(seed + 1).items():
        if name != "x":
            out[name + "_2"] = value
    return out


def reference(
    x, c, positions, w_ada, b_ada, norm1, norm2, w_in, ws_gmlp, bs_gmlp, vnorm_gmlp, w_pool,
    b_pool, pool_scale, w_branch, w_out, w_ff1, w_ff2, final_norm, a_w_in_2, a_b_f_2, a_w_out_2,
    b_w_q_2, b_w_out_2, kv_norm_g_2, w_kv_2, mix_norm_g_2, ffn_norm_g_2, ffn_w_up_2,
    ffn_conv_w_2, ffn_conv_b_2, ffn_w_down_2, final_norm_g_2,
):
    x = first_block(
        x, c, positions, w_ada, b_ada, norm1, norm2, w_in, ws_gmlp, bs_gmlp, vnorm_gmlp, w_pool,
        b_pool, pool_scale, w_branch, w_out, w_ff1, w_ff2, final_norm,
    )
    return second_block(
        x, a_w_in_2, a_b_f_2, a_w_out_2, b_w_q_2, b_w_out_2, kv_norm_g_2, w_kv_2, mix_norm_g_2,
        ffn_norm_g_2, ffn_w_up_2, ffn_conv_w_2, ffn_conv_b_2, ffn_w_down_2, final_norm_g_2,
    )


_drawn_inputs = setup_inputs


def setup_inputs(seed=0):
    import zlib

    import numpy as np

    out = dict(_drawn_inputs(seed))
    spreads = {}
    factors = {'norm1': 4.821,
     'norm2': 3.449,
     'bs_gmlp': 2.72,
     'vnorm_gmlp': 8.0,
     'b_pool': 29.19,
     'kv_norm_g_2': 3.232,
     'ffn_conv_b_2': 2.869}
    for name, (base, spread) in spreads.items():
        noise = np.random.default_rng([zlib.crc32(name.encode()), seed]).standard_normal(out[name].shape)
        drawn = base * np.exp(spread * noise) if base else spread * noise
        out[name] = __import__('jax').numpy.asarray(drawn.astype(out[name].dtype))
    for name, factor in factors.items():
        out[name] = (out[name] * factor).astype(out[name].dtype)
    return out
```

```python
from contextlib import ExitStack, contextmanager

import numpy as np

import concourse.bass as bass
from concourse import mybir

F32 = mybir.dt.float32
F32R = mybir.dt.float32r
I32 = mybir.dt.int32
ACT = mybir.ActivationFunctionType
ALU = mybir.AluOpType
AX = mybir.AxisListType

P = 128
S = 512
D = 1024
KT = D // P
TT = S // P
LAYERS = 2
R_HEADS, R_V = 4, 256
A_HEADS = 16
B_GROUPS = ((1, 128), (4, 512), (16, 512))
FF2 = 2816
SLABS = (8, 8, 6)
EPS = 1e-6
NEG = -1e30
RING = 4
AHEAD = RING - 1
TILE = KT * P

N_ADA = 6 * D // P
LAYER_TILES = N_ADA + 8 * 8 + 3 * 16 + 4 + 8 * 7
FFN2_TILES = 2 * sum(SLABS) + 8 * len(SLABS)
TILES = LAYERS * LAYER_TILES + (16 + 8 + 8 + FFN2_TILES) + (12 + 12 + 12 + 4 + FFN2_TILES)

C_ID, C_PERM, C_ONES, C_CAUSAL, C_EDGE = 0, P, 2 * P, 3 * P, 4 * P
C_FREQ = C_EDGE + 4 * 16
C_SIGN, C_EPS, C_HALFPI = C_FREQ + 1, C_FREQ + 2, C_FREQ + 3
C_SLOPE = C_FREQ + 4
C_ALL = C_SLOPE + 24
V_N1, V_N2, V_ADA, V_GAIN, V_BP, V_PS, V_ALL = 0, 8, 16, 64, 72, 80, 88
W_KV, W_MIX, W_FFN, W_FIN, W_FIN1, W_CW, W_CB, W_BF, W_ALL = 0, 8, 24, 40, 48, 56, 56 + 264, 56 + 352, 56 + 368
UP = 2 * FF2 // P


class Count:

    def __init__(self, start=0):
        self.n, self.off = start, None

    def value(self, back=0):
        return self.n - back if self.off is None else self.off + (self.n - back)

    def next(self, k=1):
        self.n += k
        return self.value()


@contextmanager
def repeat(eng, trips, steps):
    saved = [(c, c.n, c.off, k) for c, k in steps.items()]
    with eng.Fori(0, trips) as i:
        for c, _, off, k in saved:
            c.off = i * k if off is None else off + i * k
        yield i
        for c, n, _, k in saved:
            assert c.n == n + k, f"a pass adds {c.n - n}, not {k}: {[x.n - m for x, m, _, _ in saved]}"
    for c, n, off, k in saved:
        c.n, c.off = n + k * trips, off


def build(nc, stream, xT, cvec, pos, consts, decay, tables, vec1, ws, bs, vec2, wf, outT):
    with ExitStack() as ctx:
        def sb(name, shape, dt=F32):
            return ctx.enter_context(nc.sbuf_tensor(name, shape, dt))

        def sem(name):
            return ctx.enter_context(nc.semaphore(name))

        raw = sb("raw", [P, RING, TILE])
        hi = sb("hi", [P, RING, TILE], F32R)
        lo = sb("lo", [P, RING, TILE], F32R)
        x = sb("x", [P, KT, S])
        with nc.sbuf_tensor("hH", [P, KT, S], F32R) as hH, nc.sbuf_tensor("hL", [P, KT, S], F32R) as hL:
            pass
        hF = sb("hF", [P, 2 * KT * S])
        with nc.sbuf_tensor("yH", [P, KT, S], F32R) as yH, nc.sbuf_tensor("yL", [P, KT, S], F32R) as yL:
            pass
        yF = sb("yF", [P, 2 * KT * S])
        act3 = sb("act3", [P, 3 * KT, S])
        A, B, M = act3[:, 0:KT], act3[:, KT:2 * KT], act3[:, 2 * KT:3 * KT]
        st = sb("st", [P, 4, S])
        tab = sb("tab", [P, 3072])
        scr = sb("scr", [P, 1280])
        cst = sb("cst", [P, C_ALL])
        v1 = sb("v1", [P, V_ALL])
        v2 = sb("v2", [P, W_ALL])
        mod = sb("mod", [P, N_ADA])
        geff = sb("geff", [P, 8])
        bpps = sb("bpps", [P, 8])
        cs = sb("cs", [P, 3, 8])
        cH = sb("cH", [P, KT, 2], F32R)
        cL = sb("cL", [P, KT, 2], F32R)
        stat = sb("stat", [P, 16])
        pb = ctx.enter_context(nc.psum_tensor("pb", [P, 8, S], F32))

        dec = tab[:, 0:2048].rearrange("p (h s) -> p h s", h=R_HEADS)
        cosT, sinT = tab[:, 2048:2560], tab[:, 2560:3072]
        dist, pTb, tri = tab[:, 0:1280], tab[:, 1280:2560], tab[:, 2560:3072]
        wsT = scr[:, 0:512].rearrange("p (g t) -> p g t", g=4)
        bsb = scr[:, 512:1024].rearrange("p (g t) -> p g t", g=4)
        ident, perm = cst[:, C_ID:C_ID + P], cst[:, C_PERM:C_PERM + P]
        ones, causal = cst[:, C_ONES:C_ONES + P], cst[:, C_CAUSAL:C_CAUSAL + P]
        edge = cst[:, C_EDGE:C_EDGE + 64].rearrange("p (g t) -> p g t", g=4)
        epsc = cst[:, C_EPS:C_EPS + 1]
        Mf = act3[:, 2 * KT:3 * KT].rearrange("p k s -> p (k s)")
        Qr, Kr = Mf[:, 0:512], Mf[:, 512:1024]
        Vr = Mf[:, 1024:2048].rearrange("p (j e) -> p j e", j=TT)
        sT = Mf[:, 2048:3328]
        rT = Mf[:, 3328:3840]
        sT_at = [0, 512, 896, 1152]
        Qa, Ka = hF[:, 0:512], hF[:, 512:1024]
        Va = hF[:, 1024:1536].rearrange("p (j e) -> p j e", j=TT)
        Pa = [hF[:, 1536:2048], hF[:, 2048:2560]]
        pTa = [hF[:, 2560:3072], hF[:, 3072:3584]]
        cT = hF[:, 3584:4096]
        sel = hF[:, 4096:4352].rearrange("p (a b) -> p a b", a=2)
        wfraw = yF[:, 0:128]
        lf = yF[:, 128:512].rearrange("p (a b) -> p a b", a=6)
        Vall = hF[:, 0:6144].rearrange("p (g j e) -> p g j e", g=3, j=TT)
        Qb = yF[:, 2048:3584].rearrange("p (g s) -> p g s", g=3)
        Kb = yF[:, 6144:7680].rearrange("p (g s) -> p g s", g=3)
        Vb = st[:, 0:3].rearrange("p g (j e) -> p g j e", j=TT)
        Pb = [scr[:, 0:1280], hF[:, 6144:7424]]
        wfH = sb("wfH", [P, KT, 16], F32R)
        wfL = sb("wfL", [P, KT, 16], F32R)

        landed = [sem(f"landed{s}") for s in range(RING)]
        hi_ready = sem("hi_ready")
        lo_ready = sem("lo_ready")
        tile_done = sem("tile_done")
        bank_free = sem("bank_free")
        st_free = sem("st_free")
        setup_in = sem("setup_in")
        pos_in = sem("pos_in")
        vec_seen = sem("vec_seen")
        vec_in = sem("vec_in")
        tab_in = sem("tab_in")
        ws_ready = sem("ws_ready")
        layer_done = sem("layer_done")
        c_act = sem("c_act")
        c_ready = sem("c_ready")
        trig_arg = sem("trig_arg")
        trig = sem("trig")
        squared = sem("squared")
        summed = sem("summed")
        rooted = sem("rooted")
        h_ready = sem("h_ready")
        y_ready = sem("y_ready")
        rope_full = sem("rope_full")
        rope_ready = sem("rope_ready")
        vr_ready = sem("vr_ready")
        score_full = sem("score_full")
        score_ready = sem("score_ready")
        o_full = sem("o_full")
        o_normed = sem("o_normed")
        v_mean = sem("v_mean")
        x_ready = sem("x_ready")
        v_normed = sem("v_normed")
        mix_full = sem("mix_full")
        mix_free = sem("mix_free")
        f_full = sem("f_full")
        z_ready = sem("z_ready")
        e_ready = sem("e_ready")
        c_full = sem("c_full")
        c_out = sem("c_out")
        wf_ready = sem("wf_ready")
        staged = sem("staged")
        sel_ready = sem("sel_ready")
        s_full = sem("s_full")
        max_ready = sem("max_ready")
        p_ready = sem("p_ready")
        p_normed = sem("p_normed")
        t_full = sem("t_full")
        t_ready = sem("t_ready")
        pv_done = sem("pv_done")
        conv_done = sem("conv_done")
        gated = sem("gated")
        out_ready = sem("out_ready")
        out_done = sem("out_done")

        block = ctx.enter_context(nc.Block())

        B_IT = [[(g, j) for g in range(3) for j in range(TT) if j <= it and (g or j >= it - 1)] for it in range(TT)]
        A_IT = [[(0, j) for j in range(it + 1)] for it in range(TT)]

        @block.sync
        def _(sp):
            for dst, src in ((cst[:], consts), (x[:], xT), (cs[:, 0], cvec), (tab[:, 0:2048], decay), (v2[:], vec2)):
                sp.dma_start(dst, src).then_inc(setup_in, 16)
            freed = Count()
            with repeat(sp, TILES // RING, {freed: RING}) as i:
                for s in range(RING):
                    sp.wait_ge(lo_ready, freed.next())
                    sp.dma_start(raw[:, s], stream[bass.ds(i * RING + s, 1)].rearrange("a p c -> (a p) c")
                                 ).then_inc(landed[s], 16)
            for n in range(KT):
                sp.wait_ge(out_ready, n + 1)
                sp.dma_start(outT[:, n], act3[:, n]).then_inc(out_done, 16)
            sp.wait_ge(out_done, 16 * KT)

        @block.gpsimd
        def _(pool):
            pool.dma_start(st[:, 3].bitcast(I32), pos).then_inc(pos_in, 16)
            banks, heads, layers, vecs = Count(4), Count(1), Count(), Count()
            v_tok = act3[:, KT:2 * KT].rearrange("p (j a) s -> p j (a s)", j=TT)
            with repeat(pool, LAYERS, {banks: LAYER_TILES + 4, heads: 2 * R_HEADS, layers: 1, vecs: 48}) as l:
                pool.wait_ge(layer_done, layers.next())
                pool.dma_start(v1[:], vec1[bass.ds(l, 1)].rearrange("a p c -> (a p) c")).then_inc(vec_in, 16)
                pool.dma_start(scr[:, 0:512], ws[bass.ds(l, 1)].rearrange("a p c -> (a p) c")).then_inc(vec_in, 16)
                pool.dma_start(scr[:, 512:1024], bs[bass.ds(l, 1)].to_broadcast([P, 512])).then_inc(vec_in, 16)
                pool.wait_ge(vec_in, vecs.next(48))
                pool.sem_inc(vec_seen, 1)
                pool.affine_select(out=wsT, in_=wsT, pattern=[[0, 4], [1, P]], compare_op=ALU.is_ge, fill=0.0,
                                   base=0, channel_multiplier=-1).then_inc(ws_ready, 1)
                banks.next(N_ADA + 16)
                with repeat(pool, R_HEADS, {heads: 2}) as h:
                    pool.wait_ge(bank_free, banks.value())
                    pool.wait_ge(o_full, heads.value())
                    heads.next(2)
                    pool.tensor_copy(Vr, v_tok[:, :, bass.ds(h * R_V, R_V)]).then_inc(vr_ready, 1)
                banks.next(LAYER_TILES + 4 - N_ADA - 16)
            pool.wait_ge(layer_done, 1 + LAYERS)
            pool.dma_start(tab[:, 0:1280], tables[:, 0:1280]).then_inc(tab_in, 16)
            pool.dma_start(tri, tables[:, 1280:1792]).then_inc(tab_in, 16)
            pool.dma_start(wfraw, wf).then_inc(tab_in, 16)
            steps = Count(1)
            pool.wait_ge(bank_free, banks.next(24))
            v_tok = act3[:, 16:24].rearrange("p (j a) s -> p j (a s)", j=TT)
            with repeat(pool, A_HEADS // 2, {steps: 8}) as p:
                pool.wait_ge(pv_done, steps.value())
                steps.next(8)
                pool.tensor_copy(Qa, act3[:, bass.ds(p, 1), :].rearrange("p a s -> p (a s)"))
                pool.tensor_copy(Ka, act3[:, bass.ds(p + 8, 1), :].rearrange("p a s -> p (a s)"))
                pool.tensor_copy(Va, v_tok[:, :, bass.ds(p * P, P)])
                pool.drain().then_inc(staged, 1)
            pool.wait_ge(bank_free, banks.next(8 + FFN2_TILES + 36))
            q12 = act3[:, 0:12].rearrange("p (g n) s -> p g n s", g=3)
            k12 = act3[:, 12:24].rearrange("p (g n) s -> p g n s", g=3)
            with repeat(pool, 4, {steps: 8}) as p:
                pool.wait_ge(pv_done, steps.value())
                steps.next(8)
                for g in range(3):
                    pool.tensor_copy(Qb[:, g:g + 1], q12[:, g, bass.ds(p, 1), :])
                    pool.tensor_copy(Kb[:, g:g + 1], k12[:, g, bass.ds(p, 1), :])
                    pool.tensor_copy(Vb[:, g], Vall[:, g, :, bass.ds(p * P, P)])
                pool.drain().then_inc(staged, 1)

        @block.tensor
        def _(pe):
            tiles, banks = Count(4), Count()
            h_k, y_k = Count(), Count()
            sq, rope, vr, sc, vn, mix = (Count() for _ in range(6))
            on = Count(1)
            pe.sem_inc(tile_done, 4)
            for one_ahead in (o_full, pv_done, t_full):
                pe.sem_inc(one_ahead, 1)

            def three(out, whi, wlo, ahi, alo, first, last):
                pe.matmul(out, whi, ahi, start=first, stop=False)
                pe.matmul(out, whi, alo, start=False, stop=False)
                return pe.matmul(out, wlo, ahi, start=False, stop=last)

            def tile_T(s, aH, aL, ks=KT, ready=None):
                pe.wait_ge(lo_ready, tiles.next())
                pe.wait_ge(bank_free, banks.next())
                for k in range(ks):
                    if ready is not None:
                        pe.wait_ge(ready[0], ready[1] + k + 1)
                    w = slice(k * P, (k + 1) * P)
                    ins = three(pb[:, s], hi[:, s, w], lo[:, s, w], aH[:, k], aL[:, k], k == 0, k == ks - 1)
                ins.then_inc(tile_done, 1)

            def tiles_T(n, aH, aL, ready, ks=KT):
                with repeat(pe, n // RING, {tiles: RING, banks: RING}):
                    for s in range(RING):
                        tile_T(s, aH, aL, ks, ready if s == 0 else None)

            def tiles_N(groups, aH, aL):
                with repeat(pe, groups, {tiles: RING, banks: RING}):
                    pe.wait_ge(bank_free, banks.next(4))
                    for s in range(RING):
                        pe.wait_ge(lo_ready, tiles.next())
                        for t in range(TT):
                            for kk in range(2):
                                k = 2 * s + kk
                                w, a = slice(kk * S, (kk + 1) * S), slice(t * P, (t + 1) * P)
                                pe.matmul(pb[:, t], aH[:, k, a], hi[:, s, w], start=k == 0, stop=False)
                                pe.matmul(pb[:, t], aL[:, k, a], hi[:, s, w], start=False, stop=False)
                                ins = pe.matmul(pb[:, t], aH[:, k, a], lo[:, s, w], start=False, stop=k == KT - 1)
                        ins.then_inc(tile_done, 1)

            def norm_sum():
                for k in range(KT):
                    pe.wait_ge(squared, sq.next())
                    ins = pe.matmul(pb[:, 4], ones, A[:, k], start=k == 0, stop=k == KT - 1)
                ins.then_inc(summed, 1)

            def gated_pairs():
                with repeat(pe, 4, {tiles: RING, banks: RING}):
                    for s in range(RING):
                        if s % 2:
                            tile_T(s, yH, yL, KT, (y_ready, y_k.value()) if s == 1 else None)
                        else:
                            tile_T(s, hH, hL)

            with repeat(pe, LAYERS, {tiles: LAYER_TILES, banks: LAYER_TILES + 4, h_k: 16, y_k: 72, sq: 24,
                                     rope: 8, vr: 4, sc: 16, on: 8, vn: 4, mix: 8}) as l:
                pe.wait_ge(c_ready, 1)
                with repeat(pe, N_ADA // RING, {tiles: RING, banks: RING}):
                    for s in range(RING):
                        pe.wait_ge(lo_ready, tiles.next())
                        pe.wait_ge(bank_free, banks.next())
                        for k in range(KT):
                            w = slice(k * P, (k + 1) * P)
                            ins = three(pb[:, s, 0:2], hi[:, s, w], lo[:, s, w], cH[:, k], cL[:, k], k == 0, k == 7)
                        ins.then_inc(tile_done, 1)
                norm_sum()
                h0 = h_k.value()
                h_k.next(8)
                tiles_T(8, hH, hL, (h_ready, h0))
                tiles_N(2, hH, hL)
                with repeat(pe, R_HEADS, {rope: 2, vr: 1, sc: 4, on: 2, sq: 2}) as h:
                    pe.wait_ge(bank_free, banks.value(-4))
                    pe.wait_ge(o_normed, on.value())
                    for j in range(2):
                        pe.matmul(pb[:, 4 + j:5 + j], perm, act3[:, bass.ds(h + 4 * j, 1), :],
                                  start=True, stop=True).then_inc(rope_full, 1)
                    pe.wait_ge(rope_ready, rope.next(2))
                    for j in range(TT):
                        if j >= 2:
                            pe.wait_ge(score_ready, sc.value() + j - 1)
                        pe.matmul(pb[:, 6 + j % 2, 0:S - j * P], Kr[:, j * P:(j + 1) * P], Qr[:, j * P:S],
                                  start=True, stop=True).then_inc(score_full, 1)
                    pe.wait_ge(vr_ready, vr.next())
                    for e in range(2):
                        for j in range(TT):
                            if e == 0:
                                pe.wait_ge(score_ready, sc.next())
                            ins = pe.matmul(pb[:, 4 + e, j * P:S], Vr[:, j, e * P:(e + 1) * P],
                                            sT[:, sT_at[j]:sT_at[j] + S - j * P], start=j == 0, stop=j == TT - 1)
                        ins.then_inc(o_full, 1)
                    for e in range(2):
                        pe.wait_ge(squared, sq.next())
                        ins = pe.matmul(pb[:, 6], ones, Mf[:, e * S:(e + 1) * S], start=e == 0, stop=e == 1)
                    ins.then_inc(summed, 1)
                    on.next(2)
                tiles_T(8, hH, hL, None)
                gated_pairs()
                y_k.next(8)
                tiles_T(8, hH, hL, None)
                tiles_N(2, hH, hL)
                pe.wait_ge(ws_ready, l + 1)
                pe.wait_ge(v_normed, vn.next(4))
                for n in range(KT):
                    pe.wait_ge(mix_free, mix.next())
                    for t in range(TT):
                        ins = pe.matmul(pb[:, 4 + n % 2, t * P:(t + 1) * P],
                                        B[:, 2 * t + n // 4, (n % 4) * P:(n % 4 + 1) * P], wsT[:, n // 2],
                                        start=True, stop=True)
                    ins.then_inc(mix_full, 1)
                gated_pairs()
                y_k.next(8)
                tiles_T(8, hH, hL, None)
                for g in range(4):
                    pe.wait_ge(lo_ready, tiles.next())
                    pe.wait_ge(bank_free, banks.next(2))
                    pe.wait_ge(y_ready, y_k.next(2))
                    for e in range(2):
                        for k in range(2):
                            w = slice(k * 256 + e * P, k * 256 + (e + 1) * P)
                            ins = three(pb[:, (2 * g + e) % 4], hi[:, g, w], lo[:, g, w], yH[:, 2 * g + k],
                                        yL[:, 2 * g + k], k == 0, k == 1)
                    ins.then_inc(tile_done, 1)
                gated_pairs()
                y_k.next(8)
                y0 = y_k.value()
                y_k.next(8)
                tiles_T(8, yH, yL, (y_ready, y0))
                norm_sum()
                h0 = h_k.value()
                h_k.next(8)
                with repeat(pe, 4, {tiles: 16, banks: 16, y_k: 8}):
                    tiles_T(8, hH, hL, (h_ready, h0))
                    tiles_T(8, yH, yL, (y_ready, y_k.value()))
                    y_k.next(8)

            st_, mx, pn, tr, ofr, el = Count(), Count(), Count(1), Count(1), Count(), Count()

            def attention(pairs, its, scores, value, tbank, groups_T, obank):
                with repeat(pe, pairs, {st_: 1, mx: 8, pn: 8, tr: 8, ofr: 1, el: 2}) as p:
                    pe.wait_ge(staged, st_.next())
                    for n in range(10):
                        if n < 8:
                            hp, it = n // 4, n % 4
                            scores(n, hp, it)
                        if 1 <= n <= 8:
                            m, it = n - 1, (n - 1) % 4
                            pe.wait_ge(p_normed, pn.value() + m + 1)
                            nb = len(its[it])
                            for b in range(nb):
                                ins = pe.transpose(pb[:, tbank(m, b), (b % 4) * P:(b % 4 + 1) * P],
                                                   groups_T(m)[:, b * P:(b + 1) * P], ident)
                            ins.then_inc(t_full, 1)
                        if n >= 2:
                            m, hp, it = n - 2, (n - 2) // 4, (n - 2) % 4
                            if m == 0:
                                pe.wait_ge(y_ready, y_base[0] + ofr.value())
                            pe.wait_ge(t_ready, tr.value() + m + 1)
                            blocks = its[it]
                            for b, (g, j) in enumerate(blocks):
                                rhs, lhsT = value(m, b, g, j, hp)
                                ins = pe.matmul(pb[hp * 64:(hp + 1) * 64, obank, it * P:(it + 1) * P], lhsT, rhs,
                                                start=b == 0, stop=b == len(blocks) - 1)
                            ins.then_inc(pv_done, 1)
                    mx.next(8), pn.next(8), tr.next(8), ofr.next(1), el.next(2)

            def conv_ffn(last=False):
                norm_sum()
                h0 = h_k.value()
                h_k.next(8)
                for n in SLABS:
                    tiles_T(2 * n, hH, hL, (h_ready, h0))
                    tiles_T(8, yH, yL, (y_ready, y_k.value()), ks=n)
                    y_k.next(n)

            norm_sum()
            norm_sum()
            h0 = h_k.value()
            h_k.next(8)
            pe.wait_ge(wf_ready, 1)
            for t in range(TT):
                for k in range(KT):
                    pe.wait_ge(h_ready, h0 + k + 1)
                    a = slice(t * P, (t + 1) * P)
                    out = pb[:, 4, t * 16:(t + 1) * 16]
                    pe.matmul(out, hH[:, k, a], wfH[:, k], start=k == 0, stop=False)
                    pe.matmul(out, hL[:, k, a], wfH[:, k], start=False, stop=False)
                    ins = pe.matmul(out, hH[:, k, a], wfL[:, k], start=False, stop=k == KT - 1)
            ins.then_inc(f_full, 1)
            tiles_T(16, hH, hL, None)
            pe.wait_ge(z_ready, 2)
            for t in range(TT):
                ins = pe.matmul(pb[0:16, 5, t * P:S], lf[:, 5, t * 16:(t + 1) * 16], tri[:, 0:S - t * P],
                                start=t == 0, stop=t == TT - 1)
            ins.then_inc(c_full, 1)
            tiles_N(2, hH, hL)
            pe.wait_ge(c_out, 1)

            def scores_a(n, hp, it):
                w = (it + 1) * P
                if n >= 2:
                    pe.wait_ge(p_ready, pn.value() + n - 1)
                elif n == 0:
                    pe.wait_ge(p_ready, pn.value())
                if it == 0:
                    pe.wait_ge(sel_ready, el.value() + hp + 1)
                a = slice(hp * 64, (hp + 1) * 64)
                out = pb[:, n % 2]
                pe.matmul(out[:, 0:w], Qa[a, it * P:(it + 1) * P], Ka[a, 0:w], start=True, stop=False)
                pe.matmul(out[:, 0:w], sel[0:16, hp], cT[0:16, 0:w], start=False, stop=False)
                pe.matmul(out[:, it * P:w], ident, causal, start=False, stop=True).then_inc(s_full, 1)

            y_base = [y_k.value()]
            attention(A_HEADS // 2, A_IT, scores_a,
                      lambda m, b, g, j, hp: (pTa[m % 2][:, b * P:(b + 1) * P], Va[:, j, hp * 64:(hp + 1) * 64]),
                      lambda m, b: 2 + m % 2, lambda m: Pa[m % 2], 6)
            tiles_T(8, yH, yL, (y_ready, y_base[0]))
            y_k.next(8)
            conv_ffn()
            norm_sum()
            h0 = h_k.value()
            h_k.next(8)
            tiles_T(12, hH, hL, (h_ready, h0))
            tiles_T(12, yH, yL, (y_ready, y_k.value()))
            y_k.next(8)
            tiles_N(3, yH, yL)
            y_base = [y_k.value()]
            ofr = Count()

            def scores_b(n, hp, it):
                if n == 0:
                    pe.wait_ge(t_ready, tr.value())
                elif n >= 2:
                    pe.wait_ge(t_ready, tr.value() + n - 1)
                a = slice(hp * 64, (hp + 1) * 64)
                for g in range(3):
                    first = max(0, it - 1) if g == 0 else 0
                    ins = pe.matmul(pb[:, 3 * (n % 2) + g, 0:(it + 1 - first) * P], Qb[a, g, it * P:(it + 1) * P],
                                    Kb[a, g, first * P:(it + 1) * P], start=True, stop=True)
                ins.then_inc(s_full, 1)

            attention(4, B_IT, scores_b,
                      lambda m, b, g, j, hp: (pTb[:, b * P:(b + 1) * P], Vb[:, g, j, hp * 64:(hp + 1) * 64]),
                      lambda m, b: 3 * (m % 2) + b // 4, lambda m: Pb[m % 2], 6)
            pe.wait_ge(y_ready, y_base[0] + 4)
            y_k.next(4)
            for s in range(RING):
                pe.wait_ge(lo_ready, tiles.next())
                pe.wait_ge(bank_free, banks.next(2))
                for e in range(2):
                    for k in range(4):
                        w = slice((4 * e + k) * P, (4 * e + k + 1) * P)
                        ins = three(pb[:, (2 * s + e) % 4], hi[:, s, w], lo[:, s, w], yH[:, k], yL[:, k], k == 0, k == 3)
                ins.then_inc(tile_done, 1)
            conv_ffn(last=True)
            norm_sum()
            assert tiles.n == TILES + 4, (tiles.n, TILES)

        @block.scalar
        def _(act):
            split, done, stf = Count(), Count(4), Count()
            land = [Count() for _ in range(RING)]
            ring = {split: RING, done: RING, **{c: 16 for c in land}}
            act.sem_inc(bank_free, 4)
            act.sem_inc(p_ready, 1)
            act.sem_inc(t_ready, 1)
            left = [TILES]

            def tick(s, static=None):
                s = (s + AHEAD) % RING
                if static is not None and static + AHEAD >= TILES:
                    return
                act.wait_ge(landed[s], land[s].next(16))
                act.wait_ge(tile_done, split.next())
                act.activation(hi[:, s], raw[:, s], ACT.Copy).then_inc(hi_ready, 1)

            def bodies(n, steps, body, last=False):
                if last:
                    for i in range(n):
                        body(i)
                else:
                    with repeat(act, n, {**ring, **steps}) as i:
                        body(i)

            def to_st(s, scale=1.0, bias=0.0, func=ACT.Identity, bank=None):
                act.wait_ge(st_free, stf.next())
                b = s if bank is None else bank
                act.activation(st[:, s:s + 1], pb[:, b:b + 1], func, bias=bias, scale=scale).then_inc(bank_free, 1)

            def tiles_T(n, drain, uses_st=True, last=False, where=None):
                def body(i):
                    for s in range(RING):
                        t = None if not last else TILES - RING * (n // RING - i) + s
                        tick(s, t)
                        act.wait_ge(tile_done, done.next())
                        drain(i, s)
                bodies(n // RING, {stf: RING} if uses_st else {}, body, last)

            def tiles_N(groups, drain):
                def body(i):
                    for s in range(RING):
                        tick(s)
                    act.wait_ge(tile_done, done.next(4))
                    for t in range(TT):
                        drain(i, t)
                bodies(groups, {}, body)

            sums = Count()

            def norm():
                act.wait_ge(st_free, stf.value(-4))
                for k in range(KT):
                    act.activation(A[:, k], x[:, k], ACT.Square).then_inc(squared, 1)
                act.wait_ge(summed, sums.next())
                act.activation(st[:, 0], pb[:, 4], ACT.Sqrt, bias=epsc, scale=1.0 / D).then_inc(rooted, 1)

            for s in range(AHEAD):
                tick(s - AHEAD)
            act.wait_ge(setup_in, 80)
            act.activation(cs[:, 1], cs[:, 0], ACT.Silu).then_inc(c_act, 1)
            act.wait_ge(trig_arg, 1)
            act.activation(sinT, st[:, 1], ACT.Sin).then_inc(trig, 1)
            act.activation(st[:, 2], st[:, 1], ACT.Abs)
            act.drain()
            act.activation(cosT, st[:, 2], ACT.Sin, scale=-1.0, bias=cst[:, C_HALFPI:C_HALFPI + 1]).then_inc(trig, 1)

            def pairs():
                def drain(i, s):
                    to_st(s, func=ACT.Identity if s % 2 else ACT.Sigmoid)
                tiles_T(16, drain)

            vecs, of, means = Count(), Count(1), Count()
            with repeat(act, LAYERS, {split: LAYER_TILES, done: LAYER_TILES, stf: 8 + 48 + 8 + 8 + 64,
                                      sums: 6, means: 1, vecs: 1, of: 8, **{c: LAYER_TILES // RING * 16 for c in land}}) as l:
                act.wait_ge(vec_seen, vecs.next())

                def drain_mod(i, s):
                    act.activation(mod[:, bass.ds(i * RING + s, 1)], pb[:, s, 0:1], ACT.Identity,
                                   bias=v1[:, bass.ds(i * RING + s + V_ADA, 1)]).then_inc(bank_free, 1)
                tiles_T(N_ADA, drain_mod, uses_st=False)
                norm()

                def drain_to(first, func):
                    def drain(i, s):
                        act.activation(act3[:, bass.ds(i * RING + s + first, 1), :], pb[:, s:s + 1], func
                                       ).then_inc(bank_free, 1)
                    return drain

                def drain_tok(first, func):
                    def drain(i, t):
                        act.activation(act3[:, bass.ds(i + first + 2 * t, 1), :], pb[:, t:t + 1], func
                                       ).then_inc(bank_free, 1)
                    return drain
                tiles_T(8, drain_to(0, ACT.Copy), uses_st=False)
                tiles_N(2, drain_tok(8, ACT.Copy))
                with repeat(act, R_HEADS, {of: 2, sums: 1}):
                    for e in range(2):
                        act.wait_ge(o_full, of.next())
                        if e == 0:
                            act.wait_ge(o_full, of.value(-1))
                        act.activation(Mf[:, e * S:(e + 1) * S], pb[:, 4 + e], ACT.Square).then_inc(squared, 1)
                    act.wait_ge(summed, sums.next())
                    act.activation(sT[:, 0:S], pb[:, 6], ACT.Sqrt, bias=epsc, scale=1.0 / R_V).then_inc(rooted, 1)
                tiles_T(8, lambda i, s: to_st(s, func=ACT.Silu))
                pairs()
                tiles_T(8, drain_to(0, ACT.Gelu_apprx_tanh), uses_st=False)
                tiles_N(2, drain_tok(8, ACT.Gelu_apprx_tanh))
                act.wait_ge(v_mean, means.next())
                act.activation(stat[:, 8:12], stat[:, 12:16], ACT.Sqrt).then_inc(rooted, 1)
                pairs()
                tiles_T(8, drain_to(0, ACT.Copy), uses_st=False)
                for g in range(4):
                    tick(g)
                    act.wait_ge(tile_done, done.next())
                    for e in range(2):
                        n = 2 * g + e
                        to_st(n % 4, scale=v1[:, V_PS + n:V_PS + n + 1], bias=bpps[:, n:n + 1])
                pairs()
                tiles_T(8, lambda i, s: to_st(s, scale=mod[:, bass.ds(i * RING + s + 16, 1)]))
                norm()
                with repeat(act, 4, {split: 16, done: 16, stf: 16, **{c: 64 for c in land}}):
                    tiles_T(8, lambda i, s: to_st(s))
                    tiles_T(8, lambda i, s: to_st(s, scale=mod[:, bass.ds(i * RING + s + 40, 1)]))

            cv = Count()

            def conv_ffn(last=False):
                norm()
                for j, n in enumerate(SLABS):
                    def body(i):
                        for s in range(RING):
                            tick(s)
                            act.wait_ge(tile_done, done.next())
                            to_st(s)
                            if s % 2:
                                act.wait_ge(conv_done, cv.next())
                                act.activation(A[:, s], A[:, s], ACT.Silu).then_inc(gated, 1)
                    bodies(n // 2, {stf: RING, cv: 2}, body)
                    tiles_T(8, lambda i, s: to_st(s), last=last and j == len(SLABS) - 1)

            norm()
            act.wait_ge(x_ready, 1)
            norm()

            def drain_q(scale, first):
                def drain(i, s):
                    act.activation(act3[:, bass.ds(i * RING + s + first, 1), :], pb[:, s:s + 1], ACT.Copy,
                                   scale=scale).then_inc(bank_free, 1)
                return drain
            act.wait_ge(z_ready, 1)
            act.activation(lf[:, 1], lf[:, 0], ACT.Abs)
            act.drain()
            act.activation(lf[:, 2], lf[:, 1], ACT.Exp, scale=-1.0)
            act.drain()
            act.activation(lf[:, 3], lf[:, 2], ACT.Ln, bias=1.0).then_inc(e_ready, 1)
            tiles_T(8, drain_q(0.125, 0), uses_st=False)
            tiles_T(8, drain_q(1.0, 8), uses_st=False)

            def drain_v(i, t):
                act.activation(act3[:, bass.ds(i + 16 + 2 * t, 1), :], pb[:, t:t + 1], ACT.Copy).then_inc(bank_free, 1)
            tiles_N(2, drain_v)
            mx, tf, pvc = Count(), Count(1), Count(1)

            def attention(pairs_, its, exp_in, exp_out, copies):
                with repeat(act, pairs_, {mx: 8, tf: 8, pvc: 8}):
                    for n in range(9):
                        if n < 8:
                            it = n % 4
                            act.wait_ge(max_ready, mx.next())
                            w = len(its[it]) * P
                            act.activation(exp_out(n)[:, 0:w], exp_in(n, w), ACT.Exp, bias=stat[:, n % 2:n % 2 + 1],
                                           accum_out=stat[:, 2 + n % 2:3 + n % 2])
                            act.drain().then_inc(p_ready, 1)
                        if n >= 1:
                            m = n - 1
                            act.wait_ge(t_full, tf.next())
                            copies(m, len(its[m % 4]), pvc)
                    pvc.next(8)

            def copies_a(m, nb, pvc):
                act.wait_ge(pv_done, pvc.value() + max(0, m - 1))
                act.activation(pTa[m % 2][:, 0:nb * P], pb[:, 2 + m % 2, 0:nb * P], ACT.Copy).then_inc(t_ready, 1)

            attention(A_HEADS // 2, A_IT, lambda n, w: pb[:, n % 2, 0:w], lambda n: Pa[n % 2], copies_a)
            tiles_T(8, lambda i, s: to_st(s))
            conv_ffn()
            norm()
            tiles_T(12, drain_q(0.125, 0), uses_st=False)
            tiles_T(12, drain_q(1.0, 12), uses_st=False)

            def drain_vb(i, t):
                act.activation(Vall[:, bass.ds(i, 1), t], pb[:, t:t + 1], ACT.Copy).then_inc(bank_free, 1)
            tiles_N(3, drain_vb)

            def copies_b(m, nb, pvc):
                act.wait_ge(pv_done, pvc.value() + m)
                for b in range(0, nb, 4):
                    w = min(4, nb - b) * P
                    act.activation(pTb[:, b * P:b * P + w], pb[:, 3 * (m % 2) + b // 4, 0:w], ACT.Copy)
                act.drain().then_inc(t_ready, 1)

            attention(4, B_IT, lambda n, w: Pb[n % 2][:, 0:w], lambda n: Pb[n % 2], copies_b)
            for s in range(RING):
                tick(s)
                act.wait_ge(tile_done, done.next())
                for e in range(2):
                    to_st((2 * s + e) % 4)
            conv_ffn(last=True)
            norm()

        @block.vector
        def _(dve):
            split, drained = Count(), Count(4)
            ring = {split: RING, drained: RING}
            dve.sem_inc(lo_ready, 4)
            dve.sem_inc(st_free, 4)
            dve.sem_inc(o_normed, 1)
            dve.sem_inc(p_normed, 1)

            def tick(s, static=None):
                s = (s + AHEAD) % RING
                if static is not None and static + AHEAD >= TILES:
                    return
                dve.wait_ge(hi_ready, split.next())
                dve.tensor_tensor(lo[:, s], raw[:, s], hi[:, s].bitcast(F32), ALU.subtract).then_inc(lo_ready, 1)

            def bodies(n, body, last=False):
                if last:
                    for i in range(n):
                        body(i)
                else:
                    with repeat(dve, n, ring) as i:
                        body(i)

            def tiles_T(n, work, last=False):
                def body(i):
                    for s in range(RING):
                        t = None if not last else TILES - RING * (n // RING - i) + s
                        tick(s, t)
                        if work is None:
                            drained.next()
                        else:
                            dve.wait_ge(bank_free, drained.next())
                            work(i, s)
                bodies(n // RING, body, last)

            def tiles_N(groups):
                def body(i):
                    for s in range(RING):
                        tick(s)
                    drained.next(4)
                bodies(groups, body)

            def halves(src, dH, dL, by=1):
                dve.tensor_copy(dH, src)
                dve.drain()
                dve.tensor_tensor(dL, src, dH.bitcast(F32), ALU.subtract)
                dve.drain().then_inc(y_ready, by)

            roots = Count()

            def newton(bank, y, v, t, scale):
                dve.wait_ge(rooted, roots.next())
                dve.tensor_scalar(v, bank, scale, EPS, ALU.mult, ALU.add)
                dve.reciprocal(y, y)
                dve.drain()
                dve.scalar_tensor_tensor(t, y, -0.5, y, ALU.mult, ALU.mult)
                dve.drain()
                dve.tensor_tensor(t, t, v, ALU.mult)
                dve.drain()
                dve.scalar_tensor_tensor(y, t, 1.5, y, ALU.add, ALU.mult)
                dve.drain()

            def norm_to(gain, shift, dH, dL, ready):
                rstd, t = st[:, 0], st[:, 3]
                for k in range(KT):
                    dve.scalar_tensor_tensor(t, x[:, k], gain[:, k:k + 1], rstd, ALU.mult, ALU.mult)
                    dve.drain()
                    if shift is None:
                        dve.tensor_copy(dH[:, k], t)
                        dve.drain()
                        dve.tensor_tensor(dL[:, k], t, dH[:, k].bitcast(F32), ALU.subtract)
                    else:
                        dve.tensor_scalar(dH[:, k], t, shift[:, k:k + 1], None, ALU.add)
                        dve.drain()
                        dve.scalar_tensor_tensor(dL[:, k], t, shift[:, k:k + 1], dH[:, k].bitcast(F32), ALU.add,
                                                 ALU.subtract)
                    dve.drain().then_inc(ready, 1)

            def norm(gain, shift, dH, dL, ready):
                newton(pb[:, 4], st[:, 0], st[:, 1], st[:, 2], 1.0 / D)
                norm_to(gain, shift, dH, dL, ready)

            def add_to_x(i, s):
                n = bass.ds(i * RING + s, 1)
                dve.tensor_tensor(x[:, n], x[:, n], st[:, s:s + 1], ALU.add).then_inc(st_free, 1)

            for s in range(AHEAD):
                tick(s - AHEAD)
            dve.wait_ge(setup_in, 80)
            dve.wait_ge(pos_in, 16)
            pi2 = 2 * np.pi
            c1 = 6.28125
            c2 = float(np.float32(round((pi2 - c1) * 2 ** 21) / 2 ** 21))
            c3 = float(np.float32(pi2 - c1 - c2))
            dve.tensor_copy(st[:, 0], st[:, 3].bitcast(I32))
            dve.drain()
            dve.tensor_scalar(st[:, 1], st[:, 0], cst[:, C_FREQ:C_FREQ + 1], None, ALU.mult)
            dve.drain()
            dve.tensor_scalar(st[:, 2].bitcast(I32), st[:, 1], 1.0 / pi2, None, ALU.mult)
            dve.drain()
            dve.tensor_copy(st[:, 0], st[:, 2].bitcast(I32))
            dve.drain()
            for c in (c1, c2, c3):
                dve.scalar_tensor_tensor(st[:, 1], st[:, 0], -c, st[:, 1], ALU.mult, ALU.add)
                dve.drain()
            dve.tensor_scalar(st[:, 1], st[:, 1], 3.1415925, -3.1415925, ALU.min, ALU.max)
            dve.drain().then_inc(trig_arg, 1)
            dve.wait_ge(c_act, 1)
            for j in range(2):
                dve.tensor_copy(cH[:, :, j], cs[:, 1])
            dve.drain()
            for j in range(2):
                dve.tensor_tensor(cL[:, :, j], cs[:, 1], cH[:, :, j].bitcast(F32), ALU.subtract)
            dve.drain().then_inc(c_ready, 1)
            dve.wait_ge(trig, 2)
            dve.tensor_scalar(sinT, sinT, cst[:, C_SIGN:C_SIGN + 1], None, ALU.mult)
            dve.drain().then_inc(layer_done, 1)
            dve.sem_inc(mix_free, 2)

            rp, sc, mixed = Count(), Count(), Count()

            def pairs(first):
                def work(i, s):
                    if s % 2 == 0:
                        return
                    g, b = st[:, s - 1:s], st[:, s:s + 1]
                    n = bass.ds(i * 2 + s // 2 + 16, 1)
                    if first:
                        dve.tensor_tensor(act3[:, n], g, b, ALU.mult)
                    else:
                        dve.tensor_tensor(b, g, b, ALU.mult)
                        dve.drain()
                        dve.tensor_tensor(act3[:, n], act3[:, n], b, ALU.add)
                    dve.drain().then_inc(st_free, 2)
                tiles_T(16, work)

            def geff_of(norm_at, scale_at):
                dve.tensor_scalar(geff[:], mod[:, scale_at:scale_at + 8], 1.0, None, ALU.add)
                dve.drain()
                dve.tensor_tensor(geff[:], geff[:], v1[:, norm_at:norm_at + 8], ALU.mult)
                dve.drain()

            with repeat(dve, LAYERS, {split: LAYER_TILES, drained: LAYER_TILES + 4, roots: 7, rp: 8, sc: 16,
                                      mixed: 8}) as l:
                tiles_T(N_ADA, None)
                dve.wait_ge(bank_free, drained.value())
                dve.tensor_tensor(bpps[:], v1[:, V_BP:V_BP + 8], v1[:, V_PS:V_PS + 8], ALU.mult)
                geff_of(V_N1, 8)
                norm(geff, mod[:, 0:8], hH, hL, h_ready)
                tiles_T(8, None)
                tiles_N(2)
                with repeat(dve, R_HEADS, {rp: 2, sc: 4, roots: 1}) as h:
                    for j, dst in ((0, Qr), (1, Kr)):
                        f = 1.0 if j == 0 else float(P) ** -0.5
                        t = act3[:, bass.ds(h + 4 * j, 1), :].rearrange("p a s -> p (a s)")
                        dve.wait_ge(rope_full, rp.next())
                        dve.scalar_tensor_tensor(rT, pb[:, 4 + j], f, sinT, ALU.mult, ALU.mult)
                        dve.scalar_tensor_tensor(t, t, f, cosT, ALU.mult, ALU.mult)
                        dve.drain()
                        dve.tensor_tensor(dst, t, rT, ALU.add)
                        dve.drain().then_inc(rope_ready, 1)
                    for j in range(TT):
                        w = S - j * P
                        dve.wait_ge(score_full, sc.next())
                        dve.tensor_tensor(sT[:, sT_at[j]:sT_at[j] + w].rearrange("p (a s) -> p a s", a=1),
                                          pb[:, 6 + j % 2:7 + j % 2, 0:w], dec[:, bass.ds(h, 1), 0:w],
                                          ALU.mult).then_inc(score_ready, 1)
                    newton(pb[:, 6], sT[:, 0:512], sT[:, 512:1024], rT, 1.0 / R_V)
                    for e in range(2):
                        dve.tensor_tensor(act3[:, bass.ds(h + 4 * e, 1), :].rearrange("p a s -> p (a s)"),
                                          pb[:, 4 + e], sT[:, 0:512], ALU.mult).then_inc(o_normed, 1)

                def y_ret(i, s):
                    o = act3[:, bass.ds(i * 2 + 4 * (s % 2) + s // 2, 1), :]
                    n = bass.ds(i * RING + s, 1)
                    dve.tensor_tensor(st[:, s:s + 1], st[:, s:s + 1], o, ALU.mult)
                    dve.drain()
                    halves(st[:, s:s + 1], yH[:, n], yL[:, n])
                    dve.sem_inc(st_free, 1)
                tiles_T(8, y_ret)
                pairs(True)
                tiles_T(8, None)
                tiles_N(2)
                dve.wait_ge(bank_free, drained.value())
                for t in range(TT):
                    vt = act3[:, 8 + 2 * t:10 + 2 * t].rearrange("p a s -> p (a s)")
                    dve.tensor_tensor_reduce(yF[:, 0:1024], vt, vt, 1.0, 0.0, ALU.mult, ALU.add,
                                             stat[:, 8 + t:9 + t])
                    dve.drain()
                dve.tensor_scalar(stat[:, 12:16], stat[:, 8:12], 1.0 / D, EPS, ALU.mult, ALU.add)
                dve.drain().then_inc(v_mean, 1)
                y, v, t = stat[:, 8:12], stat[:, 12:16], stat[:, 4:8]
                dve.wait_ge(rooted, roots.next())
                dve.reciprocal(y, y)
                dve.drain()
                dve.scalar_tensor_tensor(t, y, -0.5, y, ALU.mult, ALU.mult)
                dve.drain()
                dve.tensor_tensor(t, t, v, ALU.mult)
                dve.drain()
                dve.scalar_tensor_tensor(y, t, 1.5, y, ALU.add, ALU.mult)
                dve.drain()
                for t in range(TT):
                    vt = act3[:, 8 + 2 * t:10 + 2 * t].rearrange("p a s -> p (a s)")
                    dve.tensor_scalar(vt, vt, stat[:, 8 + t:9 + t], None, ALU.mult).then_inc(v_normed, 1)
                for n in range(KT):
                    dve.wait_ge(mix_full, mixed.next())
                    pv = pb[:, 4 + n % 2]
                    pv4 = pv.rearrange("p (n t) -> p n t", n=TT)
                    b4 = bsb[:, n // 2:n // 2 + 1].to_broadcast([P, TT, P])
                    dve.scalar_tensor_tensor(pv4, pv4, v1[:, V_GAIN + n:V_GAIN + n + 1], b4, ALU.mult, ALU.add)
                    dve.drain()
                    dve.tensor_tensor(A[:, n], A[:, n], pv, ALU.mult)
                    dve.drain().then_inc(mix_free, 1)
                    halves(A[:, n], yH[:, n], yL[:, n])
                pairs(False)
                tiles_T(8, None)
                dve.wait_ge(bank_free, drained.value())
                for g in range(4):
                    src, cur = A[:, 2 * g:2 * g + 2], A[:, 2 * g:2 * g + 2]
                    for j in range(g + 1):
                        d, dst = 2 ** j, B[:, 2 * (j % 2):2 * (j % 2) + 2]
                        dve.tensor_tensor(dst[:, :, d:S], cur[:, :, d:S], cur[:, :, 0:S - d], ALU.add)
                        dve.tensor_copy(dst[:, :, 0:d], cur[:, :, 0:d])
                        dve.drain()
                        cur = dst
                    for j in range(2):
                        dve.tensor_tensor(cur[:, j, 0:16], cur[:, j, 0:16], edge[:, g], ALU.mult)
                    dve.drain()
                    dst = B[:, 4:6]
                    dve.scalar_tensor_tensor(dst, cur, 1.0 / 2 ** (g + 1), src, ALU.mult, ALU.subtract)
                    dve.drain()
                    halves(dst, yH[:, 2 * g:2 * g + 2], yL[:, 2 * g:2 * g + 2], 2)
                for g in range(4):
                    tick(g)
                    for e in range(2):
                        n = 2 * g + e
                        dve.wait_ge(bank_free, drained.next())
                        halves(st[:, n % 4], yH[:, n], yL[:, n])
                        dve.sem_inc(st_free, 1)
                pairs(False)
                for n in range(KT):
                    halves(M[:, n], yH[:, n], yL[:, n])
                tiles_T(8, add_to_x)
                geff_of(V_N2, 32)
                norm(geff, mod[:, 24:32], hH, hL, h_ready)
                with repeat(dve, 4, {split: 16, drained: 16}):
                    def hidden(i, s):
                        n = bass.ds(i * RING + s, 1)
                        u = st[:, s:s + 1]
                        dve.scalar_tensor_tensor(u, u, 0.0, u, ALU.max, ALU.mult)
                        dve.drain()
                        halves(u, yH[:, n], yL[:, n])
                        dve.sem_inc(st_free, 1)
                    tiles_T(8, hidden)
                    tiles_T(8, add_to_x)
                dve.drain().then_inc(layer_done, 1)

            gt = Count()

            def conv_ffn(layer, last=False):
                norm(v2[:, W_FFN + 8 * layer:W_FFN + 8 * layer + 8], None, hH, hL, h_ready)
                first = 0
                for j, n in enumerate(SLABS):
                    def body(i):
                        for s in range(RING):
                            tick(s)
                            dve.wait_ge(bank_free, drained.next())
                            ch = i * 2 + (first + s // 2 + (s % 2) * (FF2 // P))
                            w = [v2[:, bass.ds(ch + (W_CW + (layer * 3 + t) * UP), 1)] for t in range(3)]
                            b = v2[:, bass.ds(ch + (W_CB + layer * UP), 1)]
                            u, c = st[:, s], A[:, s]
                            dve.tensor_scalar(c, u, w[2], b, ALU.mult, ALU.add)
                            dve.drain()
                            dve.scalar_tensor_tensor(c[:, 1:S], u[:, 0:S - 1], w[1], c[:, 1:S], ALU.mult, ALU.add)
                            dve.drain()
                            dve.scalar_tensor_tensor(c[:, 2:S], u[:, 0:S - 2], w[0], c[:, 2:S], ALU.mult,
                                                     ALU.add).then_inc(st_free, 1)
                            dve.drain()
                            if s % 2:
                                dve.sem_inc(conv_done, 1)
                                dve.wait_ge(gated, gt.next())
                                a = A[:, s - 1:s]
                                dve.tensor_tensor(a, a, A[:, s:s + 1], ALU.mult)
                                dve.drain()
                                m = bass.ds(i * 2 + s // 2, 1)
                                halves(a, yH[:, m], yL[:, m])
                    with repeat(dve, n // 2, {**ring, gt: 2}) as i:
                        body(i)
                    first += n
                    tiles_T(8, add_to_x, last=last and j == len(SLABS) - 1)

            newton(pb[:, 4], st[:, 0], st[:, 1], st[:, 2], 1.0 / D)
            for k in range(KT):
                dve.scalar_tensor_tensor(x[:, k], x[:, k], v2[:, W_FIN1 + k:W_FIN1 + k + 1], st[:, 0], ALU.mult,
                                         ALU.mult)
            dve.drain().then_inc(x_ready, 1)
            dve.wait_ge(tab_in, 48)
            w3 = wfraw.rearrange("p (k n) -> p k n", k=KT)
            dve.tensor_copy(wfH[:], w3)
            dve.drain()
            dve.tensor_tensor(wfL[:], w3, wfH[:].bitcast(F32), ALU.subtract)
            dve.drain().then_inc(wf_ready, 1)
            norm(v2[:, W_MIX:W_MIX + 8], None, hH, hL, h_ready)
            dve.wait_ge(f_full, 1)
            for t in range(TT):
                dve.tensor_tensor(lf[:, 0, t * 16:(t + 1) * 16], pb[:, 4, t * 16:(t + 1) * 16],
                                  v2[:, W_BF:W_BF + 16], ALU.add)
            dve.drain().then_inc(z_ready, 1)
            dve.tensor_scalar(lf[:, 4], lf[:, 0], 0.0, None, ALU.min)
            dve.wait_ge(e_ready, 1)
            dve.drain()
            dve.tensor_tensor(lf[:, 5], lf[:, 4], lf[:, 3], ALU.subtract)
            dve.drain().then_inc(z_ready, 1)
            tiles_T(16, None)
            tiles_N(2)
            dve.wait_ge(bank_free, drained.value())
            dve.wait_ge(c_full, 1)
            dve.tensor_copy(cT[0:16], pb[0:16, 5])
            dve.drain().then_inc(c_out, 1)
            sf, pr, pvc, te = Count(), Count(1), Count(1), Count(1)

            def attention(pairs_, its, maximum, probs, start):
                with repeat(dve, pairs_, {sf: 8, pr: 8, pvc: 8, te: 8}) as p:
                    start(p)
                    for n in range(9):
                        if n < 8:
                            dve.wait_ge(s_full, sf.next())
                            maximum(n, n // 4, n % 4, p)
                            dve.drain().then_inc(max_ready, 1)
                        if n >= 1:
                            m = n - 1
                            w = len(its[m % 4]) * P
                            dve.wait_ge(p_ready, pr.next())
                            dve.reciprocal(stat[:, 4 + m % 2:5 + m % 2], stat[:, 2 + m % 2:3 + m % 2])
                            dve.drain()
                            dve.tensor_scalar(probs(m)[:, 0:w], probs(m)[:, 0:w], stat[:, 4 + m % 2:5 + m % 2], None,
                                              ALU.mult).then_inc(p_normed, 1)
                    dve.wait_ge(pv_done, pvc.next(8))
                    te.next(8)
                    n = bass.ds(p, 1)
                    dve.tensor_copy(yH[:, n], pb[:, 6:7])
                    dve.drain()
                    dve.tensor_tensor(yL[:, n], pb[:, 6:7], yH[:, n].bitcast(F32), ALU.subtract)
                    dve.drain().then_inc(y_ready, 1)

            def selectors(p):
                for j in range(2):
                    dve.tensor_scalar(sel[0:16, j], ones[0:16], cst[0:16, bass.ds(p * 2 + j + C_ID, 1)], -1.0,
                                      ALU.mult, ALU.mult).then_inc(sel_ready, 1)

            def maximum_a(n, hp, it, p):
                if n < 2:
                    dve.wait_ge(p_ready, pr.value())
                dve.wait_ge(t_full, te.value() + max(0, n - 1))
                dve.tensor_reduce(stat[:, n % 2:n % 2 + 1], pb[:, n % 2, 0:(it + 1) * P], AX.X, ALU.max, negate=True)

            attention(A_HEADS // 2, A_IT, maximum_a, lambda m: Pa[m % 2], selectors)
            tiles_T(8, add_to_x)
            conv_ffn(0)
            norm(v2[:, W_MIX + 8:W_MIX + 16], None, hH, hL, h_ready)
            norm_to(v2[:, W_KV:W_KV + 8], None, yH, yL, y_ready)
            tiles_T(24, None)
            tiles_N(3)
            dve.wait_ge(bank_free, drained.value())

            def maximum_b(n, hp, it, p):
                dve.wait_ge(t_full, te.value() + max(0, n - 1))
                sbuf, at = Pb[n % 2], 0
                for g in range(3):
                    first = max(0, it - 1) if g == 0 else 0
                    w = (it + 1 - first) * P
                    end = 256 + 512 * g
                    dve.scalar_tensor_tensor(sbuf[:, at:at + w], dist[:, end - w:end],
                                             cst[:, bass.ds(p * 2 + (C_SLOPE + 8 * g + hp), 1)],
                                             pb[:, 3 * (n % 2) + g, 0:w], ALU.mult, ALU.add)
                    at += w
                dve.drain()
                dve.tensor_reduce(stat[:, n % 2:n % 2 + 1], sbuf[:, 0:at], AX.X, ALU.max, negate=True)

            attention(4, B_IT, maximum_b, lambda m: Pb[m % 2], lambda p: None)
            for s in range(RING):
                tick(s)
                for e in range(2):
                    n = 2 * s + e
                    dve.wait_ge(bank_free, drained.next())
                    dve.tensor_tensor(x[:, n], x[:, n], st[:, n % 4], ALU.add).then_inc(st_free, 1)
            conv_ffn(1, last=True)
            newton(pb[:, 4], st[:, 0], st[:, 1], st[:, 2], 1.0 / D)
            for k in range(KT):
                dve.scalar_tensor_tensor(act3[:, k], x[:, k], v2[:, W_FIN + k:W_FIN + k + 1], st[:, 0], ALU.mult,
                                         ALU.mult).then_inc(out_ready, 1)


def constants():
    f = np.float32
    c = np.zeros((P, C_ALL), f)
    i, j = np.arange(P)[:, None], np.arange(P)[None]
    c[:, C_ID:C_ID + P] = i == j
    c[:, C_PERM:C_PERM + P] = (i + 64) % P == j
    c[:, C_ONES:C_ONES + P] = 1
    c[:, C_CAUSAL:C_CAUSAL + P] = np.where(j > i, f(NEG), f(0))
    for g in range(4):
        w = 2 ** (g + 1)
        c[:, C_EDGE + 16 * g:C_EDGE + 16 * g + 16] = w / np.minimum(np.arange(1, 17), w)
    half = P // 2
    freq = f(10000.0) ** (-np.arange(half, dtype=f) / f(half))
    c[:, C_FREQ] = np.concatenate([freq, freq])
    c[:, C_SIGN] = np.where(np.arange(P) < half, -1, 1)
    c[:, C_EPS] = EPS
    c[:, C_HALFPI] = np.pi / 2
    c[:, C_SLOPE:C_SLOPE + 24] = np.exp2(-8.0 * np.arange(1, 25) / 24)
    log_gamma = np.log1p(-np.power(2.0, -5.0 - np.arange(R_HEADS)))
    rel = np.arange(S)[None] - i
    decay = np.stack([np.where(rel >= 0, np.exp(lg * np.maximum(rel, 0)), 0) for lg in log_gamma], 1).astype(f)
    t = np.zeros((P, 1792), f)
    at = 0
    for dil, w in ((1, 256), (4, 512), (16, 512)):
        d = i - (np.arange(w)[None] - (w - P))
        t[:, at:at + w] = np.where((d >= 0) & (d % dil == 0) & (d <= dil * 128), -d, NEG)
        at += w
    t[:, 1280:1792] = np.arange(S)[None] >= i
    return c, decay.reshape(P, 2048), t


def tiles_t(w):
    k, c = w.shape
    t = w.reshape(k // P, P, c // P, P).transpose(2, 1, 0, 3).reshape(c // P, P, k)
    return np.pad(t, ((0, 0), (0, 0), (0, TILE - k))) if k < TILE else t


def tiles_n(w):
    g = w.shape[1] // S
    return w.reshape(4, 2, P, g, S).transpose(3, 0, 2, 1, 4).reshape(4 * g, P, TILE)


def pairs_of(a, b):
    return np.stack([a, b], 1).reshape(-1, *a.shape[1:])


def columns(v):
    return np.ascontiguousarray(v.reshape(-1, P).T)


def kernel(**inputs):
    import concourse.bacc as bacc
    from concourse.bass_utils import run_bass_kernel_spmd

    a = {k: np.asarray(v) for k, v in inputs.items()}
    parts = []
    for l in range(LAYERS):
        w = a["w_in"][l]
        q, k, v, g, u, vs, p, gates = np.split(w, np.cumsum([512, 512, 1024, 1024, 1024, 1024, 1024]), axis=1)
        gate = [tiles_t(gates[:, D * n:D * (n + 1)]) for n in range(3)]
        br = [tiles_t(a["w_branch"][l, n]) for n in range(3)]
        wp = a["w_pool"][l].reshape(4, 2, P, 256).transpose(0, 2, 1, 3).reshape(4, P, 512)
        parts += [tiles_t(a["w_ada"][l]), tiles_t(q), tiles_t(k), tiles_n(v), tiles_t(g), pairs_of(gate[0], br[0]),
                  tiles_t(u), tiles_n(vs), pairs_of(gate[1], br[1]), tiles_t(p),
                  np.pad(wp, ((0, 0), (0, 0), (0, TILE - 512))), pairs_of(gate[2], br[2]), tiles_t(a["w_out"][l])]
        for n in range(4):
            parts += [tiles_t(a["w_ff1"][l][:, D * n:D * (n + 1)]), tiles_t(a["w_ff2"][l][D * n:D * (n + 1)])]

    def conv_ffn(l):
        up, down, at = tiles_t(a["ffn_w_up_2"][l]), a["ffn_w_down_2"][l], 0
        for n in SLABS:
            yield pairs_of(up[at:at + n], up[at + UP // 2:at + UP // 2 + n])
            yield tiles_t(down[at * P:(at + n) * P])
            at += n

    w = a["a_w_in_2"][0]
    parts += [tiles_t(w[:, 0:2048]), tiles_n(w[:, 2048:3072]), tiles_t(a["a_w_out_2"][0]), *conv_ffn(0)]
    wkv = a["w_kv_2"]
    wo = tiles_t(a["b_w_out_2"][0])[:, :, 0:512].reshape(4, 2, P, 512).transpose(0, 2, 1, 3).reshape(4, P, TILE)
    parts += [tiles_t(a["b_w_q_2"][0]), tiles_t(wkv[:, 0:1536]), tiles_n(wkv[:, 1536:3072]), wo, *conv_ffn(1)]
    stream = np.concatenate(parts)
    assert stream.shape == (TILES, P, TILE), stream.shape

    c, decay, tables = constants()
    vec1 = np.stack([np.concatenate([columns(a[n][l]) for n in (
        "norm1", "norm2", "b_ada", "vnorm_gmlp", "b_pool", "pool_scale")], 1) for l in range(LAYERS)])
    bf = np.ascontiguousarray(np.broadcast_to(a["a_b_f_2"][0][None], (P, 16)))
    cw, final = a["ffn_conv_w_2"], columns(a["final_norm"])
    vec2 = np.concatenate([columns(a["kv_norm_g_2"]), columns(a["mix_norm_g_2"]), columns(a["ffn_norm_g_2"]),
                           columns(a["final_norm_g_2"]), final, columns(cw), columns(a["ffn_conv_b_2"]), bf], 1)
    data = {
        "stream": stream,
        "xT": np.ascontiguousarray(a["x"][0].T.reshape(KT, P, S).transpose(1, 0, 2)),
        "cvec": columns(a["c"][0]),
        "pos": np.ascontiguousarray(np.broadcast_to(a["positions"], (P, S))),
        "consts": c, "decay": decay, "tables": tables, "vec1": vec1,
        "ws": np.ascontiguousarray(a["ws_gmlp"].transpose(0, 3, 1, 2).reshape(LAYERS, P, 512)),
        "bs": a["bs_gmlp"].reshape(LAYERS, 512),
        "vec2": vec2,
        "wf": np.ascontiguousarray(w[:, 3072:].reshape(KT, P, 16).transpose(1, 0, 2).reshape(P, 128)),
    }
    nc = bacc.Bacc("TRN2", target_bir_lowering=False, num_devices=1)
    args = [nc.dram_tensor(n, v.shape, mybir.dt.from_np(v.dtype), kind="ExternalInput").ap() for n, v in data.items()]
    out = nc.dram_tensor("outT", (P, KT, S), F32, kind="ExternalOutput").ap()
    build(nc, *args, out)
    r = run_bass_kernel_spmd(nc, [data], core_ids=[0])
    return np.ascontiguousarray(r.results[0]["outT"].transpose(1, 0, 2).reshape(D, S).T)[None]
```

```python
from contextlib import ExitStack, contextmanager

import numpy as np

import concourse.bass as bass
from concourse import mybir

F32 = mybir.dt.float32
F32R = mybir.dt.float32r
I32 = mybir.dt.int32
ACT = mybir.ActivationFunctionType
ALU = mybir.AluOpType
AX = mybir.AxisListType

P = 128
S = 512
D = 1024
KT = D // P
TT = S // P
LAYERS = 2
R_HEADS, R_V = 4, 256
A_HEADS = 16
B_GROUPS = ((1, 128), (4, 512), (16, 512))
FF2 = 2816
SLABS = (8, 8, 6)
EPS = 1e-6
NEG = -1e30
RING = 4
AHEAD = RING - 1
TILE = KT * P

N_ADA = 6 * D // P
LAYER_TILES = N_ADA + 8 * 8 + 3 * 16 + 4 + 8 * 7
LAYER_BANKS = LAYER_TILES - N_ADA + 4
FFN2_TILES = 2 * sum(SLABS) + 8 * len(SLABS)
TILES = LAYERS * LAYER_TILES + (16 + 8 + 8 + FFN2_TILES) + (12 + 12 + 12 + 4 + FFN2_TILES)

C_ID, C_PERM, C_ONES, C_CAUSAL, C_EDGE = 0, P, 2 * P, 3 * P, 4 * P
C_FREQ = C_EDGE + 4 * 16
C_SIGN, C_EPS, C_HALFPI = C_FREQ + 1, C_FREQ + 2, C_FREQ + 3
C_SLOPE = C_FREQ + 4
C_ALL = C_SLOPE + 24
V_N1, V_N2, V_ADA, V_GAIN, V_BP, V_PS, V_ALL = 0, 8, 16, 64, 72, 80, 88
W_KV, W_MIX, W_FFN, W_FIN, W_FIN1, W_CW, W_CB, W_BF, W_ALL = 0, 8, 24, 40, 48, 56, 56 + 264, 56 + 352, 56 + 368
UP = 2 * FF2 // P


class Count:

    def __init__(self, start=0):
        self.n, self.off = start, None

    def value(self, back=0):
        return self.n - back if self.off is None else self.off + (self.n - back)

    def next(self, k=1):
        self.n += k
        return self.value()


def at(i):
    return slice(i, i + 1) if isinstance(i, int) else bass.ds(i, 1)


@contextmanager
def repeat(eng, trips, steps):
    saved = [(c, c.n, c.off, k) for c, k in steps.items()]
    with eng.Fori(0, trips) as i:
        for c, _, off, k in saved:
            c.off = i * k if off is None else off + i * k
        yield i
        for c, n, _, k in saved:
            assert c.n == n + k, f"a pass adds {c.n - n}, not {k}: {[x.n - m for x, m, _, _ in saved]}"
    for c, n, off, k in saved:
        c.n, c.off = n + k * trips, off


def build(nc, stream, xT, cvec, pos, consts, decay, tables, vec1, ws, bs, vec2, wf, outT):
    with ExitStack() as ctx:
        def sb(name, shape, dt=F32):
            return ctx.enter_context(nc.sbuf_tensor(name, shape, dt))

        def sem(name):
            return ctx.enter_context(nc.semaphore(name))

        raw = sb("raw", [P, RING, TILE])
        hi = sb("hi", [P, RING, TILE], F32R)
        lo = sb("lo", [P, RING, TILE], F32R)
        x = sb("x", [P, KT, S])
        with nc.sbuf_tensor("hH", [P, KT, S], F32R) as hH, nc.sbuf_tensor("hL", [P, KT, S], F32R) as hL:
            pass
        hF = sb("hF", [P, 2 * KT * S])
        with nc.sbuf_tensor("yH", [P, KT, S], F32R) as yH, nc.sbuf_tensor("yL", [P, KT, S], F32R) as yL:
            pass
        yF = sb("yF", [P, 2 * KT * S])
        act3 = sb("act3", [P, 3 * KT, S])
        A, B, M = act3[:, 0:KT], act3[:, KT:2 * KT], act3[:, 2 * KT:3 * KT]
        st = sb("st", [P, 4, S])
        tab = sb("tab", [P, 3072])
        scr = sb("scr", [P, 1280])
        cst = sb("cst", [P, C_ALL])
        v1 = sb("v1", [P, V_ALL])
        v2 = sb("v2", [P, S])
        mod = sb("mod", [P, N_ADA])
        geff = sb("geff", [P, 8])
        bpps = sb("bpps", [P, 8])
        cs = sb("cs", [P, 3, 8])
        cHL = sb("cHL", [P, 2 * KT + P], F32R)
        stat = sb("stat", [P, 16])
        pb = ctx.enter_context(nc.psum_tensor("pb", [P, 8, S], F32))

        dec = tab[:, 0:2048].rearrange("p (h s) -> p h s", h=R_HEADS)
        cosT, sinT = tab[:, 2048:2560], tab[:, 2560:3072]
        dist, pTb, tri = tab[:, 0:1280], tab[:, 1280:2560], tab[:, 2560:3072]
        wsT = scr[:, 0:512].rearrange("p (g t) -> p g t", g=4)
        bsb = scr[:, 512:1024].rearrange("p (g t) -> p g t", g=4)
        ident, perm = cst[:, C_ID:C_ID + P], cst[:, C_PERM:C_PERM + P]
        ones, causal = cst[:, C_ONES:C_ONES + P], cst[:, C_CAUSAL:C_CAUSAL + P]
        edge = cst[:, C_EDGE:C_EDGE + 64].rearrange("p (g t) -> p g t", g=4)
        epsc = cst[:, C_EPS:C_EPS + 1]
        Mf = act3[:, 2 * KT:3 * KT].rearrange("p k s -> p (k s)")
        Qr, Kr = Mf[:, 0:512], Mf[:, 512:1024]
        Vr = Mf[:, 1024:2048].rearrange("p (j e) -> p j e", j=TT)
        sT = Mf[:, 2048:3328]
        rT = Mf[:, 3328:3840]
        sT_at = [0, 512, 896, 1152]
        Qa, Ka = hF[:, 0:512], hF[:, 512:1024]
        Va = hF[:, 1024:1536].rearrange("p (j e) -> p j e", j=TT)
        Pa = [hF[:, 1536:2048], hF[:, 2048:2560]]
        pTa = [hF[:, 2560:3072], hF[:, 3072:3584]]
        cT = hF[:, 3584:4096]
        sel = hF[:, 4096:4352].rearrange("p (a b) -> p a b", a=2)
        wfraw = yF[:, 0:128]
        lf = yF[:, 128:512].rearrange("p (a b) -> p a b", a=6)
        Vall = hF[:, 0:6144].rearrange("p (g j e) -> p g j e", g=3, j=TT)
        Qb = yF[:, 2048:3584].rearrange("p (g s) -> p g s", g=3)
        Kb = yF[:, 6144:7680].rearrange("p (g s) -> p g s", g=3)
        Vb = st[:, 0:3].rearrange("p g (j e) -> p g j e", j=TT)
        Pb = [scr[:, 0:1280], hF[:, 6144:7424]]
        modrow = v2[0:2, 0:S]
        wfH = sb("wfH", [P, KT, 16], F32R)
        wfL = sb("wfL", [P, KT, 16], F32R)

        landed = [sem(f"landed{s}") for s in range(RING)]
        hi_ready = sem("hi_ready")
        lo_ready = sem("lo_ready")
        tile_done = sem("tile_done")
        bank_free = sem("bank_free")
        st_free = sem("st_free")
        setup_in = sem("setup_in")
        pos_in = sem("pos_in")
        vec_seen = sem("vec_seen")
        vec_in = sem("vec_in")
        tab_in = sem("tab_in")
        ws_ready = sem("ws_ready")
        layer_done = sem("layer_done")
        c_act = sem("c_act")
        c_ready = sem("c_ready")
        trig_arg = sem("trig_arg")
        trig = sem("trig")
        osq_ready = sem("osq_ready")
        squared = sem("squared")
        sq_sum = sem("sq_sum")
        rs_ready = sem("rs_ready")
        rs_full = sem("rs_full")
        row_ready = sem("row_ready")
        mod_full = sem("mod_full")
        mod_read = sem("mod_read")
        summed = sem("summed")
        rooted = sem("rooted")
        h_ready = sem("h_ready")
        y_ready = sem("y_ready")
        rope_full = sem("rope_full")
        rope_ready = sem("rope_ready")
        vr_ready = sem("vr_ready")
        score_full = sem("score_full")
        score_ready = sem("score_ready")
        o_full = sem("o_full")
        o_normed = sem("o_normed")
        v_mean = sem("v_mean")
        x_ready = sem("x_ready")
        v_normed = sem("v_normed")
        mix_full = sem("mix_full")
        mix_free = sem("mix_free")
        f_full = sem("f_full")
        z_ready = sem("z_ready")
        e_ready = sem("e_ready")
        c_full = sem("c_full")
        c_out = sem("c_out")
        wf_ready = sem("wf_ready")
        staged = sem("staged")
        sel_ready = sem("sel_ready")
        s_full = sem("s_full")
        max_ready = sem("max_ready")
        p_ready = sem("p_ready")
        p_normed = sem("p_normed")
        t_full = sem("t_full")
        t_ready = sem("t_ready")
        pv_done = sem("pv_done")
        conv_done = sem("conv_done")
        gated = sem("gated")
        out_ready = sem("out_ready")
        out_done = sem("out_done")

        block = ctx.enter_context(nc.Block())

        B_IT = [[(g, j) for g in range(3) for j in range(TT) if j <= it and (g or j >= it - 1)] for it in range(TT)]
        A_IT = [[(0, j) for j in range(it + 1)] for it in range(TT)]

        @block.sync
        def _(sp):
            for dst, src in ((cst[:], consts), (x[:], xT), (cs[:, 0], cvec), (tab[:, 0:2048], decay)):
                sp.dma_start(dst, src).then_inc(setup_in, 16)
            freed = Count()
            with repeat(sp, TILES // RING, {freed: RING}) as i:
                for s in range(RING):
                    sp.wait_ge(lo_ready, freed.next())
                    sp.dma_start(raw[:, s], stream[bass.ds(i * RING + s, 1)].rearrange("a p c -> (a p) c")
                                 ).then_inc(landed[s], 16)
            for n in range(KT):
                sp.wait_ge(out_ready, n + 1)
                sp.dma_start(outT[:, n], act3[:, n]).then_inc(out_done, 16)
            sp.wait_ge(out_done, 16 * KT)

        @block.gpsimd
        def _(pool):
            pool.dma_start(st[:, 3].bitcast(I32), pos).then_inc(pos_in, 16)
            banks, heads, layers, vecs, sq = Count(4), Count(1), Count(), Count(), Count()

            def sum_squares():
                pool.wait_ge(squared, sq.next())
                for k in range(1, KT):
                    pool.wait_ge(squared, sq.next())
                    pool.tensor_tensor(A[:, 0], A[:, 0], A[:, k], ALU.add)
                    pool.drain()
                pool.sem_inc(sq_sum, 1)

            sum_squares()
            v_tok = act3[:, KT:2 * KT].rearrange("p (j a) s -> p j (a s)", j=TT)
            with repeat(pool, LAYERS, {banks: LAYER_BANKS, heads: 2 * R_HEADS, layers: 1, vecs: 48,
                                       sq: 16}) as l:
                pool.wait_ge(layer_done, layers.next())
                pool.dma_start(v1[:], vec1[bass.ds(l, 1)].rearrange("a p c -> (a p) c")).then_inc(vec_in, 16)
                pool.dma_start(scr[:, 0:512], ws[bass.ds(l, 1)].rearrange("a p c -> (a p) c")).then_inc(vec_in, 16)
                pool.dma_start(scr[:, 512:1024], bs[bass.ds(l, 1)].to_broadcast([P, 512])).then_inc(vec_in, 16)
                pool.wait_ge(vec_in, vecs.next(48))
                pool.sem_inc(vec_seen, 1)
                pool.affine_select(out=wsT, in_=wsT, pattern=[[0, 4], [1, P]], compare_op=ALU.is_ge, fill=0.0,
                                   base=0, channel_multiplier=-1).then_inc(ws_ready, 1)
                banks.next(16)
                with repeat(pool, R_HEADS, {heads: 2}) as h:
                    pool.wait_ge(bank_free, banks.value())
                    pool.wait_ge(o_full, heads.value())
                    heads.next(2)
                    pool.tensor_copy(Vr, v_tok[:, :, bass.ds(h * R_V, R_V)]).then_inc(vr_ready, 1)
                sum_squares()
                sum_squares()
                banks.next(LAYER_BANKS - 16)
            pool.wait_ge(layer_done, 1 + LAYERS)
            pool.dma_start(tab[:, 0:1280], tables[:, 0:1280]).then_inc(tab_in, 16)
            pool.dma_start(tri, tables[:, 1280:1792]).then_inc(tab_in, 16)
            pool.dma_start(wfraw, wf).then_inc(tab_in, 16)
            pool.dma_start(v2[:, 0:W_ALL], vec2).then_inc(tab_in, 16)
            steps = Count(1)
            sum_squares()
            pool.wait_ge(bank_free, banks.next(24))
            v_tok = act3[:, 16:24].rearrange("p (j a) s -> p j (a s)", j=TT)
            with repeat(pool, A_HEADS // 2, {steps: 8}) as p:
                pool.wait_ge(pv_done, steps.value())
                steps.next(8)
                pool.tensor_copy(Qa, act3[:, bass.ds(p, 1), :].rearrange("p a s -> p (a s)"))
                pool.tensor_copy(Ka, act3[:, bass.ds(p + 8, 1), :].rearrange("p a s -> p (a s)"))
                pool.tensor_copy(Va, v_tok[:, :, bass.ds(p * P, P)])
                pool.drain().then_inc(staged, 1)
            sum_squares()
            sum_squares()
            pool.wait_ge(bank_free, banks.next(8 + FFN2_TILES + 36))
            q12 = act3[:, 0:12].rearrange("p (g n) s -> p g n s", g=3)
            k12 = act3[:, 12:24].rearrange("p (g n) s -> p g n s", g=3)
            with repeat(pool, 4, {steps: 8}) as p:
                pool.wait_ge(pv_done, steps.value())
                steps.next(8)
                for g in range(3):
                    pool.tensor_copy(Qb[:, g:g + 1], q12[:, g, bass.ds(p, 1), :])
                    pool.tensor_copy(Kb[:, g:g + 1], k12[:, g, bass.ds(p, 1), :])
                    pool.tensor_copy(Vb[:, g], Vall[:, g, :, bass.ds(p * P, P)])
                pool.drain().then_inc(staged, 1)
            sum_squares()
            sum_squares()

        @block.tensor
        def _(pe):
            tiles, banks = Count(4), Count()
            h_k, y_k = Count(), Count()
            sq, rope, vr, sc, vn, mix = (Count() for _ in range(6))
            on, ss, rs, rw, mr = Count(1), Count(), Count(), Count(), Count()
            pe.sem_inc(tile_done, 4)
            for one_ahead in (o_full, pv_done, t_full):
                pe.sem_inc(one_ahead, 1)

            def three(out, whi, wlo, ahi, alo, first, last):
                pe.matmul(out, whi, ahi, start=first, stop=False)
                pe.matmul(out, whi, alo, start=False, stop=False)
                return pe.matmul(out, wlo, ahi, start=False, stop=last)

            def tile_T(s, aH, aL, ks=KT, ready=None):
                pe.wait_ge(lo_ready, tiles.next())
                pe.wait_ge(bank_free, banks.next())
                for k in range(ks):
                    if ready is not None:
                        pe.wait_ge(ready[0], ready[1] + k + 1)
                    w = slice(k * P, (k + 1) * P)
                    ins = three(pb[:, s], hi[:, s, w], lo[:, s, w], aH[:, k], aL[:, k], k == 0, k == ks - 1)
                ins.then_inc(tile_done, 1)

            def first_T(aH, aL, ready, ks=KT):
                pe.wait_ge(lo_ready, tiles.next(3))
                pe.wait_ge(bank_free, banks.next(3))
                for k in range(ks):
                    pe.wait_ge(ready[0], ready[1] + k + 1)
                    w = slice(k * P, (k + 1) * P)
                    for s in range(3):
                        ins = three(pb[:, s], hi[:, s, w], lo[:, s, w], aH[:, k], aL[:, k], k == 0, k == ks - 1)
                        if k == ks - 1:
                            ins.then_inc(tile_done, 1)
                tile_T(3, aH, aL, ks)

            def tiles_T(n, aH, aL, ready, ks=KT, peel=False, ada=False):
                if peel:
                    first_T(aH, aL, ready, ks)
                    n -= RING
                    ready = None
                with repeat(pe, n // RING, {tiles: RING + 4 * ada, banks: RING, **({rw: 1, mr: 1} if ada else {})}):
                    for s in range(RING):
                        tile_T(s, aH, aL, ks, ready if s == 0 else None)
                    if ada:
                        ada_group()

            def ada_group():
                for s in range(RING):
                    pe.wait_ge(lo_ready, tiles.next())
                    for kk in range(2):
                        k = 2 * s + kk
                        w = slice(kk * S, (kk + 1) * S)
                        c = cHL[:, 2 * k:2 * k + P]
                        pe.matmul(pb[:, 6], c, hi[:, s, w], start=k == 0, stop=False)
                        ins = pe.matmul(pb[:, 6], c, lo[:, s, w], start=False, stop=k == KT - 1)
                    ins.then_inc(tile_done, 1)
                pe.wait_ge(row_ready, rw.next())
                pe.wait_ge(mod_read, mr.next())
                for j in range(4):
                    ins = pe.matmul(pb[:, 7, j:j + 1], modrow[:, j * P:(j + 1) * P], ones[0:2, 0:1],
                                    start=True, stop=True)
                ins.then_inc(mod_full, 1)

            def tiles_N(groups, aH, aL, ada=False):
                with repeat(pe, groups, {tiles: RING + 4 * ada, banks: RING, **({rw: 1, mr: 1} if ada else {})}):
                    pe.wait_ge(bank_free, banks.next(4))
                    for s in range(RING):
                        pe.wait_ge(lo_ready, tiles.next())
                        for t in range(TT):
                            for kk in range(2):
                                k = 2 * s + kk
                                w, a = slice(kk * S, (kk + 1) * S), slice(t * P, (t + 1) * P)
                                pe.matmul(pb[:, t], aH[:, k, a], hi[:, s, w], start=k == 0, stop=False)
                                pe.matmul(pb[:, t], aL[:, k, a], hi[:, s, w], start=False, stop=False)
                                ins = pe.matmul(pb[:, t], aH[:, k, a], lo[:, s, w], start=False, stop=k == KT - 1)
                        ins.then_inc(tile_done, 1)
                    if ada:
                        ada_group()

            def norm_sum():
                pe.wait_ge(sq_sum, ss.next())
                for t in range(TT):
                    ins = pe.matmul(pb[:, 4, t:t + 1], A[:, 0, t * P:(t + 1) * P], ones[:, 0:1], start=True, stop=True)
                ins.then_inc(summed, 1)
                spread()

            def spread():
                pe.wait_ge(rs_ready, rs.next())
                for t in range(TT):
                    ins = pe.matmul(pb[:, 5, t * P:(t + 1) * P], stat[:, 8 + t:9 + t].to_broadcast([P, P]), ident,
                                    start=True, stop=True)
                ins.then_inc(rs_full, 1)

            def gated_pairs():
                with repeat(pe, 4, {tiles: RING, banks: RING}):
                    for s in range(RING):
                        if s % 2:
                            tile_T(s, yH, yL, KT, (y_ready, y_k.value()) if s == 1 else None)
                        else:
                            tile_T(s, hH, hL)

            with repeat(pe, LAYERS, {tiles: LAYER_TILES, banks: LAYER_BANKS, h_k: 16, y_k: 72, sq: 8,
                                     rope: 8, vr: 4, sc: 16, on: 8, vn: 4, mix: 8, ss: 2, rs: 2, rw: 12, mr: 12}) as l:
                norm_sum()
                pe.wait_ge(c_ready, 1)
                with repeat(pe, 4, {tiles: RING, rw: 1, mr: 1}):
                    ada_group()
                h0 = h_k.value()
                h_k.next(8)
                tiles_T(8, hH, hL, (h_ready, h0), peel=True)
                tiles_N(2, hH, hL)
                with repeat(pe, R_HEADS, {rope: 2, vr: 1, sc: 4, on: 2, sq: 2}) as h:
                    pe.wait_ge(bank_free, banks.value(-4))
                    pe.wait_ge(o_normed, on.value())
                    for j in range(2):
                        pe.matmul(pb[:, 4 + j:5 + j], perm, act3[:, bass.ds(h + 4 * j, 1), :],
                                  start=True, stop=True).then_inc(rope_full, 1)
                    pe.wait_ge(rope_ready, rope.next(2))
                    for j in range(TT):
                        if j >= 2:
                            pe.wait_ge(score_ready, sc.value() + j - 1)
                        pe.matmul(pb[:, 6 + j % 2, 0:S - j * P], Kr[:, j * P:(j + 1) * P], Qr[:, j * P:S],
                                  start=True, stop=True).then_inc(score_full, 1)
                    pe.wait_ge(vr_ready, vr.next())
                    for e in range(2):
                        for j in range(TT):
                            if e == 0:
                                pe.wait_ge(score_ready, sc.next())
                            ins = pe.matmul(pb[:, 4 + e, j * P:S], Vr[:, j, e * P:(e + 1) * P],
                                            sT[:, sT_at[j]:sT_at[j] + S - j * P], start=j == 0, stop=j == TT - 1)
                        ins.then_inc(o_full, 1)
                    for e in range(2):
                        pe.wait_ge(osq_ready, sq.next())
                        ins = pe.matmul(pb[:, 6], ones, Mf[:, e * S:(e + 1) * S], start=e == 0, stop=e == 1)
                    ins.then_inc(summed, 1)
                    on.next(2)
                tiles_T(8, hH, hL, None, ada=True)
                gated_pairs()
                y_k.next(8)
                tiles_T(8, hH, hL, None, ada=True)
                tiles_N(2, hH, hL, ada=True)
                pe.wait_ge(ws_ready, l + 1)
                pe.wait_ge(v_normed, vn.next(4))
                for n in range(KT):
                    pe.wait_ge(mix_free, mix.next())
                    for t in range(TT):
                        ins = pe.matmul(pb[:, 4 + n % 2, t * P:(t + 1) * P],
                                        B[:, 2 * t + n // 4, (n % 4) * P:(n % 4 + 1) * P], wsT[:, n // 2],
                                        start=True, stop=True)
                    ins.then_inc(mix_full, 1)
                gated_pairs()
                y_k.next(8)
                tiles_T(8, hH, hL, None, ada=True)
                for g in range(4):
                    pe.wait_ge(lo_ready, tiles.next())
                    pe.wait_ge(bank_free, banks.next(2))
                    pe.wait_ge(y_ready, y_k.next(2))
                    for e in range(2):
                        for k in range(2):
                            w = slice(k * 256 + e * P, k * 256 + (e + 1) * P)
                            ins = three(pb[:, (2 * g + e) % 4], hi[:, g, w], lo[:, g, w], yH[:, 2 * g + k],
                                        yL[:, 2 * g + k], k == 0, k == 1)
                    ins.then_inc(tile_done, 1)
                gated_pairs()
                y_k.next(8)
                y0 = y_k.value()
                y_k.next(8)
                tiles_T(8, yH, yL, (y_ready, y0), peel=True)
                norm_sum()
                h0 = h_k.value()
                h_k.next(8)
                tiles_T(8, hH, hL, (h_ready, h0), peel=True)
                with repeat(pe, 3, {tiles: 16, banks: 16, y_k: 8}):
                    tiles_T(8, yH, yL, (y_ready, y_k.value()))
                    y_k.next(8)
                    tiles_T(8, hH, hL, None)
                tiles_T(8, yH, yL, (y_ready, y_k.value()))
                y_k.next(8)

            st_, mx, pn, tr, ofr, el = Count(), Count(), Count(1), Count(1), Count(), Count()

            def attention(pairs, its, scores, value, tbank, groups_T, obank):
                with repeat(pe, pairs, {st_: 1, mx: 8, pn: 8, tr: 8, ofr: 1, el: 2}) as p:
                    pe.wait_ge(staged, st_.next())
                    for n in range(10):
                        if n < 8:
                            hp, it = n // 4, n % 4
                            scores(n, hp, it)
                        if 1 <= n <= 8:
                            m, it = n - 1, (n - 1) % 4
                            pe.wait_ge(p_normed, pn.value() + m + 1)
                            nb = len(its[it])
                            for b in range(nb):
                                ins = pe.transpose(pb[:, tbank(m, b), (b % 4) * P:(b % 4 + 1) * P],
                                                   groups_T(m)[:, b * P:(b + 1) * P], ident)
                            ins.then_inc(t_full, 1)
                        if n >= 2:
                            m, hp, it = n - 2, (n - 2) // 4, (n - 2) % 4
                            if m == 0:
                                pe.wait_ge(y_ready, y_base[0] + ofr.value())
                            pe.wait_ge(t_ready, tr.value() + m + 1)
                            blocks = its[it]
                            for b, (g, j) in enumerate(blocks):
                                rhs, lhsT = value(m, b, g, j, hp)
                                ins = pe.matmul(pb[hp * 64:(hp + 1) * 64, obank, it * P:(it + 1) * P], lhsT, rhs,
                                                start=b == 0, stop=b == len(blocks) - 1)
                            ins.then_inc(pv_done, 1)
                    mx.next(8), pn.next(8), tr.next(8), ofr.next(1), el.next(2)

            def conv_ffn(last=False):
                norm_sum()
                h0 = h_k.value()
                h_k.next(8)
                for j, n in enumerate(SLABS):
                    tiles_T(2 * n, hH, hL, (h_ready, h0), peel=j == 0)
                    tiles_T(8, yH, yL, (y_ready, y_k.value()), ks=n)
                    y_k.next(n)

            norm_sum()
            norm_sum()
            h0 = h_k.value()
            h_k.next(8)
            pe.wait_ge(wf_ready, 1)
            for t in range(TT):
                for k in range(KT):
                    pe.wait_ge(h_ready, h0 + k + 1)
                    a = slice(t * P, (t + 1) * P)
                    out = pb[:, 4, t * 16:(t + 1) * 16]
                    pe.matmul(out, hH[:, k, a], wfH[:, k], start=k == 0, stop=False)
                    pe.matmul(out, hL[:, k, a], wfH[:, k], start=False, stop=False)
                    ins = pe.matmul(out, hH[:, k, a], wfL[:, k], start=False, stop=k == KT - 1)
            ins.then_inc(f_full, 1)
            tiles_T(16, hH, hL, None)
            pe.wait_ge(z_ready, 2)
            for t in range(TT):
                ins = pe.matmul(pb[0:16, 5, t * P:S], lf[:, 5, t * 16:(t + 1) * 16], tri[:, 0:S - t * P],
                                start=t == 0, stop=t == TT - 1)
            ins.then_inc(c_full, 1)
            tiles_N(2, hH, hL)
            pe.wait_ge(c_out, 1)

            def scores_a(n, hp, it):
                w = (it + 1) * P
                if n >= 2:
                    pe.wait_ge(p_ready, pn.value() + n - 1)
                elif n == 0:
                    pe.wait_ge(p_ready, pn.value())
                if it == 0:
                    pe.wait_ge(sel_ready, el.value() + hp + 1)
                a = slice(hp * 64, (hp + 1) * 64)
                out = pb[:, n % 2]
                pe.matmul(out[:, 0:w], Qa[a, it * P:(it + 1) * P], Ka[a, 0:w], start=True, stop=False)
                pe.matmul(out[:, 0:w], sel[0:16, hp], cT[0:16, 0:w], start=False, stop=False)
                pe.matmul(out[:, it * P:w], ident, causal, start=False, stop=True).then_inc(s_full, 1)

            y_base = [y_k.value()]
            attention(A_HEADS // 2, A_IT, scores_a,
                      lambda m, b, g, j, hp: (pTa[m % 2][:, b * P:(b + 1) * P], Va[:, j, hp * 64:(hp + 1) * 64]),
                      lambda m, b: 2 + m % 2, lambda m: Pa[m % 2], 6)
            tiles_T(8, yH, yL, (y_ready, y_base[0]))
            y_k.next(8)
            conv_ffn()
            norm_sum()
            h0 = h_k.value()
            h_k.next(8)
            tiles_T(12, hH, hL, (h_ready, h0), peel=True)
            tiles_T(12, yH, yL, (y_ready, y_k.value()))
            y_k.next(8)
            tiles_N(3, yH, yL)
            y_base = [y_k.value()]
            ofr = Count()

            def scores_b(n, hp, it):
                if n == 0:
                    pe.wait_ge(t_ready, tr.value())
                elif n >= 2:
                    pe.wait_ge(t_ready, tr.value() + n - 1)
                a = slice(hp * 64, (hp + 1) * 64)
                for g in range(3):
                    first = max(0, it - 1) if g == 0 else 0
                    ins = pe.matmul(pb[:, 3 * (n % 2) + g, 0:(it + 1 - first) * P], Qb[a, g, it * P:(it + 1) * P],
                                    Kb[a, g, first * P:(it + 1) * P], start=True, stop=True)
                ins.then_inc(s_full, 1)

            attention(4, B_IT, scores_b,
                      lambda m, b, g, j, hp: (pTb[:, b * P:(b + 1) * P], Vb[:, g, j, hp * 64:(hp + 1) * 64]),
                      lambda m, b: 3 * (m % 2) + b // 4, lambda m: Pb[m % 2], 6)
            pe.wait_ge(y_ready, y_base[0] + 4)
            y_k.next(4)
            for s in range(RING):
                pe.wait_ge(lo_ready, tiles.next())
                pe.wait_ge(bank_free, banks.next(2))
                for e in range(2):
                    for k in range(4):
                        w = slice((4 * e + k) * P, (4 * e + k + 1) * P)
                        ins = three(pb[:, (2 * s + e) % 4], hi[:, s, w], lo[:, s, w], yH[:, k], yL[:, k], k == 0, k == 3)
                ins.then_inc(tile_done, 1)
            conv_ffn(last=True)
            norm_sum()
            assert tiles.n == TILES + 4, (tiles.n, TILES)

        @block.scalar
        def _(act):
            split, done, stf = Count(), Count(4), Count()
            land = [Count() for _ in range(RING)]
            ring = {split: RING, done: RING, **{c: 16 for c in land}}
            ada_ring = {split: 2 * RING, done: 2 * RING, **{c: 32 for c in land}}
            act.sem_inc(bank_free, 4)
            act.sem_inc(p_ready, 1)
            act.sem_inc(t_ready, 1)
            left = [TILES]

            def tick(s, static=None):
                s = (s + AHEAD) % RING
                if static is not None and static + AHEAD >= TILES:
                    return
                act.wait_ge(landed[s], land[s].next(16))
                act.wait_ge(tile_done, split.next())
                act.activation(hi[:, s], raw[:, s], ACT.Copy).then_inc(hi_ready, 1)

            def bodies(n, steps, body, last=False):
                if last:
                    for i in range(n):
                        body(i)
                else:
                    with repeat(act, n, {**ring, **steps}) as i:
                        body(i)

            def to_st(s, scale=1.0, bias=0.0, func=ACT.Identity, bank=None):
                act.wait_ge(st_free, stf.next())
                b = s if bank is None else bank
                act.activation(st[:, s:s + 1], pb[:, b:b + 1], func, bias=bias, scale=scale).then_inc(bank_free, 1)

            def tiles_T(n, drain, uses_st=True, last=False, peel=False, ada=False):
                def body(i, first=False):
                    for s in range(RING):
                        t = None if not last else TILES - RING * (n // RING - i) + s
                        if s or not first:
                            tick(s, t)
                        act.wait_ge(tile_done, done.next())
                        drain(i, s)
                    if ada:
                        ada_group()
                if peel:
                    body(0, True)
                    bodies(n // RING - 1, {stf: RING} if uses_st else {}, lambda i: body(i + 1))
                    return
                bodies(n // RING, {**({stf: RING} if uses_st else {}), **(dict(ada_ring) if ada else {})}, body, last)

            def ada_group():
                for s in range(RING):
                    tick(s)
                act.wait_ge(tile_done, done.next(4))
                act.activation(modrow, pb[0:2, 6], ACT.Copy).then_inc(row_ready, 1)

            def tiles_N(groups, drain, ada=False):
                def body(i):
                    for s in range(RING):
                        tick(s)
                    act.wait_ge(tile_done, done.next(4))
                    for t in range(TT):
                        drain(i, t)
                    if ada:
                        ada_group()
                bodies(groups, ada_ring if ada else {}, body)

            sums = Count()

            def square(k):
                act.activation(act3[:, at(k)], x[:, at(k)], ACT.Square).then_inc(squared, 1)

            def root(early=True):
                if early:
                    tick(0)
                act.wait_ge(summed, sums.next())
                act.activation(stat[:, 8:12], pb[:, 4, 0:4], ACT.Sqrt, bias=epsc, scale=1.0 / D).then_inc(rooted, 1)

            def to_x(n, drain, **how):
                def both(i, s):
                    drain(i, s)
                    for k in ([s - 1] if s else []) + ([3] if s == 3 else []):
                        act.wait_ge(st_free, stf.value(-4 + (s - k)))
                        square(i * RING + k)
                tiles_T(n, both, **how)

            for s in range(AHEAD):
                tick(s - AHEAD)
            act.wait_ge(setup_in, 64)
            act.activation(cs[:, 1], cs[:, 0], ACT.Silu).then_inc(c_act, 1)
            act.wait_ge(trig_arg, 1)
            act.activation(sinT, st[:, 1], ACT.Sin).then_inc(trig, 1)
            act.activation(st[:, 2], st[:, 1], ACT.Abs)
            act.drain()
            act.activation(cosT, st[:, 2], ACT.Sin, scale=-1.0, bias=cst[:, C_HALFPI:C_HALFPI + 1]).then_inc(trig, 1)

            def pairs():
                def drain(i, s):
                    to_st(s, func=ACT.Identity if s % 2 else ACT.Sigmoid)
                tiles_T(16, drain)

            for k in range(KT):
                square(k)
            vecs, of, means = Count(), Count(1), Count()
            with repeat(act, LAYERS, {split: LAYER_TILES, done: LAYER_TILES, stf: 8 + 48 + 8 + 8 + 64,
                                      sums: 6, means: 1, vecs: 1, of: 8, **{c: LAYER_TILES // RING * 16 for c in land}}) as l:
                act.wait_ge(vec_seen, vecs.next())
                root(early=False)
                with repeat(act, 4, ring):
                    ada_group()
                tick(0)

                def drain_to(first, func):
                    def drain(i, s):
                        act.activation(act3[:, at(i * RING + s + first), :], pb[:, s:s + 1], func
                                       ).then_inc(bank_free, 1)
                    return drain

                def drain_tok(first, func):
                    def drain(i, t):
                        act.activation(act3[:, bass.ds(i + first + 2 * t, 1), :], pb[:, t:t + 1], func
                                       ).then_inc(bank_free, 1)
                    return drain
                tiles_T(8, drain_to(0, ACT.Copy), uses_st=False, peel=True)
                tiles_N(2, drain_tok(8, ACT.Copy))
                with repeat(act, R_HEADS, {of: 2, sums: 1}):
                    for e in range(2):
                        act.wait_ge(o_full, of.next())
                        if e == 0:
                            act.wait_ge(o_full, of.value(-1))
                        act.activation(Mf[:, e * S:(e + 1) * S], pb[:, 4 + e], ACT.Square).then_inc(osq_ready, 1)
                    act.wait_ge(summed, sums.next())
                    act.activation(sT[:, 0:S], pb[:, 6], ACT.Sqrt, bias=epsc, scale=1.0 / R_V).then_inc(rooted, 1)
                tiles_T(8, lambda i, s: to_st(s, func=ACT.Silu), ada=True)
                pairs()
                tiles_T(8, drain_to(0, ACT.Gelu_apprx_tanh), uses_st=False, ada=True)
                tiles_N(2, drain_tok(8, ACT.Gelu_apprx_tanh), ada=True)
                act.wait_ge(v_mean, means.next())
                act.activation(stat[:, 8:12], stat[:, 12:16], ACT.Sqrt).then_inc(rooted, 1)
                pairs()
                tiles_T(8, drain_to(0, ACT.Copy), uses_st=False, ada=True)
                for g in range(4):
                    tick(g)
                    act.wait_ge(tile_done, done.next())
                    for e in range(2):
                        n = 2 * g + e
                        to_st(n % 4, scale=v1[:, V_PS + n:V_PS + n + 1], bias=bpps[:, n:n + 1])
                pairs()
                def gate_by(first):
                    def drain(i, s):
                        m = i * RING + s + first
                        to_st(s, scale=mod[:, at(m)])
                    return drain
                tick(0)
                to_x(8, gate_by(16), peel=True)
                root()
                tiles_T(8, lambda i, s: to_st(s), peel=True)
                with repeat(act, 3, {split: 16, done: 16, stf: 16, **{c: 64 for c in land}}):
                    tiles_T(8, gate_by(40))
                    tiles_T(8, lambda i, s: to_st(s))
                to_x(8, gate_by(40))

            cv = Count()

            def conv_ffn(last=False):
                root()
                for j, n in enumerate(SLABS):
                    def body(i, first=False):
                        for s in range(RING):
                            if s or not first:
                                tick(s)
                            act.wait_ge(tile_done, done.next())
                            to_st(s)
                            if s % 2:
                                act.wait_ge(conv_done, cv.next())
                                act.activation(A[:, s], A[:, s], ACT.Silu).then_inc(gated, 1)
                    if j == 0:
                        body(0, True)
                    bodies(n // 2 - (j == 0), {stf: RING, cv: 2}, body)
                    if j == len(SLABS) - 1:
                        to_x(8, lambda i, s: to_st(s), last=last)
                    else:
                        tiles_T(8, lambda i, s: to_st(s))

            root(early=False)
            for k in range(KT):
                act.wait_ge(x_ready, k + 1)
                square(k)
            root(early=False)

            def drain_q(scale, first):
                def drain(i, s):
                    act.activation(act3[:, at(i * RING + s + first), :], pb[:, s:s + 1], ACT.Copy,
                                   scale=scale).then_inc(bank_free, 1)
                return drain
            act.wait_ge(z_ready, 1)
            act.activation(lf[:, 1], lf[:, 0], ACT.Abs)
            act.drain()
            act.activation(lf[:, 2], lf[:, 1], ACT.Exp, scale=-1.0)
            act.drain()
            act.activation(lf[:, 3], lf[:, 2], ACT.Ln, bias=1.0).then_inc(e_ready, 1)
            tiles_T(8, drain_q(0.125, 0), uses_st=False)
            tiles_T(8, drain_q(1.0, 8), uses_st=False)

            def drain_v(i, t):
                act.activation(act3[:, bass.ds(i + 16 + 2 * t, 1), :], pb[:, t:t + 1], ACT.Copy).then_inc(bank_free, 1)
            tiles_N(2, drain_v)
            mx, tf, pvc = Count(), Count(1), Count(1)

            def attention(pairs_, its, exp_in, exp_out, copies):
                with repeat(act, pairs_, {mx: 8, tf: 8, pvc: 8}):
                    for n in range(9):
                        if n < 8:
                            it = n % 4
                            act.wait_ge(max_ready, mx.next())
                            w = len(its[it]) * P
                            act.activation(exp_out(n)[:, 0:w], exp_in(n, w), ACT.Exp, bias=stat[:, n % 2:n % 2 + 1],
                                           accum_out=stat[:, 2 + n % 2:3 + n % 2])
                            act.drain().then_inc(p_ready, 1)
                        if n >= 1:
                            m = n - 1
                            act.wait_ge(t_full, tf.next())
                            copies(m, len(its[m % 4]), pvc)
                    pvc.next(8)

            def copies_a(m, nb, pvc):
                act.wait_ge(pv_done, pvc.value() + max(0, m - 1))
                act.activation(pTa[m % 2][:, 0:nb * P], pb[:, 2 + m % 2, 0:nb * P], ACT.Copy).then_inc(t_ready, 1)

            attention(A_HEADS // 2, A_IT, lambda n, w: pb[:, n % 2, 0:w], lambda n: Pa[n % 2], copies_a)
            to_x(8, lambda i, s: to_st(s))
            conv_ffn()
            root()
            tiles_T(12, drain_q(0.125, 0), uses_st=False, peel=True)
            tiles_T(12, drain_q(1.0, 12), uses_st=False)

            def drain_vb(i, t):
                act.activation(Vall[:, bass.ds(i, 1), t], pb[:, t:t + 1], ACT.Copy).then_inc(bank_free, 1)
            tiles_N(3, drain_vb)

            def copies_b(m, nb, pvc):
                act.wait_ge(pv_done, pvc.value() + m)
                for b in range(0, nb, 4):
                    w = min(4, nb - b) * P
                    act.activation(pTb[:, b * P:b * P + w], pb[:, 3 * (m % 2) + b // 4, 0:w], ACT.Copy)
                act.drain().then_inc(t_ready, 1)

            attention(4, B_IT, lambda n, w: Pb[n % 2][:, 0:w], lambda n: Pb[n % 2], copies_b)
            for s in range(RING):
                tick(s)
                act.wait_ge(tile_done, done.next())
                for e in range(2):
                    n = 2 * s + e
                    to_st(n % 4)
                    if n:
                        act.wait_ge(st_free, stf.value(-3))
                        square(n - 1)
            act.wait_ge(st_free, stf.value(-4))
            square(7)
            conv_ffn(last=True)
            root(early=False)

        @block.vector
        def _(dve):
            split, drained = Count(), Count(4)
            ring = {split: RING, drained: RING}
            dve.sem_inc(lo_ready, 4)
            dve.sem_inc(st_free, 4)
            dve.sem_inc(o_normed, 1)
            dve.sem_inc(p_normed, 1)

            def tick(s, static=None):
                s = (s + AHEAD) % RING
                if static is not None and static + AHEAD >= TILES:
                    return
                dve.wait_ge(hi_ready, split.next())
                dve.tensor_tensor(lo[:, s], raw[:, s], hi[:, s].bitcast(F32), ALU.subtract).then_inc(lo_ready, 1)

            mf, rf = Count(), Count()

            def bodies(n, body, last=False, steps=None):
                if last:
                    for i in range(n):
                        body(i)
                else:
                    with repeat(dve, n, steps or ring) as i:
                        body(i)

            def tiles_T(n, work, last=False, peel=False, ada=None):
                def body(i, first=False):
                    for s in range(RING):
                        t = None if not last else TILES - RING * (n // RING - i) + s
                        if s or not first:
                            tick(s, t)
                        if work is None:
                            drained.next()
                        else:
                            dve.wait_ge(bank_free, drained.next())
                            work(i, s)
                    if ada is not None:
                        ada_group(i + ada)
                if peel:
                    body(0, True)
                    bodies(n // RING - 1, lambda i: body(i + 1))
                    return
                bodies(n // RING, body, last, {split: 2 * RING, drained: RING, mf: 1} if ada is not None else None)

            def tiles_N(groups, ada=None):
                def body(i):
                    for s in range(RING):
                        tick(s)
                    drained.next(4)
                    if ada is not None:
                        ada_group(i + ada)
                bodies(groups, body, False, {split: 2 * RING, drained: RING, mf: 1} if ada is not None else None)

            def ada_group(g):
                for s in range(RING):
                    tick(s)
                dve.wait_ge(mod_full, mf.next())
                dve.tensor_tensor(mod[:, bass.ds(g * 4, 4)], pb[:, 7, 0:4], v1[:, bass.ds(g * 4 + V_ADA, 4)],
                                  ALU.add).then_inc(mod_read, 1)

            def halves(src, dH, dL, by=1):
                dve.tensor_copy(dH, src)
                dve.drain()
                dve.tensor_tensor(dL, src, dH.bitcast(F32), ALU.subtract)
                dve.drain().then_inc(y_ready, by)

            roots = Count()

            def newton(bank, y, v, t, scale):
                dve.wait_ge(rooted, roots.next())
                dve.tensor_scalar(v, bank, scale, EPS, ALU.mult, ALU.add)
                dve.reciprocal(y, y)
                dve.drain()
                dve.scalar_tensor_tensor(t, y, -0.5, y, ALU.mult, ALU.mult)
                dve.drain()
                dve.tensor_tensor(t, t, v, ALU.mult)
                dve.drain()
                dve.scalar_tensor_tensor(y, t, 1.5, y, ALU.add, ALU.mult)
                dve.drain()

            def norm_to(gain, shift, dH, dL, ready):
                for k in range(KT):
                    t = st[:, k % 4]
                    dve.scalar_tensor_tensor(t, x[:, k], gain[:, k:k + 1], pb[:, 5], ALU.mult, ALU.mult)
                    dve.drain()
                    if shift is None:
                        dve.tensor_copy(dH[:, k], t)
                        dve.drain()
                        dve.tensor_tensor(dL[:, k], t, dH[:, k].bitcast(F32), ALU.subtract)
                    else:
                        dve.tensor_scalar(dH[:, k], t, shift[:, k:k + 1], None, ALU.add)
                        dve.drain()
                        dve.scalar_tensor_tensor(dL[:, k], t, shift[:, k:k + 1], dH[:, k].bitcast(F32), ALU.add,
                                                 ALU.subtract)
                    dve.drain().then_inc(ready, 1)

            def rstd(early=True):
                if early:
                    tick(0)
                newton(pb[:, 4, 0:4], stat[:, 8:12], stat[:, 12:16], stat[:, 4:8], 1.0 / D)
                dve.sem_inc(rs_ready, 1)

            def norm(gain, shift, dH, dL, ready, early=True):
                rstd(early)
                dve.wait_ge(rs_full, rf.next())
                norm_to(gain, shift, dH, dL, ready)

            def add_to_x(i, s):
                n = at(i * RING + s)
                dve.tensor_tensor(x[:, n], x[:, n], st[:, s:s + 1], ALU.add).then_inc(st_free, 1)

            for s in range(AHEAD):
                tick(s - AHEAD)
            dve.wait_ge(setup_in, 64)
            dve.wait_ge(pos_in, 16)
            pi2 = 2 * np.pi
            c1 = 6.28125
            c2 = float(np.float32(round((pi2 - c1) * 2 ** 21) / 2 ** 21))
            c3 = float(np.float32(pi2 - c1 - c2))
            dve.tensor_copy(st[:, 0], st[:, 3].bitcast(I32))
            dve.drain()
            dve.tensor_scalar(st[:, 1], st[:, 0], cst[:, C_FREQ:C_FREQ + 1], None, ALU.mult)
            dve.drain()
            dve.tensor_scalar(st[:, 2].bitcast(I32), st[:, 1], 1.0 / pi2, None, ALU.mult)
            dve.drain()
            dve.tensor_copy(st[:, 0], st[:, 2].bitcast(I32))
            dve.drain()
            for c in (c1, c2, c3):
                dve.scalar_tensor_tensor(st[:, 1], st[:, 0], -c, st[:, 1], ALU.mult, ALU.add)
                dve.drain()
            dve.tensor_scalar(st[:, 1], st[:, 1], 3.1415925, -3.1415925, ALU.min, ALU.max)
            dve.drain().then_inc(trig_arg, 1)
            dve.wait_ge(c_act, 1)
            cHL2 = cHL[:, 0:2 * KT].rearrange("p (k a) -> p k a", a=2)
            dve.tensor_scalar(cHL[:, 2 * KT:], ones, 0.0, None, ALU.mult)
            dve.tensor_copy(cHL2[:, :, 0], cs[:, 1])
            dve.drain()
            dve.tensor_tensor(cHL2[:, :, 1], cs[:, 1], cHL2[:, :, 0].bitcast(F32), ALU.subtract)
            dve.drain().then_inc(c_ready, 1)
            dve.wait_ge(trig, 2)
            dve.tensor_scalar(sinT, sinT, cst[:, C_SIGN:C_SIGN + 1], None, ALU.mult)
            dve.drain().then_inc(layer_done, 1)
            dve.sem_inc(mix_free, 2)
            dve.sem_inc(mod_read, 1)

            rp, sc, mixed = Count(), Count(), Count()

            def pairs(first):
                def work(i, s):
                    if s % 2 == 0:
                        return
                    g, b = st[:, s - 1:s], st[:, s:s + 1]
                    n = bass.ds(i * 2 + s // 2 + 16, 1)
                    if first:
                        dve.tensor_tensor(act3[:, n], g, b, ALU.mult)
                    else:
                        dve.tensor_tensor(b, g, b, ALU.mult)
                        dve.drain()
                        dve.tensor_tensor(act3[:, n], act3[:, n], b, ALU.add)
                    dve.drain().then_inc(st_free, 2)
                tiles_T(16, work)

            def geff_of(norm_at, scale_at):
                dve.tensor_scalar(geff[:], mod[:, scale_at:scale_at + 8], 1.0, None, ALU.add)
                dve.drain()
                dve.tensor_tensor(geff[:], geff[:], v1[:, norm_at:norm_at + 8], ALU.mult)
                dve.drain()

            with repeat(dve, LAYERS, {split: LAYER_TILES, drained: LAYER_BANKS, roots: 7, rp: 8, sc: 16,
                                      mixed: 8, mf: 12, rf: 2}) as l:
                rstd(early=False)
                with repeat(dve, 4, {split: RING, mf: 1}) as i:
                    ada_group(i)
                dve.drain()
                tick(0)
                dve.tensor_tensor(bpps[:], v1[:, V_BP:V_BP + 8], v1[:, V_PS:V_PS + 8], ALU.mult)
                geff_of(V_N1, 8)
                dve.wait_ge(rs_full, rf.next())
                norm_to(geff, mod[:, 0:8], hH, hL, h_ready)
                tiles_T(8, None, peel=True)
                tiles_N(2)
                with repeat(dve, R_HEADS, {rp: 2, sc: 4, roots: 1}) as h:
                    for j, dst in ((0, Qr), (1, Kr)):
                        f = 1.0 if j == 0 else float(P) ** -0.5
                        t = act3[:, bass.ds(h + 4 * j, 1), :].rearrange("p a s -> p (a s)")
                        dve.wait_ge(rope_full, rp.next())
                        dve.scalar_tensor_tensor(rT, pb[:, 4 + j], f, sinT, ALU.mult, ALU.mult)
                        dve.scalar_tensor_tensor(t, t, f, cosT, ALU.mult, ALU.mult)
                        dve.drain()
                        dve.tensor_tensor(dst, t, rT, ALU.add)
                        dve.drain().then_inc(rope_ready, 1)
                    for j in range(TT):
                        w = S - j * P
                        dve.wait_ge(score_full, sc.next())
                        dve.tensor_tensor(sT[:, sT_at[j]:sT_at[j] + w].rearrange("p (a s) -> p a s", a=1),
                                          pb[:, 6 + j % 2:7 + j % 2, 0:w], dec[:, bass.ds(h, 1), 0:w],
                                          ALU.mult).then_inc(score_ready, 1)
                    newton(pb[:, 6], sT[:, 0:512], sT[:, 512:1024], rT, 1.0 / R_V)
                    for e in range(2):
                        dve.tensor_tensor(act3[:, bass.ds(h + 4 * e, 1), :].rearrange("p a s -> p (a s)"),
                                          pb[:, 4 + e], sT[:, 0:512], ALU.mult).then_inc(o_normed, 1)

                def y_ret(i, s):
                    o = act3[:, bass.ds(i * 2 + 4 * (s % 2) + s // 2, 1), :]
                    n = bass.ds(i * RING + s, 1)
                    dve.tensor_tensor(st[:, s:s + 1], st[:, s:s + 1], o, ALU.mult)
                    dve.drain()
                    halves(st[:, s:s + 1], yH[:, n], yL[:, n])
                    dve.sem_inc(st_free, 1)
                tiles_T(8, y_ret, ada=4)
                pairs(True)
                tiles_T(8, None, ada=6)
                tiles_N(2, ada=8)
                dve.wait_ge(bank_free, drained.value())
                for t in range(TT):
                    vt = act3[:, 8 + 2 * t:10 + 2 * t].rearrange("p a s -> p (a s)")
                    dve.tensor_tensor_reduce(yF[:, 0:1024], vt, vt, 1.0, 0.0, ALU.mult, ALU.add,
                                             stat[:, 8 + t:9 + t])
                    dve.drain()
                dve.tensor_scalar(stat[:, 12:16], stat[:, 8:12], 1.0 / D, EPS, ALU.mult, ALU.add)
                dve.drain().then_inc(v_mean, 1)
                y, v, t = stat[:, 8:12], stat[:, 12:16], stat[:, 4:8]
                dve.wait_ge(rooted, roots.next())
                dve.reciprocal(y, y)
                dve.drain()
                dve.scalar_tensor_tensor(t, y, -0.5, y, ALU.mult, ALU.mult)
                dve.drain()
                dve.tensor_tensor(t, t, v, ALU.mult)
                dve.drain()
                dve.scalar_tensor_tensor(y, t, 1.5, y, ALU.add, ALU.mult)
                dve.drain()
                for t in range(TT):
                    vt = act3[:, 8 + 2 * t:10 + 2 * t].rearrange("p a s -> p (a s)")
                    dve.tensor_scalar(vt, vt, stat[:, 8 + t:9 + t], None, ALU.mult).then_inc(v_normed, 1)
                for n in range(KT):
                    dve.wait_ge(mix_full, mixed.next())
                    pv = pb[:, 4 + n % 2]
                    pv4 = pv.rearrange("p (n t) -> p n t", n=TT)
                    b4 = bsb[:, n // 2:n // 2 + 1].to_broadcast([P, TT, P])
                    dve.scalar_tensor_tensor(pv4, pv4, v1[:, V_GAIN + n:V_GAIN + n + 1], b4, ALU.mult, ALU.add)
                    dve.drain()
                    dve.tensor_tensor(A[:, n], A[:, n], pv, ALU.mult)
                    dve.drain().then_inc(mix_free, 1)
                    halves(A[:, n], yH[:, n], yL[:, n])
                pairs(False)
                tiles_T(8, None, ada=10)
                dve.wait_ge(bank_free, drained.value())
                for g in range(4):
                    src, cur = A[:, 2 * g:2 * g + 2], A[:, 2 * g:2 * g + 2]
                    for j in range(g + 1):
                        d, dst = 2 ** j, B[:, 2 * (j % 2):2 * (j % 2) + 2]
                        dve.tensor_tensor(dst[:, :, d:S], cur[:, :, d:S], cur[:, :, 0:S - d], ALU.add)
                        dve.tensor_copy(dst[:, :, 0:d], cur[:, :, 0:d])
                        dve.drain()
                        cur = dst
                    for j in range(2):
                        dve.tensor_tensor(cur[:, j, 0:16], cur[:, j, 0:16], edge[:, g], ALU.mult)
                    dve.drain()
                    dst = B[:, 4:6]
                    dve.scalar_tensor_tensor(dst, cur, 1.0 / 2 ** (g + 1), src, ALU.mult, ALU.subtract)
                    dve.drain()
                    halves(dst, yH[:, 2 * g:2 * g + 2], yL[:, 2 * g:2 * g + 2], 2)
                for g in range(4):
                    tick(g)
                    for e in range(2):
                        n = 2 * g + e
                        dve.wait_ge(bank_free, drained.next())
                        halves(st[:, n % 4], yH[:, n], yL[:, n])
                        dve.sem_inc(st_free, 1)
                pairs(False)
                tick(0)
                for n in range(KT):
                    halves(M[:, n], yH[:, n], yL[:, n])
                tiles_T(8, add_to_x, peel=True)
                geff_of(V_N2, 32)
                norm(geff, mod[:, 24:32], hH, hL, h_ready)
                def hidden(i, s):
                        n = at(i * RING + s)
                        u = st[:, s:s + 1]
                        dve.scalar_tensor_tensor(u, u, 0.0, u, ALU.max, ALU.mult)
                        dve.drain()
                        halves(u, yH[:, n], yL[:, n])
                        dve.sem_inc(st_free, 1)
                tiles_T(8, hidden, peel=True)
                with repeat(dve, 3, {split: 16, drained: 16}):
                    tiles_T(8, add_to_x)
                    tiles_T(8, hidden)
                tiles_T(8, add_to_x)
                dve.drain().then_inc(layer_done, 1)

            gt = Count()

            def conv_ffn(layer, last=False):
                norm(v2[:, W_FFN + 8 * layer:W_FFN + 8 * layer + 8], None, hH, hL, h_ready)
                first = 0
                for j, n in enumerate(SLABS):
                    def body(i, skip=False):
                        for s in range(RING):
                            if s or not skip:
                                tick(s)
                            dve.wait_ge(bank_free, drained.next())
                            ch = i * 2 + (first + s // 2 + (s % 2) * (FF2 // P))
                            w = [v2[:, at(ch + (W_CW + (layer * 3 + t) * UP))] for t in range(3)]
                            b = v2[:, at(ch + (W_CB + layer * UP))]
                            u, c = st[:, s], A[:, s]
                            dve.tensor_scalar(c, u, w[2], b, ALU.mult, ALU.add)
                            dve.drain()
                            dve.scalar_tensor_tensor(c[:, 1:S], u[:, 0:S - 1], w[1], c[:, 1:S], ALU.mult, ALU.add)
                            dve.drain()
                            dve.scalar_tensor_tensor(c[:, 2:S], u[:, 0:S - 2], w[0], c[:, 2:S], ALU.mult,
                                                     ALU.add).then_inc(st_free, 1)
                            dve.drain()
                            if s % 2:
                                dve.sem_inc(conv_done, 1)
                                dve.wait_ge(gated, gt.next())
                                a = A[:, s - 1:s]
                                dve.tensor_tensor(a, a, A[:, s:s + 1], ALU.mult)
                                dve.drain()
                                m = at(i * 2 + s // 2)
                                halves(a, yH[:, m], yL[:, m])
                    if j == 0:
                        body(0, True)
                        with repeat(dve, n // 2 - 1, {**ring, gt: 2}) as i:
                            body(i + 1)
                    else:
                        with repeat(dve, n // 2, {**ring, gt: 2}) as i:
                            body(i)
                    first += n
                    tiles_T(8, add_to_x, last=last and j == len(SLABS) - 1)

            rstd(early=False)
            dve.wait_ge(tab_in, 64)
            dve.wait_ge(rs_full, rf.next())
            for k in range(KT):
                dve.scalar_tensor_tensor(x[:, k], x[:, k], v2[:, W_FIN1 + k:W_FIN1 + k + 1], pb[:, 5], ALU.mult,
                                         ALU.mult).then_inc(x_ready, 1)
            w3 = wfraw.rearrange("p (k n) -> p k n", k=KT)
            dve.tensor_copy(wfH[:], w3)
            dve.drain()
            dve.tensor_tensor(wfL[:], w3, wfH[:].bitcast(F32), ALU.subtract)
            dve.drain().then_inc(wf_ready, 1)
            norm(v2[:, W_MIX:W_MIX + 8], None, hH, hL, h_ready, early=False)
            dve.wait_ge(f_full, 1)
            for t in range(TT):
                dve.tensor_tensor(lf[:, 0, t * 16:(t + 1) * 16], pb[:, 4, t * 16:(t + 1) * 16],
                                  v2[:, W_BF:W_BF + 16], ALU.add)
            dve.drain().then_inc(z_ready, 1)
            dve.tensor_scalar(lf[:, 4], lf[:, 0], 0.0, None, ALU.min)
            dve.wait_ge(e_ready, 1)
            dve.drain()
            dve.tensor_tensor(lf[:, 5], lf[:, 4], lf[:, 3], ALU.subtract)
            dve.drain().then_inc(z_ready, 1)
            tiles_T(16, None)
            tiles_N(2)
            dve.wait_ge(bank_free, drained.value())
            dve.wait_ge(c_full, 1)
            dve.tensor_copy(cT[0:16], pb[0:16, 5])
            dve.drain().then_inc(c_out, 1)
            sf, pr, pvc, te = Count(), Count(1), Count(1), Count(1)

            def attention(pairs_, its, maximum, probs, start):
                with repeat(dve, pairs_, {sf: 8, pr: 8, pvc: 8, te: 8}) as p:
                    start(p)
                    for n in range(9):
                        if n < 8:
                            dve.wait_ge(s_full, sf.next())
                            maximum(n, n // 4, n % 4, p)
                            dve.drain().then_inc(max_ready, 1)
                        if n >= 1:
                            m = n - 1
                            w = len(its[m % 4]) * P
                            dve.wait_ge(p_ready, pr.next())
                            dve.reciprocal(stat[:, 4 + m % 2:5 + m % 2], stat[:, 2 + m % 2:3 + m % 2])
                            dve.drain()
                            dve.tensor_scalar(probs(m)[:, 0:w], probs(m)[:, 0:w], stat[:, 4 + m % 2:5 + m % 2], None,
                                              ALU.mult).then_inc(p_normed, 1)
                    dve.wait_ge(pv_done, pvc.next(8))
                    te.next(8)
                    n = bass.ds(p, 1)
                    dve.tensor_copy(yH[:, n], pb[:, 6:7])
                    dve.drain()
                    dve.tensor_tensor(yL[:, n], pb[:, 6:7], yH[:, n].bitcast(F32), ALU.subtract)
                    dve.drain().then_inc(y_ready, 1)

            def selectors(p):
                for j in range(2):
                    dve.tensor_scalar(sel[0:16, j], ones[0:16], cst[0:16, bass.ds(p * 2 + j + C_ID, 1)], -1.0,
                                      ALU.mult, ALU.mult).then_inc(sel_ready, 1)

            def maximum_a(n, hp, it, p):
                if n < 2:
                    dve.wait_ge(p_ready, pr.value())
                dve.wait_ge(t_full, te.value() + max(0, n - 1))
                dve.tensor_reduce(stat[:, n % 2:n % 2 + 1], pb[:, n % 2, 0:(it + 1) * P], AX.X, ALU.max, negate=True)

            attention(A_HEADS // 2, A_IT, maximum_a, lambda m: Pa[m % 2], selectors)
            tiles_T(8, add_to_x)
            conv_ffn(0)
            norm(v2[:, W_MIX + 8:W_MIX + 16], None, hH, hL, h_ready)
            norm_to(v2[:, W_KV:W_KV + 8], None, yH, yL, y_ready)
            tiles_T(12, None, peel=True)
            tiles_T(12, None)
            tiles_N(3)
            dve.wait_ge(bank_free, drained.value())

            def maximum_b(n, hp, it, p):
                dve.wait_ge(t_full, te.value() + max(0, n - 1))
                sbuf, o = Pb[n % 2], 0
                for g in range(3):
                    first = max(0, it - 1) if g == 0 else 0
                    w = (it + 1 - first) * P
                    end = 256 + 512 * g
                    dve.scalar_tensor_tensor(sbuf[:, o:o + w], dist[:, end - w:end],
                                             cst[:, bass.ds(p * 2 + (C_SLOPE + 8 * g + hp), 1)],
                                             pb[:, 3 * (n % 2) + g, 0:w], ALU.mult, ALU.add)
                    o += w
                dve.drain()
                dve.tensor_reduce(stat[:, n % 2:n % 2 + 1], sbuf[:, 0:o], AX.X, ALU.max, negate=True)

            attention(4, B_IT, maximum_b, lambda m: Pb[m % 2], lambda p: None)
            for s in range(RING):
                tick(s)
                for e in range(2):
                    n = 2 * s + e
                    dve.wait_ge(bank_free, drained.next())
                    dve.tensor_tensor(x[:, n], x[:, n], st[:, n % 4], ALU.add).then_inc(st_free, 1)
            conv_ffn(1, last=True)
            rstd(early=False)
            dve.wait_ge(rs_full, rf.next())
            for k in range(KT):
                dve.scalar_tensor_tensor(act3[:, k], x[:, k], v2[:, W_FIN + k:W_FIN + k + 1], pb[:, 5], ALU.mult,
                                         ALU.mult).then_inc(out_ready, 1)


def constants():
    f = np.float32
    c = np.zeros((P, C_ALL), f)
    i, j = np.arange(P)[:, None], np.arange(P)[None]
    c[:, C_ID:C_ID + P] = i == j
    c[:, C_PERM:C_PERM + P] = (i + 64) % P == j
    c[:, C_ONES:C_ONES + P] = 1
    c[:, C_CAUSAL:C_CAUSAL + P] = np.where(j > i, f(NEG), f(0))
    for g in range(4):
        w = 2 ** (g + 1)
        c[:, C_EDGE + 16 * g:C_EDGE + 16 * g + 16] = w / np.minimum(np.arange(1, 17), w)
    half = P // 2
    freq = f(10000.0) ** (-np.arange(half, dtype=f) / f(half))
    c[:, C_FREQ] = np.concatenate([freq, freq])
    c[:, C_SIGN] = np.where(np.arange(P) < half, -1, 1)
    c[:, C_EPS] = EPS
    c[:, C_HALFPI] = np.pi / 2
    c[:, C_SLOPE:C_SLOPE + 24] = np.exp2(-8.0 * np.arange(1, 25) / 24)
    log_gamma = np.log1p(-np.power(2.0, -5.0 - np.arange(R_HEADS)))
    rel = np.arange(S)[None] - i
    decay = np.stack([np.where(rel >= 0, np.exp(lg * np.maximum(rel, 0)), 0) for lg in log_gamma], 1).astype(f)
    t = np.zeros((P, 1792), f)
    at = 0
    for dil, w in ((1, 256), (4, 512), (16, 512)):
        d = i - (np.arange(w)[None] - (w - P))
        t[:, at:at + w] = np.where((d >= 0) & (d % dil == 0) & (d <= dil * 128), -d, NEG)
        at += w
    t[:, 1280:1792] = np.arange(S)[None] >= i
    return c, decay.reshape(P, 2048), t


def tiles_t(w):
    k, c = w.shape
    t = w.reshape(k // P, P, c // P, P).transpose(2, 1, 0, 3).reshape(c // P, P, k)
    return np.pad(t, ((0, 0), (0, 0), (0, TILE - k))) if k < TILE else t


def tiles_n(w):
    g = w.shape[1] // S
    return w.reshape(4, 2, P, g, S).transpose(3, 0, 2, 1, 4).reshape(4 * g, P, TILE)


def pairs_of(a, b):
    return np.stack([a, b], 1).reshape(-1, *a.shape[1:])


def with_ada(w, ada):
    return np.stack([w.reshape(2, 4, P, TILE), ada.reshape(2, 4, P, TILE)], 1).reshape(16, P, TILE)


def columns(v):
    return np.ascontiguousarray(v.reshape(-1, P).T)


def kernel(**inputs):
    import concourse.bacc as bacc
    from concourse.bass_utils import run_bass_kernel_spmd

    a = {k: np.asarray(v) for k, v in inputs.items()}
    parts = []
    for l in range(LAYERS):
        w = a["w_in"][l]
        q, k, v, g, u, vs, p, gates = np.split(w, np.cumsum([512, 512, 1024, 1024, 1024, 1024, 1024]), axis=1)
        gate = [tiles_t(gates[:, D * n:D * (n + 1)]) for n in range(3)]
        br = [tiles_t(a["w_branch"][l, n]) for n in range(3)]
        wp = a["w_pool"][l].reshape(4, 2, P, 256).transpose(0, 2, 1, 3).reshape(4, P, 512)
        ada = tiles_n(a["w_ada"][l])
        parts += [ada[0:16], tiles_t(q), tiles_t(k), tiles_n(v), with_ada(tiles_t(g), ada[16:24]),
                  pairs_of(gate[0], br[0]), with_ada(tiles_t(u), ada[24:32]), with_ada(tiles_n(vs), ada[32:40]),
                  pairs_of(gate[1], br[1]), with_ada(tiles_t(p), ada[40:48]),
                  np.pad(wp, ((0, 0), (0, 0), (0, TILE - 512))), pairs_of(gate[2], br[2]), tiles_t(a["w_out"][l])]
        for n in range(4):
            parts += [tiles_t(a["w_ff1"][l][:, D * n:D * (n + 1)]), tiles_t(a["w_ff2"][l][D * n:D * (n + 1)])]

    def conv_ffn(l):
        up, down, at = tiles_t(a["ffn_w_up_2"][l]), a["ffn_w_down_2"][l], 0
        for n in SLABS:
            yield pairs_of(up[at:at + n], up[at + UP // 2:at + UP // 2 + n])
            yield tiles_t(down[at * P:(at + n) * P])
            at += n

    w = a["a_w_in_2"][0]
    parts += [tiles_t(w[:, 0:2048]), tiles_n(w[:, 2048:3072]), tiles_t(a["a_w_out_2"][0]), *conv_ffn(0)]
    wkv = a["w_kv_2"]
    wo = tiles_t(a["b_w_out_2"][0])[:, :, 0:512].reshape(4, 2, P, 512).transpose(0, 2, 1, 3).reshape(4, P, TILE)
    parts += [tiles_t(a["b_w_q_2"][0]), tiles_t(wkv[:, 0:1536]), tiles_n(wkv[:, 1536:3072]), wo, *conv_ffn(1)]
    stream = np.concatenate(parts)
    assert stream.shape == (TILES, P, TILE), stream.shape

    c, decay, tables = constants()
    vec1 = np.stack([np.concatenate([columns(a[n][l]) for n in (
        "norm1", "norm2", "b_ada", "vnorm_gmlp", "b_pool", "pool_scale")], 1) for l in range(LAYERS)])
    bf = np.ascontiguousarray(np.broadcast_to(a["a_b_f_2"][0][None], (P, 16)))
    cw, final = a["ffn_conv_w_2"], columns(a["final_norm"])
    vec2 = np.concatenate([columns(a["kv_norm_g_2"]), columns(a["mix_norm_g_2"]), columns(a["ffn_norm_g_2"]),
                           columns(a["final_norm_g_2"]), final, columns(cw), columns(a["ffn_conv_b_2"]), bf], 1)
    data = {
        "stream": stream,
        "xT": np.ascontiguousarray(a["x"][0].T.reshape(KT, P, S).transpose(1, 0, 2)),
        "cvec": columns(a["c"][0]),
        "pos": np.ascontiguousarray(np.broadcast_to(a["positions"], (P, S))),
        "consts": c, "decay": decay, "tables": tables, "vec1": vec1,
        "ws": np.ascontiguousarray(a["ws_gmlp"].transpose(0, 3, 1, 2).reshape(LAYERS, P, 512)),
        "bs": a["bs_gmlp"].reshape(LAYERS, 512),
        "vec2": vec2,
        "wf": np.ascontiguousarray(w[:, 3072:].reshape(KT, P, 16).transpose(1, 0, 2).reshape(P, 128)),
    }
    nc = bacc.Bacc("TRN2", target_bir_lowering=False, num_devices=1)
    args = [nc.dram_tensor(n, v.shape, mybir.dt.from_np(v.dtype), kind="ExternalInput").ap() for n, v in data.items()]
    out = nc.dram_tensor("outT", (P, KT, S), F32, kind="ExternalOutput").ap()
    build(nc, *args, out)
    r = run_bass_kernel_spmd(nc, [data], core_ids=[0])
    return np.ascontiguousarray(r.results[0]["outT"].transpose(1, 0, 2).reshape(D, S).T)[None]
```

```python
from contextlib import ExitStack, contextmanager

import numpy as np

import concourse.bass as bass
from concourse import mybir

F32 = mybir.dt.float32
F32R = mybir.dt.float32r
I32 = mybir.dt.int32
ACT = mybir.ActivationFunctionType
ALU = mybir.AluOpType
AX = mybir.AxisListType

P = 128
S = 512
D = 1024
KT = D // P
TT = S // P
LAYERS = 2
R_HEADS, R_V = 4, 256
A_HEADS = 16
B_GROUPS = ((1, 128), (4, 512), (16, 512))
FF2 = 2816
SLABS = (8, 8, 6)
EPS = 1e-6
NEG = -1e30
RING = 4
AHEAD = RING - 1
TILE = KT * P

N_ADA = 6 * D // P
LAYER_TILES = N_ADA + 8 * 8 + 3 * 16 + 4 + 8 * 7
LAYER_BANKS = LAYER_TILES - N_ADA + 4
FFN2_TILES = 2 * sum(SLABS) + 8 * len(SLABS)
TILES = LAYERS * LAYER_TILES + (16 + 8 + 8 + FFN2_TILES) + (12 + 12 + 12 + 4 + FFN2_TILES)

C_ID, C_PERM, C_ONES, C_CAUSAL, C_EDGE = 0, P, 2 * P, 3 * P, 4 * P
C_FREQ = C_EDGE + 4 * 16
C_SIGN, C_EPS, C_HALFPI = C_FREQ + 1, C_FREQ + 2, C_FREQ + 3
C_SLOPE = C_FREQ + 4
C_ALL = C_SLOPE + 24
V_N1, V_N2, V_ADA, V_GAIN, V_BP, V_PS, V_ALL = 0, 8, 16, 64, 72, 80, 88
W_KV, W_MIX, W_FFN, W_FIN, W_FIN1, W_CW, W_CB, W_BF, W_ALL = 0, 8, 24, 40, 48, 56, 56 + 264, 56 + 352, 56 + 368
UP = 2 * FF2 // P


class Count:

    def __init__(self, start=0):
        self.n, self.off = start, None

    def value(self, back=0):
        return self.n - back if self.off is None else self.off + (self.n - back)

    def next(self, k=1):
        self.n += k
        return self.value()


def at(i):
    return slice(i, i + 1) if isinstance(i, int) else bass.ds(i, 1)


@contextmanager
def repeat(eng, trips, steps):
    saved = [(c, c.n, c.off, k) for c, k in steps.items()]
    with eng.Fori(0, trips) as i:
        for c, _, off, k in saved:
            c.off = i * k if off is None else off + i * k
        yield i
        for c, n, _, k in saved:
            assert c.n == n + k, f"a pass adds {c.n - n}, not {k}: {[x.n - m for x, m, _, _ in saved]}"
    for c, n, off, k in saved:
        c.n, c.off = n + k * trips, off


def build(nc, stream, xT, cvec, pos, consts, decay, tables, vec1, ws, bs, vec2, wf, outT):
    with ExitStack() as ctx:
        def sb(name, shape, dt=F32):
            return ctx.enter_context(nc.sbuf_tensor(name, shape, dt))

        def sem(name):
            return ctx.enter_context(nc.semaphore(name))

        raw = sb("raw", [P, RING, TILE])
        hi = sb("hi", [P, RING, TILE], F32R)
        lo = sb("lo", [P, RING, TILE], F32R)
        x = sb("x", [P, KT, S])
        with nc.sbuf_tensor("hH", [P, KT, S], F32R) as hH, nc.sbuf_tensor("hL", [P, KT, S], F32R) as hL:
            pass
        hF = sb("hF", [P, 2 * KT * S])
        with nc.sbuf_tensor("yH", [P, KT, S], F32R) as yH, nc.sbuf_tensor("yL", [P, KT, S], F32R) as yL:
            pass
        yF = sb("yF", [P, 2 * KT * S])
        with nc.sbuf_tensor("halved", [P, 3 * KT, S], F32R) as halved:
            pass
        act3 = sb("act3", [P, 3 * KT, S])
        halfB, halfA, halfM = halved[:, KT:2 * KT], halved[:, 0:KT], halved[:, 2 * KT:3 * KT]
        A, B, M = act3[:, 0:KT], act3[:, KT:2 * KT], act3[:, 2 * KT:3 * KT]
        st = sb("st", [P, 4, S])
        tab = sb("tab", [P, 3072])
        with nc.sbuf_tensor("cHalves", [P, 2, S], F32R) as cHalves:
            pass
        scr = sb("scr", [P, 1280])
        cst = sb("cst", [P, C_ALL])
        v1 = sb("v1", [P, V_ALL])
        v2 = sb("v2", [P, S])
        mod = sb("mod", [P, N_ADA])
        geff = sb("geff", [P, 8])
        bpps = sb("bpps", [P, 8])
        cs = sb("cs", [P, 3, 8])
        cHL = sb("cHL", [P, 2 * KT + P], F32R)
        stat = sb("stat", [P, 16])
        pb = ctx.enter_context(nc.psum_tensor("pb", [P, 8, S], F32))

        dec = tab[:, 0:2048].rearrange("p (h s) -> p h s", h=R_HEADS)
        cosT, sinT = tab[:, 2048:2560], tab[:, 2560:3072]
        dist, pTb, tri = tab[:, 0:1280], tab[:, 1280:2560], tab[:, 2560:3072]
        wsT = scr[:, 0:512].rearrange("p (g t) -> p g t", g=4)
        bsb = scr[:, 512:1024].rearrange("p (g t) -> p g t", g=4)
        ident, perm = cst[:, C_ID:C_ID + P], cst[:, C_PERM:C_PERM + P]
        ones, causal = cst[:, C_ONES:C_ONES + P], cst[:, C_CAUSAL:C_CAUSAL + P]
        edge = cst[:, C_EDGE:C_EDGE + 64].rearrange("p (g t) -> p g t", g=4)
        epsc = cst[:, C_EPS:C_EPS + 1]
        Mf = act3[:, 2 * KT:3 * KT].rearrange("p k s -> p (k s)")
        Qr, Kr = ([Mf[:, (2 * a + b) * S:(2 * a + b + 1) * S] for a in range(2)] for b in range(2))
        sT = Mf[:, 2048:3328]
        rT = Mf[:, 3328:3840]
        sT_at = [0, 512, 896, 1152]
        Osq, root_r, mean_r, temp_r = (yF[:, j * 2 * S:(j + 1) * 2 * S] for j in range(4))
        QaH, QaL, KaH, KaL = ([hH[:, j + q] for q in range(2)] for j in (0, 2, 4, 6))
        Va = [hF[:, (8 + q) * S:(9 + q) * S].rearrange("p (j e) -> p j e", j=TT) for q in range(2)]
        Pa = [hF[:, (10 + n) * S:(11 + n) * S] for n in range(3)]
        pTa = hF[:, 13 * S:14 * S]
        cTH, cTL = cHalves[:, 0], cHalves[:, 1]
        sel = hL[:, 6].rearrange("p (a b) -> p a b", a=4)
        causalR, identR = (hL[:, 7, j * P:(j + 1) * P] for j in range(2))
        wfraw = yF[:, 0:128]
        lf = yF[:, 128:512].rearrange("p (a b) -> p a b", a=6)
        Vall = hF[:, 0:6144].rearrange("p (g j e) -> p g j e", g=3, j=TT)
        Qb = [yF[:, 3584:4096], yF[:, 7680:8192], hF[:, 7680:8192]]
        Kb = yF[:, 2048:3584].rearrange("p (g s) -> p g s", g=3)
        Vb = st[:, 0:3].rearrange("p g (j e) -> p g j e", j=TT)
        Pb = [scr[:, 0:1280], hF[:, 6144:7424], yF[:, 6144:7424]]
        modrow = v2[0:2, 0:S]
        wfH = sb("wfH", [P, KT, 16], F32R)
        wfL = sb("wfL", [P, KT, 16], F32R)

        landed = [sem(f"landed{s}") for s in range(RING)]
        hi_ready = sem("hi_ready")
        lo_ready = sem("lo_ready")
        tile_done = sem("tile_done")
        bank_free = sem("bank_free")
        st_free = sem("st_free")
        setup_in = sem("setup_in")
        pos_in = sem("pos_in")
        vec_seen = sem("vec_seen")
        vec_in = sem("vec_in")
        tab_in = sem("tab_in")
        ws_ready = sem("ws_ready")
        layer_done = sem("layer_done")
        c_act = sem("c_act")
        c_ready = sem("c_ready")
        trig_arg = sem("trig_arg")
        trig = sem("trig")
        osq_ready = sem("osq_ready")
        squared = sem("squared")
        sq_sum = sem("sq_sum")
        rs_ready = sem("rs_ready")
        rs_full = sem("rs_full")
        row_ready = sem("row_ready")
        mod_full = sem("mod_full")
        mod_read = sem("mod_read")
        summed = sem("summed")
        rooted = sem("rooted")
        h_ready = sem("h_ready")
        y_ready = sem("y_ready")
        rope_full = sem("rope_full")
        rope_ready = sem("rope_ready")
        score_full = sem("score_full")
        score_ready = sem("score_ready")
        o_full = sem("o_full")
        o_normed = sem("o_normed")
        half_ready = sem("half_ready")
        v_mean = sem("v_mean")
        x_ready = sem("x_ready")
        v_normed = sem("v_normed")
        mix_full = sem("mix_full")
        mix_free = sem("mix_free")
        f_full = sem("f_full")
        z_ready = sem("z_ready")
        e_ready = sem("e_ready")
        c_full = sem("c_full")
        c_out = sem("c_out")
        wf_ready = sem("wf_ready")
        qk_staged = sem("qk_staged")
        k_staged = sem("k_staged")
        v_staged = sem("v_staged")
        sel_ready = sem("sel_ready")
        s_full = sem("s_full")
        s_read = sem("s_read")
        max_ready = sem("max_ready")
        p_ready = sem("p_ready")
        p_normed = sem("p_normed")
        t_full = sem("t_full")
        t_ready = sem("t_ready")
        pv_done = sem("pv_done")
        conv_done = sem("conv_done")
        gated = sem("gated")
        out_ready = sem("out_ready")
        out_done = sem("out_done")

        block = ctx.enter_context(nc.Block())

        B_IT = [[(g, j) for g in range(3) for j in range(TT) if j <= it and (g or j >= it - 1)] for it in range(TT)]
        A_IT = [[(0, j) for j in range(it + 1)] for it in range(TT)]

        @block.sync
        def _(sp):
            for dst, src in ((cst[:], consts), (x[:], xT), (cs[:, 0], cvec), (tab[:, 0:2048], decay)):
                sp.dma_start(dst, src).then_inc(setup_in, 16)
            freed = Count()
            with repeat(sp, TILES // RING, {freed: RING}) as i:
                for s in range(RING):
                    sp.wait_ge(lo_ready, freed.next())
                    sp.dma_start(raw[:, s], stream[bass.ds(i * RING + s, 1)].rearrange("a p c -> (a p) c")
                                 ).then_inc(landed[s], 16)
            for n in range(KT):
                sp.wait_ge(out_ready, n + 1)
                sp.dma_start(outT[:, n], act3[:, n]).then_inc(out_done, 16)
            sp.wait_ge(out_done, 16 * KT)

        @block.gpsimd
        def _(pool):
            pool.dma_start(st[:, 3].bitcast(I32), pos).then_inc(pos_in, 16)
            banks, layers, vecs, sq = Count(4), Count(), Count(), Count()

            def sum_squares():
                pool.wait_ge(squared, sq.next())
                for k in range(1, KT):
                    pool.wait_ge(squared, sq.next())
                    pool.tensor_tensor(A[:, 0], A[:, 0], A[:, k], ALU.add)
                    pool.drain()
                pool.sem_inc(sq_sum, 1)

            sum_squares()
            with repeat(pool, LAYERS, {banks: LAYER_BANKS, layers: 1, vecs: 48,
                                       sq: 16}) as l:
                pool.wait_ge(layer_done, layers.next())
                pool.dma_start(v1[:], vec1[bass.ds(l, 1)].rearrange("a p c -> (a p) c")).then_inc(vec_in, 16)
                pool.dma_start(scr[:, 0:512], ws[bass.ds(l, 1)].rearrange("a p c -> (a p) c")).then_inc(vec_in, 16)
                pool.dma_start(scr[:, 512:1024], bs[bass.ds(l, 1)].to_broadcast([P, 512])).then_inc(vec_in, 16)
                pool.wait_ge(vec_in, vecs.next(48))
                pool.sem_inc(vec_seen, 1)
                pool.affine_select(out=wsT, in_=wsT, pattern=[[0, 4], [1, P]], compare_op=ALU.is_ge, fill=0.0,
                                   base=0, channel_multiplier=-1).then_inc(ws_ready, 1)
                banks.next(16)
                sum_squares()
                sum_squares()
                banks.next(LAYER_BANKS - 16)
            pool.wait_ge(layer_done, 1 + LAYERS)
            pool.dma_start(tab[:, 0:1280], tables[:, 0:1280]).then_inc(tab_in, 16)
            pool.dma_start(tri, tables[:, 1280:1792]).then_inc(tab_in, 16)
            pool.dma_start(wfraw, wf).then_inc(tab_in, 16)
            pool.dma_start(v2[:, 0:W_ALL], vec2).then_inc(tab_in, 16)
            steps = Count(9)
            sum_squares()
            pool.wait_ge(bank_free, banks.next(24))
            v_tok = act3[:, 16:24].rearrange("p (j a) s -> p j (a s)", j=TT)
            with repeat(pool, A_HEADS // 4, {steps: 16}) as i:
                for q in range(2):
                    pool.wait_ge(pv_done, steps.value(0 if q else 8))
                    p = i * 2 + q
                    qk = [act3[:, bass.ds(p + j, 1), :].rearrange("p a s -> p (a s)") for j in (0, 8)]
                    pool.tensor_copy(QaH[q], qk[0])
                    pool.tensor_copy(KaH[q], qk[1])
                    pool.drain()
                    pool.tensor_tensor(QaL[q], qk[0], QaH[q].bitcast(F32), ALU.subtract)
                    pool.tensor_tensor(KaL[q], qk[1], KaH[q].bitcast(F32), ALU.subtract)
                    pool.drain().then_inc(qk_staged, 1)
                    pool.tensor_copy(Va[q], v_tok[:, :, bass.ds(p * P, P)]).then_inc(v_staged, 1)
                steps.next(16)
            sum_squares()
            sum_squares()
            pool.wait_ge(bank_free, banks.next(8 + FFN2_TILES + 36))
            q12 = act3[:, 0:12].rearrange("p (g n) s -> p g n s", g=3)
            chunks = Count(8 * A_HEADS // 2)
            with repeat(pool, 4, {steps: 8, chunks: 24}) as p:
                pool.wait_ge(s_full, chunks.value())
                for g in range(3):
                    pool.tensor_copy(Qb[g].rearrange("p (a s) -> p a s", a=1), q12[:, g, bass.ds(p, 1), :])
                pool.drain().then_inc(qk_staged, 1)
                pool.wait_ge(pv_done, steps.value())
                for g in range(3):
                    pool.tensor_copy(Vb[:, g], Vall[:, g, :, bass.ds(p * P, P)])
                pool.drain().then_inc(v_staged, 1)
                chunks.next(24), steps.next(8)
            sum_squares()
            sum_squares()

        @block.tensor
        def _(pe):
            tiles, banks = Count(4), Count()
            h_k, y_k, half_k = Count(), Count(), Count()
            sq, rope, sc, vn, mix = (Count() for _ in range(5))
            on, ss, rs, rw, mr = Count(1), Count(), Count(), Count(), Count()
            pe.sem_inc(tile_done, 4)
            pe.sem_inc(o_full, 1)
            pe.sem_inc(pv_done, 9)
            pe.sem_inc(t_full, 2)

            def three(out, whi, wlo, ahi, alo, first, last):
                pe.matmul(out, whi, ahi, start=first, stop=False)
                pe.matmul(out, whi, alo, start=False, stop=False)
                return pe.matmul(out, wlo, ahi, start=False, stop=last)

            def tile_T(s, aH, aL, ks=KT, ready=None, slot=None):
                slot = s if slot is None else slot
                pe.wait_ge(lo_ready, tiles.next())
                pe.wait_ge(bank_free, banks.next())
                for k in range(ks):
                    if ready is not None:
                        pe.wait_ge(ready[0], ready[1] + k + 1)
                    w = slice(k * P, (k + 1) * P)
                    ins = three(pb[:, s], hi[:, slot, w], lo[:, slot, w], aH[:, k], aL[:, k], k == 0, k == ks - 1)
                ins.then_inc(tile_done, 1)

            def first_T(aH, aL, ready, ks=KT):
                pe.wait_ge(lo_ready, tiles.next(3))
                pe.wait_ge(bank_free, banks.next(3))
                for k in range(ks):
                    pe.wait_ge(ready[0], ready[1] + k + 1)
                    w = slice(k * P, (k + 1) * P)
                    for s in range(3):
                        ins = three(pb[:, s], hi[:, s, w], lo[:, s, w], aH[:, k], aL[:, k], k == 0, k == ks - 1)
                        if k == ks - 1:
                            ins.then_inc(tile_done, 1)
                tile_T(3, aH, aL, ks)

            def tiles_T(n, aH, aL, ready, ks=KT, peel=False, ada=False, normed=None):
                if peel:
                    first_T(aH, aL, ready, ks)
                    n -= RING
                    ready = None
                with repeat(pe, n // RING, {tiles: RING + 4 * ada, banks: RING, **({rw: 1, mr: 1} if ada else {})}):
                    for s in range(RING):
                        tile_T(s, aH, aL, ks, ready if s == 0 else None, slot=2 * s % RING if ada else s)
                        if ada:
                            if s == 0 and normed is not None:
                                pe.wait_ge(o_normed, normed)
                            ada_tile(s, (2 * s + 1) % RING)
                    if ada:
                        ada_columns()

            def ada_tile(s, slot):
                pe.wait_ge(lo_ready, tiles.next())
                for kk in range(2):
                    k = 2 * s + kk
                    w = slice(kk * S, (kk + 1) * S)
                    c = cHL[:, 2 * k:2 * k + P]
                    pe.matmul(pb[:, 6], c, hi[:, slot, w], start=k == 0, stop=False)
                    ins = pe.matmul(pb[:, 6], c, lo[:, slot, w], start=False, stop=k == KT - 1)
                ins.then_inc(tile_done, 1)

            def ada_columns():
                pe.wait_ge(row_ready, rw.next())
                pe.wait_ge(mod_read, mr.next())
                for j in range(4):
                    ins = pe.matmul(pb[:, 7, j:j + 1], modrow[:, j * P:(j + 1) * P], ones[0:2, 0:1],
                                    start=True, stop=True)
                ins.then_inc(mod_full, 1)

            def tiles_N(groups, aH, aL, ada=False):
                with repeat(pe, groups, {tiles: RING + 4 * ada, banks: RING, **({rw: 1, mr: 1} if ada else {})}):
                    pe.wait_ge(bank_free, banks.next(4))
                    for s in range(RING):
                        slot = 2 * s % RING if ada else s
                        pe.wait_ge(lo_ready, tiles.next())
                        for t in range(TT):
                            for kk in range(2):
                                k = 2 * s + kk
                                w, a = slice(kk * S, (kk + 1) * S), slice(t * P, (t + 1) * P)
                                pe.matmul(pb[:, t], aH[:, k, a], hi[:, slot, w], start=k == 0, stop=False)
                                pe.matmul(pb[:, t], aL[:, k, a], hi[:, slot, w], start=False, stop=False)
                                ins = pe.matmul(pb[:, t], aH[:, k, a], lo[:, slot, w], start=False, stop=k == KT - 1)
                        ins.then_inc(tile_done, 1)
                        if ada:
                            ada_tile(s, (2 * s + 1) % RING)
                    if ada:
                        ada_columns()

            def norm_sum():
                pe.wait_ge(sq_sum, ss.next())
                for t in range(TT):
                    ins = pe.matmul(pb[:, 4, t:t + 1], A[:, 0, t * P:(t + 1) * P], ones[:, 0:1], start=True, stop=True)
                ins.then_inc(summed, 1)
                spread()

            def spread():
                pe.wait_ge(rs_ready, rs.next())
                for t in range(TT):
                    ins = pe.matmul(pb[:, 5, t * P:(t + 1) * P], stat[:, 8 + t:9 + t].to_broadcast([P, P]), ident,
                                    start=True, stop=True)
                ins.then_inc(rs_full, 1)

            def gated_pairs():
                with repeat(pe, 4, {tiles: RING, banks: RING}):
                    for s in range(RING):
                        if s % 2:
                            tile_T(s, yH, yL, KT, (y_ready, y_k.value()) if s == 1 else None)
                        else:
                            tile_T(s, hH, hL)

            with repeat(pe, LAYERS, {tiles: LAYER_TILES, banks: LAYER_BANKS, h_k: 16, y_k: 56, half_k: 16, sq: 8,
                                     rope: 8, sc: 16, on: 8, vn: 4, mix: 8, ss: 2, rs: 2, rw: 12, mr: 12}) as l:
                norm_sum()
                pe.wait_ge(c_ready, 1)
                with repeat(pe, 4, {tiles: RING, rw: 1, mr: 1}):
                    for s in range(RING):
                        ada_tile(s, s)
                    ada_columns()
                h0 = h_k.value()
                h_k.next(8)
                tiles_T(8, hH, hL, (h_ready, h0), peel=True)
                tiles_N(2, hH, hL)
                pe.wait_ge(bank_free, banks.value(-4))
                v_tok = act3[:, KT:2 * KT].rearrange("p (j a) s -> p j (a s)", j=TT)
                o_bank = lambda h: 2 + 2 * (h % 2)

                def swap(h):
                    if h:
                        pe.wait_ge(rope_ready, rope.value() + 2 * h)
                    for j in range(2):
                        pe.matmul(pb[:, j], perm, act3[:, h + 4 * j], start=True, stop=True).then_inc(rope_full, 1)

                def scores(h):
                    pe.wait_ge(rope_ready, rope.value() + 2 * h + 2)
                    for j in range(TT):
                        if j >= 2:
                            pe.wait_ge(score_ready, sc.value() + 4 * h + j - 1)
                        elif j == 0 and h >= 2:
                            pe.wait_ge(o_normed, on.value() + 2 * (h - 1))
                        pe.matmul(pb[:, 6 + j % 2, 0:S - j * P], Kr[h % 2][:, j * P:(j + 1) * P],
                                  Qr[h % 2][:, j * P:S], start=True, stop=True).then_inc(score_full, 1)
                    pe.wait_ge(score_ready, sc.value() + 4 * h + 4)

                def square_sum(h):
                    if h:
                        pe.wait_ge(o_normed, on.value() + 2 * h)
                    for e in range(2):
                        pe.wait_ge(osq_ready, sq.next())
                        ins = pe.matmul(pb[:, 6], ones, Osq[:, e * S:(e + 1) * S], start=e == 0, stop=e == 1)
                    ins.then_inc(summed, 1)

                swap(0)
                scores(0)
                swap(1)
                for h in range(R_HEADS):
                    if h >= 2:
                        pe.wait_ge(o_normed, on.value() + 2 * (h - 1))
                    for e in range(2):
                        for j in range(TT):
                            ins = pe.matmul(pb[:, o_bank(h) + e, j * P:S],
                                            v_tok[:, j, h * R_V + e * P:h * R_V + (e + 1) * P],
                                            sT[:, sT_at[j]:sT_at[j] + S - j * P], start=j == 0, stop=j == TT - 1)
                        ins.then_inc(o_full, 1)
                    if h + 1 < R_HEADS:
                        scores(h + 1)
                    if h + 2 < R_HEADS:
                        swap(h + 2)
                    square_sum(h)
                on.next(8), rope.next(8), sc.next(16)
                tiles_T(8, hH, hL, None, ada=True, normed=on.value())
                gated_pairs()
                y_k.next(8)
                tiles_N(2, hH, hL, ada=True)
                tiles_T(8, hH, hL, None, ada=True)
                pe.wait_ge(ws_ready, l + 1)
                pe.wait_ge(v_normed, vn.next(4))
                for n in range(KT):
                    pe.wait_ge(mix_free, mix.next())
                    for t in range(TT):
                        ins = pe.matmul(pb[:, 4 + n % 2, t * P:(t + 1) * P],
                                        B[:, 2 * t + n // 4, (n % 4) * P:(n % 4 + 1) * P], wsT[:, n // 2],
                                        start=True, stop=True)
                    ins.then_inc(mix_full, 1)
                tiles_T(8, hH, hL, None, ada=True)
                gated_pairs()
                y_k.next(8)
                for g in range(4):
                    pe.wait_ge(lo_ready, tiles.next())
                    pe.wait_ge(bank_free, banks.next(2))
                    pe.wait_ge(half_ready, half_k.next(2))
                    for e in range(2):
                        for k in range(2):
                            w = slice(k * 256 + e * P, k * 256 + (e + 1) * P)
                            ins = three(pb[:, (2 * g + e) % 4], hi[:, g, w], lo[:, g, w],
                                        halfB[:, 2 * g + k], halfA[:, 2 * g + k], k == 0, k == 1)
                    ins.then_inc(tile_done, 1)
                gated_pairs()
                y_k.next(8)
                m0 = half_k.value()
                half_k.next(8)
                tiles_T(8, halfB, halfM, (half_ready, m0), peel=True)
                norm_sum()
                h0 = h_k.value()
                h_k.next(8)
                tiles_T(8, hH, hL, (h_ready, h0), peel=True)
                with repeat(pe, 3, {tiles: 16, banks: 16, y_k: 8}):
                    tiles_T(8, yH, yL, (y_ready, y_k.value()))
                    y_k.next(8)
                    tiles_T(8, hH, hL, None)
                tiles_T(8, yH, yL, (y_ready, y_k.value()))
                y_k.next(8)

            pairs_in, exped, normed, moved, el, s_base = Count(), Count(1), Count(1), Count(2), Count(), Count()
            v_in = Count()

            def attention(passes, by, its, scores, probs, pT, value, y0):
                N, T = 8 * by, 16 * by if its is B_IT else 8 * by
                y_done = Count(y0)
                with repeat(pe, passes, {pairs_in: by, exped: N, normed: N, moved: T, y_done: by, v_in: by,
                                         el: 2 * by, s_base: 3 * N}):
                    at_T = 0
                    sent = [0]
                    for n in range(N + 3):
                        if n >= 3:
                            m, q, hp, it = n - 3, (n - 3) // 8, (n - 3) // 4 % 2, (n - 3) % 4
                            if m % 8 == 0:
                                if m == 0:
                                    pe.wait_ge(y_ready, y_done.value())
                                pe.wait_ge(v_staged, v_in.value() + q + 1)
                            blocks = its[it]
                            sent[0] += -(-len(blocks) // 4)
                            pe.wait_ge(t_ready, moved.value() + sent[0])
                            for b, (g, j) in enumerate(blocks):
                                ins = pe.matmul(pb[hp * 64:(hp + 1) * 64, 6 + q, it * P:(it + 1) * P],
                                                value(q, g, j, hp), pT[:, b * P:(b + 1) * P],
                                                start=b == 0, stop=b == len(blocks) - 1)
                            ins.then_inc(pv_done, 1)
                        if n < N and n % 8 == 0:
                            pe.wait_ge(qk_staged, pairs_in.value() + n // 8 + 1)
                            if its is B_IT:
                                pe.wait_ge(k_staged, pairs_in.value(A_HEADS // 2) + 1)
                        blocks = its[(n - 2) % 4] if 2 <= n < N + 2 else []
                        for c in range(3):
                            if n < N:
                                scores(n, c)
                            if 4 * c < len(blocks):
                                m = n - 2
                                if c == 0:
                                    pe.wait_ge(p_normed, normed.value() + m + 1)
                                pe.wait_ge(t_ready, moved.value() + max(0, at_T - 1))
                                for b in range(4 * c, min(4 * c + 4, len(blocks))):
                                    ins = pe.transpose(pb[:, 4 + at_T % 2, (b % 4) * P:(b % 4 + 1) * P],
                                                       probs[m % 3][:, b * P:(b + 1) * P], ident)
                                ins.then_inc(t_full, 1)
                                at_T += 1
                    pairs_in.next(by), exped.next(N), normed.next(N), moved.next(T), y_done.next(by)
                    v_in.next(by), el.next(2 * by), s_base.next(3 * N)

            def conv_ffn(last=False):
                norm_sum()
                h0 = h_k.value()
                h_k.next(8)
                for j, n in enumerate(SLABS):
                    tiles_T(2 * n, hH, hL, (h_ready, h0), peel=j == 0)
                    tiles_T(8, yH, yL, (y_ready, y_k.value()), ks=n)
                    y_k.next(n)

            norm_sum()
            norm_sum()
            h0 = h_k.value()
            h_k.next(8)
            pe.wait_ge(wf_ready, 1)
            for t in range(TT):
                for k in range(KT):
                    pe.wait_ge(h_ready, h0 + k + 1)
                    a = slice(t * P, (t + 1) * P)
                    out = pb[:, 4, t * 16:(t + 1) * 16]
                    pe.matmul(out, hH[:, k, a], wfH[:, k], start=k == 0, stop=False)
                    pe.matmul(out, hL[:, k, a], wfH[:, k], start=False, stop=False)
                    ins = pe.matmul(out, hH[:, k, a], wfL[:, k], start=False, stop=k == KT - 1)
            ins.then_inc(f_full, 1)
            tiles_T(16, hH, hL, None)
            pe.wait_ge(z_ready, 2)
            for t in range(TT):
                ins = pe.matmul(pb[0:16, 5, t * P:S], lf[:, 5, t * 16:(t + 1) * 16], tri[:, 0:S - t * P],
                                start=t == 0, stop=t == TT - 1)
            ins.then_inc(c_full, 1)
            tiles_N(2, hH, hL)
            pe.wait_ge(c_out, 1)

            def scores_a(n, c):
                if c:
                    return
                q, hp, it = n // 8, n // 4 % 2, n % 4
                w = (it + 1) * P
                pe.wait_ge(p_ready, exped.value() + max(0, n - 3))
                if it == 0:
                    pe.wait_ge(sel_ready, el.value() + n // 4 + 1)
                a = slice(hp * 64, (hp + 1) * 64)
                out = pb[:, n % 4]
                for qs, ks in ((QaH, KaH), (QaH, KaL), (QaL, KaH)):
                    pe.matmul(out[:, 0:w], qs[q][a, it * P:(it + 1) * P], ks[q][a, 0:w], start=ks is KaH and qs is QaH,
                              stop=False)
                pe.matmul(out[:, 0:w], sel[0:16, n // 4], cTH[0:16, 0:w], start=False, stop=False)
                pe.matmul(out[:, 0:w], sel[0:16, n // 4], cTL[0:16, 0:w], start=False, stop=False)
                pe.matmul(out[:, it * P:w], identR, causalR, start=False, stop=True).then_inc(s_full, 1)

            y_base = [y_k.value()]
            attention(A_HEADS // 4, 2, A_IT, scores_a, Pa, pTa,
                      lambda q, g, j, hp: Va[q][:, j, hp * 64:(hp + 1) * 64], y_base[0])
            tiles_T(8, yH, yL, (y_ready, y_base[0]))
            y_k.next(8)
            conv_ffn()
            norm_sum()
            h0 = h_k.value()
            h_k.next(8)
            tiles_T(12, hH, hL, (h_ready, h0), peel=True)
            tiles_T(12, yH, yL, (y_ready, y_k.value()))
            y_k.next(8)
            tiles_N(3, yH, yL)
            y_base = [y_k.value()]
            s_base.n = 4

            def scores_b(n, g):
                hp, it = n // 4, n % 4
                pe.wait_ge(s_read, s_base.value() + max(0, 3 * n + g - 3))
                a = slice(hp * 64, (hp + 1) * 64)
                first = max(0, it - 1) if g == 0 else 0
                pe.matmul(pb[:, (3 * n + g) % 4, 0:(it + 1 - first) * P], Qb[g][a, it * P:(it + 1) * P],
                          Kb[a, g, first * P:(it + 1) * P], start=True, stop=True).then_inc(s_full, 1)

            attention(4, 1, B_IT, scores_b, Pb, pTb,
                      lambda q, g, j, hp: Vb[:, g, j, hp * 64:(hp + 1) * 64], y_base[0])
            pe.wait_ge(y_ready, y_base[0] + 4)
            y_k.next(4)
            for s in range(RING):
                pe.wait_ge(lo_ready, tiles.next())
                pe.wait_ge(bank_free, banks.next(2))
                for e in range(2):
                    for k in range(4):
                        w = slice((4 * e + k) * P, (4 * e + k + 1) * P)
                        ins = three(pb[:, (2 * s + e) % 4], hi[:, s, w], lo[:, s, w], yH[:, k], yL[:, k], k == 0, k == 3)
                ins.then_inc(tile_done, 1)
            conv_ffn(last=True)
            norm_sum()
            assert tiles.n == TILES + 4, (tiles.n, TILES)

        @block.scalar
        def _(act):
            split, done, stf = Count(), Count(4), Count()
            land = [Count() for _ in range(RING)]
            ring = {split: RING, done: RING, **{c: 16 for c in land}}
            ada_ring = {split: 2 * RING, done: 2 * RING, **{c: 32 for c in land}}
            act.sem_inc(bank_free, 4)
            act.sem_inc(p_ready, 1)
            act.sem_inc(t_ready, 2)

            def tick(s, static=None):
                s = (s + AHEAD) % RING
                if static is not None and static + AHEAD >= TILES:
                    return
                act.wait_ge(landed[s], land[s].next(16))
                act.wait_ge(tile_done, split.next())
                act.activation(hi[:, s], raw[:, s], ACT.Copy).then_inc(hi_ready, 1)

            def bodies(n, steps, body, last=False):
                if last:
                    for i in range(n):
                        body(i)
                else:
                    with repeat(act, n, {**ring, **steps}) as i:
                        body(i)

            def to_st(s, scale=1.0, bias=0.0, func=ACT.Identity, bank=None):
                act.wait_ge(st_free, stf.next())
                b = s if bank is None else bank
                act.activation(st[:, s:s + 1], pb[:, b:b + 1], func, bias=bias, scale=scale).then_inc(bank_free, 1)

            def tiles_T(n, drain, uses_st=True, last=False, peel=False, ada=False):
                def body(i, first=False):
                    for s in range(RING):
                        t = None if not last else TILES - RING * (n // RING - i) + s
                        if s or not first:
                            tick(2 * s if ada else s, t)
                        act.wait_ge(tile_done, done.next())
                        drain(i, s)
                        if ada:
                            tick(2 * s + 1)
                            done.next()
                    if ada:
                        ada_row()
                if peel:
                    body(0, True)
                    bodies(n // RING - 1, {stf: RING} if uses_st else {}, lambda i: body(i + 1))
                    return
                bodies(n // RING, {**({stf: RING} if uses_st else {}), **(dict(ada_ring) if ada else {})}, body, last)

            def ada_row():
                act.wait_ge(tile_done, done.value())
                act.activation(modrow, pb[0:2, 6], ACT.Copy).then_inc(row_ready, 1)

            def tiles_N(groups, drain, ada=False):
                def body(i):
                    for s in range(2 * RING if ada else RING):
                        tick(s)
                    act.wait_ge(tile_done, done.next(7 if ada else 4))
                    for t in range(TT):
                        drain(i, t)
                    if ada:
                        done.next()
                        ada_row()
                bodies(groups, ada_ring if ada else {}, body)

            sums = Count()

            def square(k):
                act.activation(act3[:, at(k)], x[:, at(k)], ACT.Square).then_inc(squared, 1)

            def root(early=True):
                if early:
                    tick(0)
                act.wait_ge(summed, sums.next())
                act.activation(stat[:, 8:12], pb[:, 4, 0:4], ACT.Sqrt, bias=epsc, scale=1.0 / D).then_inc(rooted, 1)

            def to_x(n, drain, **how):
                def both(i, s):
                    drain(i, s)
                    for k in ([s - 1] if s else []) + ([3] if s == 3 else []):
                        act.wait_ge(st_free, stf.value(-4 + (s - k)))
                        square(i * RING + k)
                tiles_T(n, both, **how)

            for s in range(AHEAD):
                tick(s - AHEAD)
            act.wait_ge(setup_in, 64)
            act.activation(cs[:, 1], cs[:, 0], ACT.Silu).then_inc(c_act, 1)
            act.wait_ge(trig_arg, 1)
            act.activation(sinT, st[:, 1], ACT.Sin).then_inc(trig, 1)
            act.activation(st[:, 2], st[:, 1], ACT.Abs)
            act.drain()
            act.activation(cosT, st[:, 2], ACT.Sin, scale=-1.0, bias=cst[:, C_HALFPI:C_HALFPI + 1]).then_inc(trig, 1)

            def pairs():
                def drain(i, s):
                    to_st(s, func=ACT.Identity if s % 2 else ACT.Sigmoid)
                tiles_T(16, drain)

            for k in range(KT):
                square(k)
            vecs, of, means = Count(), Count(1), Count()
            with repeat(act, LAYERS, {split: LAYER_TILES, done: LAYER_TILES, stf: 8 + 48 + 8 + 8 + 64,
                                      sums: 6, means: 1, vecs: 1, of: 8, **{c: LAYER_TILES // RING * 16 for c in land}}) as l:
                act.wait_ge(vec_seen, vecs.next())
                root(early=False)
                with repeat(act, 4, ring):
                    for s in range(RING):
                        tick(s)
                    done.next(4)
                    ada_row()
                tick(0)

                def drain_to(first, func):
                    def drain(i, s):
                        act.activation(act3[:, at(i * RING + s + first), :], pb[:, s:s + 1], func
                                       ).then_inc(bank_free, 1)
                    return drain

                def drain_tok(first, func):
                    def drain(i, t):
                        act.activation(act3[:, bass.ds(i + first + 2 * t, 1), :], pb[:, t:t + 1], func
                                       ).then_inc(bank_free, 1)
                    return drain
                tiles_T(8, drain_to(0, ACT.Copy), uses_st=False, peel=True)
                tiles_N(2, drain_tok(8, ACT.Copy))
                for h in range(R_HEADS):
                    for e in range(2):
                        act.wait_ge(o_full, of.next())
                        act.activation(Osq[:, e * S:(e + 1) * S], pb[:, 2 + 2 * (h % 2) + e],
                                       ACT.Square).then_inc(osq_ready, 1)
                    act.wait_ge(summed, sums.next())
                    act.activation(root_r[:, 0:S], pb[:, 6], ACT.Sqrt, bias=epsc, scale=1.0 / R_V).then_inc(rooted, 1)
                tiles_T(8, lambda i, s: to_st(s, func=ACT.Silu), ada=True)
                pairs()
                tiles_N(2, drain_tok(8, ACT.Gelu_apprx_tanh), ada=True)
                act.wait_ge(v_mean, means.next())
                act.activation(stat[:, 8:12], stat[:, 12:16], ACT.Sqrt).then_inc(rooted, 1)
                tiles_T(8, drain_to(0, ACT.Gelu_apprx_tanh), uses_st=False, ada=True)

                def drain_p(i, s):
                    act.wait_ge(y_ready, l * 56 + 16)
                    drain_to(0, ACT.Copy)(i, s)
                tiles_T(8, drain_p, uses_st=False, ada=True)
                pairs()
                for g in range(4):
                    tick(g)
                    act.wait_ge(tile_done, done.next())
                    for e in range(2):
                        n = 2 * g + e
                        to_st(n % 4, scale=v1[:, V_PS + n:V_PS + n + 1], bias=bpps[:, n:n + 1])
                pairs()
                def gate_by(first):
                    def drain(i, s):
                        m = i * RING + s + first
                        to_st(s, scale=mod[:, at(m)])
                    return drain
                tick(0)
                to_x(8, gate_by(16), peel=True)
                root()
                tiles_T(8, lambda i, s: to_st(s), peel=True)
                with repeat(act, 3, {split: 16, done: 16, stf: 16, **{c: 64 for c in land}}):
                    tiles_T(8, gate_by(40))
                    tiles_T(8, lambda i, s: to_st(s))
                to_x(8, gate_by(40))

            cv = Count()

            def conv_ffn(last=False):
                root()
                for j, n in enumerate(SLABS):
                    def body(i, first=False):
                        for s in range(RING):
                            if s or not first:
                                tick(s)
                            act.wait_ge(tile_done, done.next())
                            to_st(s)
                            if s % 2:
                                act.wait_ge(conv_done, cv.next())
                                act.activation(A[:, s], A[:, s], ACT.Silu).then_inc(gated, 1)
                    if j == 0:
                        body(0, True)
                    bodies(n // 2 - (j == 0), {stf: RING, cv: 2}, body)
                    if j == len(SLABS) - 1:
                        to_x(8, lambda i, s: to_st(s), last=last)
                    else:
                        tiles_T(8, lambda i, s: to_st(s))

            root(early=False)
            for k in range(KT):
                act.wait_ge(x_ready, k + 1)
                square(k)
            root(early=False)

            def drain_q(scale, first):
                def drain(i, s):
                    act.activation(act3[:, at(i * RING + s + first), :], pb[:, s:s + 1], ACT.Copy,
                                   scale=scale).then_inc(bank_free, 1)
                return drain
            act.wait_ge(z_ready, 1)
            act.activation(lf[:, 1], lf[:, 0], ACT.Abs)
            act.drain()
            act.activation(lf[:, 2], lf[:, 1], ACT.Exp, scale=-1.0)
            act.drain()
            act.activation(lf[:, 3], lf[:, 2], ACT.Ln, bias=1.0).then_inc(e_ready, 1)
            tiles_T(8, drain_q(0.125, 0), uses_st=False)
            tiles_T(8, drain_q(1.0, 8), uses_st=False)

            def drain_v(i, t):
                act.activation(act3[:, bass.ds(i + 16 + 2 * t, 1), :], pb[:, t:t + 1], ACT.Copy).then_inc(bank_free, 1)
            tiles_N(2, drain_v)
            mx, tf, pvc = Count(), Count(2), Count(9)
            k12 = act3[:, 12:24].rearrange("p (g n) s -> p g n s", g=3)

            def attention(passes, by, its, exp_in, probs, pT):
                N, T = 8 * by, 16 * by if its is B_IT else 8 * by
                with repeat(act, passes, {mx: N, tf: T, pvc: N}) as p:
                    at_T = 0
                    if its is B_IT:
                        act.drain()
                        for g in range(3):
                            act.activation(Kb[:, g:g + 1], k12[:, g, bass.ds(p, 1), :], ACT.Copy)
                        act.drain().then_inc(k_staged, 1)
                    for n in range(N + 2):
                        if n >= 2:
                            m = n - 2
                            nb = len(its[m % 4])
                            for b in range(0, nb, 4):
                                act.wait_ge(t_full, tf.next())
                                if b == 0:
                                    act.wait_ge(pv_done, pvc.value() + m)
                                w = min(4, nb - b) * P
                                act.activation(pT[:, b * P:b * P + w], pb[:, 4 + at_T % 2, 0:w],
                                               ACT.Copy).then_inc(t_ready, 1)
                                at_T += 1
                        if n < N:
                            act.wait_ge(max_ready, mx.next())
                            w = len(its[n % 4]) * P
                            act.activation(probs[n % 3][:, 0:w], exp_in(n, w), ACT.Exp, bias=stat[:, n % 2:n % 2 + 1],
                                           accum_out=stat[:, 2 + n % 2:3 + n % 2])
                            act.drain().then_inc(p_ready, 1)
                    pvc.next(N)

            attention(A_HEADS // 4, 2, A_IT, lambda n, w: pb[:, n % 4, 0:w], Pa, pTa)
            to_x(8, lambda i, s: to_st(s))
            conv_ffn()
            root()
            tiles_T(12, drain_q(0.125, 0), uses_st=False, peel=True)
            tiles_T(12, drain_q(1.0, 12), uses_st=False)

            def drain_vb(i, t):
                act.activation(Vall[:, bass.ds(i, 1), t], pb[:, t:t + 1], ACT.Copy).then_inc(bank_free, 1)
            tiles_N(3, drain_vb)

            attention(4, 1, B_IT, lambda n, w: Pb[n % 3][:, 0:w], Pb, pTb)
            for s in range(RING):
                tick(s)
                act.wait_ge(tile_done, done.next())
                for e in range(2):
                    n = 2 * s + e
                    to_st(n % 4)
                    if n:
                        act.wait_ge(st_free, stf.value(-3))
                        square(n - 1)
            act.wait_ge(st_free, stf.value(-4))
            square(7)
            conv_ffn(last=True)
            root(early=False)

        @block.vector
        def _(dve):
            split, drained = Count(), Count(4)
            ring = {split: RING, drained: RING}
            dve.sem_inc(lo_ready, 4)
            dve.sem_inc(st_free, 4)
            dve.sem_inc(o_normed, 1)
            dve.sem_inc(p_normed, 1)
            dve.sem_inc(s_read, 4)

            def tick(s, static=None):
                s = (s + AHEAD) % RING
                if static is not None and static + AHEAD >= TILES:
                    return
                dve.wait_ge(hi_ready, split.next())
                dve.tensor_tensor(lo[:, s], raw[:, s], hi[:, s].bitcast(F32), ALU.subtract).then_inc(lo_ready, 1)

            mf, rf = Count(), Count()

            def bodies(n, body, last=False, steps=None):
                if last:
                    for i in range(n):
                        body(i)
                else:
                    with repeat(dve, n, steps or ring) as i:
                        body(i)

            def tiles_T(n, work, last=False, peel=False, ada=None):
                def body(i, first=False):
                    for s in range(RING):
                        t = None if not last else TILES - RING * (n // RING - i) + s
                        if s or not first:
                            tick(s if ada is None else 2 * s, t)
                        if work is None:
                            drained.next()
                        else:
                            dve.wait_ge(bank_free, drained.next())
                            work(i, s)
                        if ada is not None:
                            tick(2 * s + 1)
                    if ada is not None:
                        ada_out(i + ada)
                if peel:
                    body(0, True)
                    bodies(n // RING - 1, lambda i: body(i + 1))
                    return
                bodies(n // RING, body, last, {split: 2 * RING, drained: RING, mf: 1} if ada is not None else None)

            def tiles_N(groups, ada=None):
                def body(i):
                    for s in range(RING if ada is None else 2 * RING):
                        tick(s)
                    drained.next(4)
                    if ada is not None:
                        ada_out(i + ada)
                bodies(groups, body, False, {split: 2 * RING, drained: RING, mf: 1} if ada is not None else None)

            def ada_out(g):
                dve.wait_ge(mod_full, mf.next())
                dve.tensor_tensor(mod[:, bass.ds(g * 4, 4)], pb[:, 7, 0:4], v1[:, bass.ds(g * 4 + V_ADA, 4)],
                                  ALU.add).then_inc(mod_read, 1)

            def halves(src, dH, dL, by=1):
                dve.tensor_copy(dH, src)
                dve.drain()
                dve.tensor_tensor(dL, src, dH.bitcast(F32), ALU.subtract)
                dve.drain().then_inc(y_ready, by)

            roots = Count()

            def newton(bank, y, v, t, scale):
                dve.wait_ge(rooted, roots.next())
                dve.tensor_scalar(v, bank, scale, EPS, ALU.mult, ALU.add)
                dve.reciprocal(y, y)
                dve.drain()
                dve.scalar_tensor_tensor(t, y, -0.5, y, ALU.mult, ALU.mult)
                dve.drain()
                dve.tensor_tensor(t, t, v, ALU.mult)
                dve.drain()
                dve.scalar_tensor_tensor(y, t, 1.5, y, ALU.add, ALU.mult)
                dve.drain()

            def norm_to(gain, shift, dH, dL, ready):
                for k in range(KT):
                    t = st[:, k % 4]
                    dve.scalar_tensor_tensor(t, x[:, k], gain[:, k:k + 1], pb[:, 5], ALU.mult, ALU.mult)
                    dve.drain()
                    if shift is None:
                        dve.tensor_copy(dH[:, k], t)
                        dve.drain()
                        dve.tensor_tensor(dL[:, k], t, dH[:, k].bitcast(F32), ALU.subtract)
                    else:
                        dve.tensor_scalar(dH[:, k], t, shift[:, k:k + 1], None, ALU.add)
                        dve.drain()
                        dve.scalar_tensor_tensor(dL[:, k], t, shift[:, k:k + 1], dH[:, k].bitcast(F32), ALU.add,
                                                 ALU.subtract)
                    dve.drain().then_inc(ready, 1)

            def rstd(early=True):
                if early:
                    tick(0)
                newton(pb[:, 4, 0:4], stat[:, 8:12], stat[:, 12:16], stat[:, 4:8], 1.0 / D)
                dve.sem_inc(rs_ready, 1)

            def norm(gain, shift, dH, dL, ready, early=True):
                rstd(early)
                dve.wait_ge(rs_full, rf.next())
                norm_to(gain, shift, dH, dL, ready)

            def add_to_x(i, s):
                n = at(i * RING + s)
                dve.tensor_tensor(x[:, n], x[:, n], st[:, s:s + 1], ALU.add).then_inc(st_free, 1)

            for s in range(AHEAD):
                tick(s - AHEAD)
            dve.wait_ge(setup_in, 64)
            dve.wait_ge(pos_in, 16)
            pi2 = 2 * np.pi
            c1 = 6.28125
            c2 = float(np.float32(round((pi2 - c1) * 2 ** 21) / 2 ** 21))
            c3 = float(np.float32(pi2 - c1 - c2))
            dve.tensor_copy(st[:, 0], st[:, 3].bitcast(I32))
            dve.drain()
            dve.tensor_scalar(st[:, 1], st[:, 0], cst[:, C_FREQ:C_FREQ + 1], None, ALU.mult)
            dve.drain()
            dve.tensor_scalar(st[:, 2].bitcast(I32), st[:, 1], 1.0 / pi2, None, ALU.mult)
            dve.drain()
            dve.tensor_copy(st[:, 0], st[:, 2].bitcast(I32))
            dve.drain()
            for c in (c1, c2, c3):
                dve.scalar_tensor_tensor(st[:, 1], st[:, 0], -c, st[:, 1], ALU.mult, ALU.add)
                dve.drain()
            dve.tensor_scalar(st[:, 1], st[:, 1], 3.1415925, -3.1415925, ALU.min, ALU.max)
            dve.drain().then_inc(trig_arg, 1)
            dve.wait_ge(c_act, 1)
            cHL2 = cHL[:, 0:2 * KT].rearrange("p (k a) -> p k a", a=2)
            dve.tensor_scalar(cHL[:, 2 * KT:], ones, 0.0, None, ALU.mult)
            dve.tensor_copy(cHL2[:, :, 0], cs[:, 1])
            dve.drain()
            dve.tensor_tensor(cHL2[:, :, 1], cs[:, 1], cHL2[:, :, 0].bitcast(F32), ALU.subtract)
            dve.drain().then_inc(c_ready, 1)
            dve.wait_ge(trig, 2)
            dve.tensor_scalar(sinT, sinT, cst[:, C_SIGN:C_SIGN + 1], None, ALU.mult)
            dve.drain().then_inc(layer_done, 1)
            dve.sem_inc(mix_free, 2)
            dve.sem_inc(mod_read, 1)

            rp, sc, mixed = Count(), Count(), Count()

            def merge(i, s, first):
                if s % 2 == 0:
                    return
                g, b = st[:, s - 1:s], st[:, s:s + 1]
                n = at(i * 2 + s // 2 + 16)
                if first:
                    dve.tensor_tensor(act3[:, n], g, b, ALU.mult)
                else:
                    dve.tensor_tensor(b, g, b, ALU.mult)
                    dve.drain()
                    dve.tensor_tensor(act3[:, n], act3[:, n], b, ALU.add)
                dve.drain().then_inc(st_free, 2)

            def pairs(first):
                tiles_T(16, lambda i, s: merge(i, s, first))

            def geff_of(norm_at, scale_at):
                dve.tensor_scalar(geff[:], mod[:, scale_at:scale_at + 8], 1.0, None, ALU.add)
                dve.drain()
                dve.tensor_tensor(geff[:], geff[:], v1[:, norm_at:norm_at + 8], ALU.mult)
                dve.drain()

            with repeat(dve, LAYERS, {split: LAYER_TILES, drained: LAYER_BANKS, roots: 7, rp: 8, sc: 16,
                                      mixed: 8, mf: 12, rf: 2}) as l:
                rstd(early=False)
                with repeat(dve, 4, {split: RING, mf: 1}) as i:
                    for s in range(RING):
                        tick(s)
                    ada_out(i)
                dve.drain()
                tick(0)
                dve.tensor_tensor(bpps[:], v1[:, V_BP:V_BP + 8], v1[:, V_PS:V_PS + 8], ALU.mult)
                geff_of(V_N1, 8)
                dve.wait_ge(rs_full, rf.next())
                norm_to(geff, mod[:, 0:8], hH, hL, h_ready)
                tiles_T(8, None, peel=True)
                tiles_N(2)
                def rotate(h):
                    for j, dst in ((0, Qr[h % 2]), (1, Kr[h % 2])):
                        f = 1.0 if j == 0 else float(P) ** -0.5
                        t = act3[:, h + 4 * j]
                        dve.wait_ge(rope_full, rp.next())
                        dve.scalar_tensor_tensor(rT, pb[:, j], f, sinT, ALU.mult, ALU.mult)
                        dve.scalar_tensor_tensor(t, t, f, cosT, ALU.mult, ALU.mult)
                        dve.drain()
                        dve.tensor_tensor(dst, t, rT, ALU.add)
                        dve.drain().then_inc(rope_ready, 1)

                def decayed(h):
                    for j in range(TT):
                        w = S - j * P
                        dve.wait_ge(score_full, sc.next())
                        dve.tensor_tensor(sT[:, sT_at[j]:sT_at[j] + w], pb[:, 6 + j % 2, 0:w], dec[:, h, 0:w],
                                          ALU.mult).then_inc(score_ready, 1)

                rotate(0)
                decayed(0)
                rotate(1)
                for h in range(R_HEADS):
                    if h + 1 < R_HEADS:
                        decayed(h + 1)
                    if h + 2 < R_HEADS:
                        rotate(h + 2)
                    newton(pb[:, 6], root_r[:, 0:S], mean_r[:, 0:S], temp_r[:, 0:S], 1.0 / R_V)
                    for e in range(2):
                        dve.tensor_tensor(act3[:, h + 4 * e], pb[:, 2 + 2 * (h % 2) + e], root_r[:, 0:S],
                                          ALU.mult).then_inc(o_normed, 1)

                def y_ret(i, s):
                    o = act3[:, bass.ds(i * 2 + 4 * (s % 2) + s // 2, 1), :]
                    n = bass.ds(i * RING + s, 1)
                    dve.tensor_tensor(st[:, s:s + 1], st[:, s:s + 1], o, ALU.mult)
                    dve.drain()
                    halves(st[:, s:s + 1], yH[:, n], yL[:, n])
                    dve.sem_inc(st_free, 1)
                tiles_T(8, y_ret, ada=4)
                pairs(True)
                tiles_N(2, ada=6)
                dve.wait_ge(bank_free, drained.value())
                for t in range(TT):
                    vt = act3[:, 8 + 2 * t:10 + 2 * t].rearrange("p a s -> p (a s)")
                    dve.tensor_tensor_reduce(yF[:, 0:1024], vt, vt, 1.0, 0.0, ALU.mult, ALU.add,
                                             stat[:, 8 + t:9 + t])
                    dve.drain()
                dve.tensor_scalar(stat[:, 12:16], stat[:, 8:12], 1.0 / D, EPS, ALU.mult, ALU.add)
                dve.drain().then_inc(v_mean, 1)
                y, v, t = stat[:, 8:12], stat[:, 12:16], stat[:, 4:8]
                dve.wait_ge(rooted, roots.next())
                dve.reciprocal(y, y)
                dve.drain()
                dve.scalar_tensor_tensor(t, y, -0.5, y, ALU.mult, ALU.mult)
                dve.drain()
                dve.tensor_tensor(t, t, v, ALU.mult)
                dve.drain()
                dve.scalar_tensor_tensor(y, t, 1.5, y, ALU.add, ALU.mult)
                dve.drain()
                for t in range(TT):
                    vt = act3[:, 8 + 2 * t:10 + 2 * t].rearrange("p a s -> p (a s)")
                    dve.tensor_scalar(vt, vt, stat[:, 8 + t:9 + t], None, ALU.mult).then_inc(v_normed, 1)
                tiles_T(8, None, ada=8)
                dve.wait_ge(bank_free, drained.value())
                for n in range(KT):
                    dve.wait_ge(mix_full, mixed.next())
                    pv = pb[:, 4 + n % 2]
                    pv4 = pv.rearrange("p (n t) -> p n t", n=TT)
                    b4 = bsb[:, n // 2:n // 2 + 1].to_broadcast([P, TT, P])
                    dve.scalar_tensor_tensor(pv4, pv4, v1[:, V_GAIN + n:V_GAIN + n + 1], b4, ALU.mult, ALU.add)
                    dve.drain()
                    dve.tensor_tensor(A[:, n], A[:, n], pv, ALU.mult)
                    dve.drain().then_inc(mix_free, 1)
                    halves(A[:, n], yH[:, n], yL[:, n])
                tiles_T(8, None, ada=10)

                def pool_tile(n):
                    g, src, cur = n // 2, A[:, n], A[:, n]
                    turns = [scr[:, 0:S], scr[:, S:2 * S]]
                    for j in range(g + 1):
                        d, dst = 2 ** j, turns[j % 2]
                        dve.tensor_tensor(dst[:, d:S], cur[:, d:S], cur[:, 0:S - d], ALU.add)
                        dve.tensor_copy(dst[:, 0:d], cur[:, 0:d])
                        dve.drain()
                        cur = dst
                    dve.tensor_tensor(cur[:, 0:16], cur[:, 0:16], edge[:, g], ALU.mult)
                    dve.drain()
                    dst = turns[(g + 1) % 2]
                    dve.scalar_tensor_tensor(dst, cur, 1.0 / 2 ** (g + 1), src, ALU.mult, ALU.subtract)
                    dve.drain()
                    dve.tensor_copy(halfB[:, n], dst)
                    dve.drain()
                    dve.tensor_tensor(halfA[:, n], dst, halfB[:, n].bitcast(F32), ALU.subtract)
                    dve.drain().then_inc(half_ready, 1)

                for i in range(4):
                    for s in range(RING):
                        tick(s)
                        dve.wait_ge(bank_free, drained.next())
                        merge(i, s, False)
                        if s % 2:
                            pool_tile(2 * i + s // 2)
                for g in range(4):
                    tick(g)
                    for e in range(2):
                        n = 2 * g + e
                        dve.wait_ge(bank_free, drained.next())
                        halves(st[:, n % 4], yH[:, n], yL[:, n])
                        dve.sem_inc(st_free, 1)

                def last_branch(i, s):
                    if s % 2:
                        g, b, n = st[:, s - 1:s], st[:, s:s + 1], at(i * 2 + s // 2)
                        dve.tensor_tensor(b, g, b, ALU.mult)
                        dve.drain()
                        dve.tensor_tensor(b, M[:, n], b, ALU.add)
                        dve.drain()
                        dve.tensor_copy(halfB[:, n], b)
                        dve.drain()
                        dve.tensor_tensor(halfM[:, n], b, halfB[:, n].bitcast(F32), ALU.subtract)
                        dve.drain().then_inc(half_ready, 1)
                        dve.sem_inc(st_free, 2)
                tiles_T(16, last_branch)
                tick(0)
                tiles_T(8, add_to_x, peel=True)
                geff_of(V_N2, 32)
                norm(geff, mod[:, 24:32], hH, hL, h_ready)
                def hidden(i, s):
                        n = at(i * RING + s)
                        u = st[:, s:s + 1]
                        dve.scalar_tensor_tensor(u, u, 0.0, u, ALU.max, ALU.mult)
                        dve.drain()
                        halves(u, yH[:, n], yL[:, n])
                        dve.sem_inc(st_free, 1)
                tiles_T(8, hidden, peel=True)
                with repeat(dve, 3, {split: 16, drained: 16}):
                    tiles_T(8, add_to_x)
                    tiles_T(8, hidden)
                tiles_T(8, add_to_x)
                dve.drain().then_inc(layer_done, 1)

            gt = Count()

            def conv_ffn(layer, last=False):
                norm(v2[:, W_FFN + 8 * layer:W_FFN + 8 * layer + 8], None, hH, hL, h_ready)
                first = 0
                for j, n in enumerate(SLABS):
                    def body(i, skip=False):
                        for s in range(RING):
                            if s or not skip:
                                tick(s)
                            dve.wait_ge(bank_free, drained.next())
                            ch = i * 2 + (first + s // 2 + (s % 2) * (FF2 // P))
                            w = [v2[:, at(ch + (W_CW + (layer * 3 + t) * UP))] for t in range(3)]
                            b = v2[:, at(ch + (W_CB + layer * UP))]
                            u, c = st[:, s], A[:, s]
                            dve.tensor_scalar(c, u, w[2], b, ALU.mult, ALU.add)
                            dve.drain()
                            dve.scalar_tensor_tensor(c[:, 1:S], u[:, 0:S - 1], w[1], c[:, 1:S], ALU.mult, ALU.add)
                            dve.drain()
                            dve.scalar_tensor_tensor(c[:, 2:S], u[:, 0:S - 2], w[0], c[:, 2:S], ALU.mult,
                                                     ALU.add).then_inc(st_free, 1)
                            dve.drain()
                            if s % 2:
                                dve.sem_inc(conv_done, 1)
                                dve.wait_ge(gated, gt.next())
                                a = A[:, s - 1:s]
                                dve.tensor_tensor(a, a, A[:, s:s + 1], ALU.mult)
                                dve.drain()
                                m = at(i * 2 + s // 2)
                                halves(a, yH[:, m], yL[:, m])
                    if j == 0:
                        body(0, True)
                        with repeat(dve, n // 2 - 1, {**ring, gt: 2}) as i:
                            body(i + 1)
                    else:
                        with repeat(dve, n // 2, {**ring, gt: 2}) as i:
                            body(i)
                    first += n
                    tiles_T(8, add_to_x, last=last and j == len(SLABS) - 1)

            rstd(early=False)
            dve.wait_ge(tab_in, 64)
            dve.wait_ge(rs_full, rf.next())
            for k in range(KT):
                dve.scalar_tensor_tensor(x[:, k], x[:, k], v2[:, W_FIN1 + k:W_FIN1 + k + 1], pb[:, 5], ALU.mult,
                                         ALU.mult).then_inc(x_ready, 1)
            w3 = wfraw.rearrange("p (k n) -> p k n", k=KT)
            dve.tensor_copy(wfH[:], w3)
            dve.drain()
            dve.tensor_tensor(wfL[:], w3, wfH[:].bitcast(F32), ALU.subtract)
            dve.drain().then_inc(wf_ready, 1)
            norm(v2[:, W_MIX:W_MIX + 8], None, hH, hL, h_ready, early=False)
            dve.wait_ge(f_full, 1)
            for t in range(TT):
                dve.tensor_tensor(lf[:, 0, t * 16:(t + 1) * 16], pb[:, 4, t * 16:(t + 1) * 16],
                                  v2[:, W_BF:W_BF + 16], ALU.add)
            dve.drain().then_inc(z_ready, 1)
            dve.tensor_scalar(lf[:, 4], lf[:, 0], 0.0, None, ALU.min)
            dve.wait_ge(e_ready, 1)
            dve.drain()
            dve.tensor_tensor(lf[:, 5], lf[:, 4], lf[:, 3], ALU.subtract)
            dve.drain().then_inc(z_ready, 1)
            tiles_T(16, None)
            tiles_N(2)
            dve.wait_ge(bank_free, drained.value())
            dve.wait_ge(c_full, 1)
            dve.tensor_copy(cTH[0:16], pb[0:16, 5])
            dve.tensor_copy(causalR, causal)
            dve.tensor_copy(identR, ident)
            dve.drain()
            dve.tensor_tensor(cTL[0:16], pb[0:16, 5], cTH[0:16].bitcast(F32), ALU.subtract)
            dve.drain().then_inc(c_out, 1)
            sf, pr, pvc, te = Count(), Count(1), Count(9), Count(2)

            def attention(passes, by, its, maximum, probs, start):
                N, T = 8 * by, 16 * by if its is B_IT else 8 * by
                banks_of = [-(-len(its[n % 4]) // 4) for n in range(N)]
                with repeat(dve, passes, {sf: 3 * N if its is B_IT else N, pr: N, pvc: N, te: T}) as i:
                    def output(q):
                        dve.wait_ge(pv_done, pvc.value() + 8 * (q + 1))
                        k = bass.ds(i * by + q, 1)
                        dve.tensor_copy(yH[:, k], pb[:, 6 + q:7 + q])
                        dve.drain()
                        dve.tensor_tensor(yL[:, k], pb[:, 6 + q:7 + q], yH[:, k].bitcast(F32), ALU.subtract)
                        dve.drain().then_inc(y_ready, 1)
                    start(i)
                    for n in range(N + 1):
                        if n < N:
                            dve.wait_ge(t_full, te.value() + sum(banks_of[0:max(0, n - 2)]))
                            maximum(n, n // 4 % 2, n % 4, i)
                            dve.drain().then_inc(max_ready, 1)
                        if n >= 1:
                            m = n - 1
                            w = len(its[m % 4]) * P
                            dve.wait_ge(p_ready, pr.next())
                            dve.reciprocal(stat[:, 4 + m % 2:5 + m % 2], stat[:, 2 + m % 2:3 + m % 2])
                            dve.drain()
                            dve.tensor_scalar(probs[m % 3][:, 0:w], probs[m % 3][:, 0:w],
                                              stat[:, 4 + m % 2:5 + m % 2], None, ALU.mult).then_inc(p_normed, 1)
                        if n >= 11 and n % 8 == 3:
                            output((n - 11) // 8)
                    output(by - 1)
                    pvc.next(N), te.next(T)

            def selectors(i):
                for j in range(4):
                    dve.tensor_scalar(sel[0:16, j], ones[0:16], cst[0:16, bass.ds(i * 4 + j + C_ID, 1)], -1.0,
                                      ALU.mult, ALU.mult).then_inc(sel_ready, 1)

            def maximum_a(n, hp, it, i):
                dve.wait_ge(s_full, sf.next())
                dve.tensor_reduce(stat[:, n % 2:n % 2 + 1], pb[:, n % 4, 0:(it + 1) * P], AX.X, ALU.max, negate=True)

            attention(A_HEADS // 4, 2, A_IT, maximum_a, Pa, selectors)
            tiles_T(8, add_to_x)
            conv_ffn(0)
            norm(v2[:, W_MIX + 8:W_MIX + 16], None, hH, hL, h_ready)
            norm_to(v2[:, W_KV:W_KV + 8], None, yH, yL, y_ready)
            tiles_T(12, None, peel=True)
            tiles_T(12, None)
            tiles_N(3)
            dve.wait_ge(bank_free, drained.value())

            def maximum_b(n, hp, it, p):
                sbuf, o = Pb[n % 3], 0
                for g in range(3):
                    first = max(0, it - 1) if g == 0 else 0
                    w = (it + 1 - first) * P
                    end = 256 + 512 * g
                    dve.wait_ge(s_full, sf.next())
                    dve.scalar_tensor_tensor(sbuf[:, o:o + w], dist[:, end - w:end],
                                             cst[:, bass.ds(p * 2 + (C_SLOPE + 8 * g + hp), 1)],
                                             pb[:, (3 * n + g) % 4, 0:w], ALU.mult, ALU.add).then_inc(s_read, 1)
                    o += w
                dve.drain()
                dve.tensor_reduce(stat[:, n % 2:n % 2 + 1], sbuf[:, 0:o], AX.X, ALU.max, negate=True)

            attention(4, 1, B_IT, maximum_b, Pb, lambda i: None)
            for s in range(RING):
                tick(s)
                for e in range(2):
                    n = 2 * s + e
                    dve.wait_ge(bank_free, drained.next())
                    dve.tensor_tensor(x[:, n], x[:, n], st[:, n % 4], ALU.add).then_inc(st_free, 1)
            conv_ffn(1, last=True)
            rstd(early=False)
            dve.wait_ge(rs_full, rf.next())
            for k in range(KT):
                dve.scalar_tensor_tensor(act3[:, k], x[:, k], v2[:, W_FIN + k:W_FIN + k + 1], pb[:, 5], ALU.mult,
                                         ALU.mult).then_inc(out_ready, 1)


def constants():
    f = np.float32
    c = np.zeros((P, C_ALL), f)
    i, j = np.arange(P)[:, None], np.arange(P)[None]
    c[:, C_ID:C_ID + P] = i == j
    c[:, C_PERM:C_PERM + P] = (i + 64) % P == j
    c[:, C_ONES:C_ONES + P] = 1
    c[:, C_CAUSAL:C_CAUSAL + P] = np.where(j > i, f(NEG), f(0))
    for g in range(4):
        w = 2 ** (g + 1)
        c[:, C_EDGE + 16 * g:C_EDGE + 16 * g + 16] = w / np.minimum(np.arange(1, 17), w)
    half = P // 2
    freq = f(10000.0) ** (-np.arange(half, dtype=f) / f(half))
    c[:, C_FREQ] = np.concatenate([freq, freq])
    c[:, C_SIGN] = np.where(np.arange(P) < half, -1, 1)
    c[:, C_EPS] = EPS
    c[:, C_HALFPI] = np.pi / 2
    c[:, C_SLOPE:C_SLOPE + 24] = np.exp2(-8.0 * np.arange(1, 25) / 24)
    log_gamma = np.log1p(-np.power(2.0, -5.0 - np.arange(R_HEADS)))
    rel = np.arange(S)[None] - i
    decay = np.stack([np.where(rel >= 0, np.exp(lg * np.maximum(rel, 0)), 0) for lg in log_gamma], 1).astype(f)
    t = np.zeros((P, 1792), f)
    at = 0
    for dil, w in ((1, 256), (4, 512), (16, 512)):
        d = i - (np.arange(w)[None] - (w - P))
        t[:, at:at + w] = np.where((d >= 0) & (d % dil == 0) & (d <= dil * 128), -d, NEG)
        at += w
    t[:, 1280:1792] = np.arange(S)[None] >= i
    return c, decay.reshape(P, 2048), t


def tiles_t(w):
    k, c = w.shape
    t = w.reshape(k // P, P, c // P, P).transpose(2, 1, 0, 3).reshape(c // P, P, k)
    return np.pad(t, ((0, 0), (0, 0), (0, TILE - k))) if k < TILE else t


def tiles_n(w):
    g = w.shape[1] // S
    return w.reshape(4, 2, P, g, S).transpose(3, 0, 2, 1, 4).reshape(4 * g, P, TILE)


def pairs_of(a, b):
    return np.stack([a, b], 1).reshape(-1, *a.shape[1:])


def columns(v):
    return np.ascontiguousarray(v.reshape(-1, P).T)


def kernel(**inputs):
    import concourse.bacc as bacc
    from concourse.bass_utils import run_bass_kernel_spmd

    a = {k: np.asarray(v) for k, v in inputs.items()}
    parts = []
    for l in range(LAYERS):
        w = a["w_in"][l]
        q, k, v, g, u, vs, p, gates = np.split(w, np.cumsum([512, 512, 1024, 1024, 1024, 1024, 1024]), axis=1)
        gate = [tiles_t(gates[:, D * n:D * (n + 1)]) for n in range(3)]
        br = [tiles_t(a["w_branch"][l, n]) for n in range(3)]
        wp = a["w_pool"][l].reshape(4, 2, P, 256).transpose(0, 2, 1, 3).reshape(4, P, 512)
        ada = tiles_n(a["w_ada"][l])
        parts += [ada[0:16], tiles_t(q), tiles_t(k), tiles_n(v), pairs_of(tiles_t(g), ada[16:24]),
                  pairs_of(gate[0], br[0]), pairs_of(tiles_n(vs), ada[24:32]), pairs_of(tiles_t(u), ada[32:40]),
                  pairs_of(tiles_t(p), ada[40:48]), pairs_of(gate[1], br[1]),
                  np.pad(wp, ((0, 0), (0, 0), (0, TILE - 512))), pairs_of(gate[2], br[2]), tiles_t(a["w_out"][l])]
        for n in range(4):
            parts += [tiles_t(a["w_ff1"][l][:, D * n:D * (n + 1)]), tiles_t(a["w_ff2"][l][D * n:D * (n + 1)])]

    def conv_ffn(l):
        up, down, at = tiles_t(a["ffn_w_up_2"][l]), a["ffn_w_down_2"][l], 0
        for n in SLABS:
            yield pairs_of(up[at:at + n], up[at + UP // 2:at + UP // 2 + n])
            yield tiles_t(down[at * P:(at + n) * P])
            at += n

    w = a["a_w_in_2"][0]
    parts += [tiles_t(w[:, 0:2048]), tiles_n(w[:, 2048:3072]), tiles_t(a["a_w_out_2"][0]), *conv_ffn(0)]
    wkv = a["w_kv_2"]
    wo = tiles_t(a["b_w_out_2"][0])[:, :, 0:512].reshape(4, 2, P, 512).transpose(0, 2, 1, 3).reshape(4, P, TILE)
    parts += [tiles_t(a["b_w_q_2"][0]), tiles_t(wkv[:, 0:1536]), tiles_n(wkv[:, 1536:3072]), wo, *conv_ffn(1)]
    stream = np.concatenate(parts)
    assert stream.shape == (TILES, P, TILE), stream.shape

    c, decay, tables = constants()
    vec1 = np.stack([np.concatenate([columns(a[n][l]) for n in (
        "norm1", "norm2", "b_ada", "vnorm_gmlp", "b_pool", "pool_scale")], 1) for l in range(LAYERS)])
    bf = np.ascontiguousarray(np.broadcast_to(a["a_b_f_2"][0][None], (P, 16)))
    cw, final = a["ffn_conv_w_2"], columns(a["final_norm"])
    vec2 = np.concatenate([columns(a["kv_norm_g_2"]), columns(a["mix_norm_g_2"]), columns(a["ffn_norm_g_2"]),
                           columns(a["final_norm_g_2"]), final, columns(cw), columns(a["ffn_conv_b_2"]), bf], 1)
    data = {
        "stream": stream,
        "xT": np.ascontiguousarray(a["x"][0].T.reshape(KT, P, S).transpose(1, 0, 2)),
        "cvec": columns(a["c"][0]),
        "pos": np.ascontiguousarray(np.broadcast_to(a["positions"], (P, S))),
        "consts": c, "decay": decay, "tables": tables, "vec1": vec1,
        "ws": np.ascontiguousarray(a["ws_gmlp"].transpose(0, 3, 1, 2).reshape(LAYERS, P, 512)),
        "bs": a["bs_gmlp"].reshape(LAYERS, 512),
        "vec2": vec2,
        "wf": np.ascontiguousarray(w[:, 3072:].reshape(KT, P, 16).transpose(1, 0, 2).reshape(P, 128)),
    }
    nc = bacc.Bacc("TRN2", target_bir_lowering=False, num_devices=1)
    args = [nc.dram_tensor(n, v.shape, mybir.dt.from_np(v.dtype), kind="ExternalInput").ap() for n, v in data.items()]
    out = nc.dram_tensor("outT", (P, KT, S), F32, kind="ExternalOutput").ap()
    build(nc, *args, out)
    r = run_bass_kernel_spmd(nc, [data], core_ids=[0])
    return np.ascontiguousarray(r.results[0]["outT"].transpose(1, 0, 2).reshape(D, S).T)[None]
```
